# Optimizing a Trainium2 kernel written in Bass

```python
import math, functools
import jax, jax.numpy as jnp
from jax import lax
import numpy as np

D_MODEL = 1024
BATCH = 1
SEQ = 1024
DEPTH = 2
DEC_BATCH = 8
DEC_SEQ = 4
PAST_LEN = 4096
PAGE_SIZE = 128

N_A_LAYERS = DEPTH // 2
N_B_LAYERS = DEPTH - N_A_LAYERS
D_CONV = D_MODEL
CONV_A_WIDTH = 31
HEAD_DIM = 64
N_HEADS = D_MODEL // HEAD_DIM
D_FF = ((8 * D_MODEL // 3 + 127) // 128) * 128
FFN_CONV_WIDTH = 3
Q_BLOCK = 128
SB_BIAS_INIT = -6.0
EPS = 1e-6

kernel_name = "yoco_conformer_stickbreaking_step"

def rms_norm(x, g):
    xf = x.astype(jnp.float32)
    y = xf * lax.rsqrt(jnp.mean(xf * xf, axis=-1, keepdims=True) + EPS) * g.astype(jnp.float32)
    return y.astype(x.dtype)

def layer_norm(x, g, b):
    xf = x.astype(jnp.float32)
    mu = jnp.mean(xf, axis=-1, keepdims=True)
    xc = xf - mu
    var = jnp.mean(xc * xc, axis=-1, keepdims=True)
    y = xc * lax.rsqrt(var + EPS) * g.astype(jnp.float32) + b.astype(jnp.float32)
    return y.astype(x.dtype)

def depthwise_causal_conv(x_ext, w):
    c = x_ext.shape[-1]
    return lax.conv_general_dilated(
        x_ext, w[:, None, :].astype(x_ext.dtype), window_strides=(1,), padding='VALID',
        dimension_numbers=('NWC', 'WIO', 'NWC'), feature_group_count=c)

def conformer_conv_module(x, prev, w_glu, b_glu, w_dw, b_dw, ln_g, ln_b, w_out, b_out):
    a, g = jnp.split(x @ w_glu + b_glu, 2, axis=-1)
    u = a * jax.nn.sigmoid(g)
    u_ext = jnp.concatenate([prev.astype(u.dtype), u], axis=1)
    c = depthwise_causal_conv(u_ext, w_dw) + b_dw
    c = jax.nn.silu(layer_norm(c, ln_g, ln_b))
    return c @ w_out + b_out, u_ext[:, -(CONV_A_WIDTH - 1):]

def conv_ffn(x, prev, w_gate, w_up, w_dw, w_down):
    g = x @ w_gate
    g_ext = jnp.concatenate([prev.astype(g.dtype), g], axis=1)
    g_c = depthwise_causal_conv(g_ext, w_dw)
    y = (jax.nn.gelu(g_c, approximate=True) * (x @ w_up)) @ w_down
    return y, g_ext[:, -(FFN_CONV_WIDTH - 1):]

def stick_breaking_attention(q, k, v, bias, q_offset):
    tq = q.shape[1]
    scale = q.shape[-1] ** -0.5
    bias_f = bias.astype(jnp.float32)[None, :, None, None]
    outs = []
    for start in range(0, tq, Q_BLOCK):
        stop = min(start + Q_BLOCK, tq)
        n_keys = q_offset + stop
        qb = q[:, start:stop].astype(jnp.float32)
        kb = k[:, :n_keys].astype(jnp.float32)
        vb = v[:, :n_keys].astype(jnp.float32)
        z = jnp.einsum('bqhd,bkhd->bhqk', qb, kb) * scale + bias_f
        t_pos = q_offset + start + jnp.arange(stop - start)
        s_pos = jnp.arange(n_keys)
        causal = s_pos[None, :] < t_pos[:, None]
        log_one_minus = jnp.where(causal, jax.nn.log_sigmoid(-z), 0.0)
        after = lax.cumsum(log_one_minus, axis=3, reverse=True) - log_one_minus
        w = jnp.where(causal, jnp.exp(jax.nn.log_sigmoid(z) + after), 0.0)
        o = jnp.einsum('bhqk,bkhd->bqhd', w, vb)
        outs.append(o.astype(q.dtype))
    return jnp.concatenate(outs, axis=1)

def trunk(x, conv_prev, ffn_prev, past_k, past_v, p):
    b, t, _ = x.shape
    h = x
    new_conv, new_ffn = [], []
    k_new = v_new = keys = values = None
    for layer in range(DEPTH):
        hn = rms_norm(h, p['norm_mix_pre'][layer])
        if layer < N_A_LAYERS:
            m, st = conformer_conv_module(
                hn, conv_prev[layer], p['conv_w_glu'][layer], p['conv_b_glu'][layer],
                p['conv_w_dw'][layer], p['conv_b_dw'][layer], p['conv_ln_g'][layer],
                p['conv_ln_b'][layer], p['conv_w_out'][layer], p['conv_b_out'][layer])
            new_conv.append(st)
        else:
            if layer == N_A_LAYERS:
                kv_in = rms_norm(h, p['kv_norm'])
                k_new = (kv_in @ p['w_k']).reshape(b, t, N_HEADS, HEAD_DIM)
                v_new = (kv_in @ p['w_v']).reshape(b, t, N_HEADS, HEAD_DIM)
                keys = jnp.concatenate([past_k.astype(k_new.dtype), k_new], axis=1)
                values = jnp.concatenate([past_v.astype(v_new.dtype), v_new], axis=1)
            j = layer - N_A_LAYERS
            q = (hn @ p['w_q'][j]).reshape(b, t, N_HEADS, HEAD_DIM)
            o = stick_breaking_attention(q, keys, values, p['sb_bias'][j], past_k.shape[1])
            m = o.reshape(b, t, N_HEADS * HEAD_DIM) @ p['w_o'][j]
        h = h + rms_norm(m, p['norm_mix_post'][layer])
        f, st_f = conv_ffn(rms_norm(h, p['norm_ffn_pre'][layer]), ffn_prev[layer],
                           p['ffn_w_gate'][layer], p['ffn_w_up'][layer],
                           p['ffn_w_dw'][layer], p['ffn_w_down'][layer])
        new_ffn.append(st_f)
        h = h + rms_norm(f, p['norm_ffn_post'][layer])
    return h, jnp.stack(new_conv), jnp.stack(new_ffn), k_new, v_new

def setup_inputs(seed: int = 0) -> dict:
    key = jax.random.key(seed)
    ks = iter(jax.random.split(key, 40))
    f32 = jnp.float32
    n_pages = PAST_LEN // PAGE_SIZE
    n_used = DEC_BATCH * n_pages
    n_pool = n_used + max(n_used // 4, 1)
    hd = N_HEADS * HEAD_DIM

    def nrm(shape, scale):
        return jax.random.normal(next(ks), shape, f32) * scale

    def gain(shape):
        return 1.0 + nrm(shape, 0.02)

    x_prompt = nrm((BATCH, SEQ, D_MODEL), 1.0)
    x_sample = nrm((DEC_BATCH, DEC_SEQ, D_MODEL), 1.0)
    state_conv_a = nrm((N_A_LAYERS, DEC_BATCH, CONV_A_WIDTH - 1, D_CONV), 0.5)
    state_ffn_conv = nrm((DEPTH, DEC_BATCH, FFN_CONV_WIDTH - 1, D_FF), 1.0)
    cache_k = nrm((n_pool, PAGE_SIZE, N_HEADS, HEAD_DIM), 1.0)
    cache_v = nrm((n_pool, PAGE_SIZE, N_HEADS, HEAD_DIM), 1.0)
    perm = jax.random.permutation(next(ks), n_pool)
    page_table = perm[:n_used].reshape(DEC_BATCH, n_pages).astype(jnp.int32)
    return {
        'x_prompt': x_prompt,
        'x_sample': x_sample,
        'state_conv_a': state_conv_a,
        'state_ffn_conv': state_ffn_conv,
        'cache_k': cache_k,
        'cache_v': cache_v,
        'page_table': page_table,
        'norm_mix_pre': gain((DEPTH, D_MODEL)),
        'norm_mix_post': gain((DEPTH, D_MODEL)),
        'norm_ffn_pre': gain((DEPTH, D_MODEL)),
        'norm_ffn_post': gain((DEPTH, D_MODEL)),
        'conv_w_glu': nrm((N_A_LAYERS, D_MODEL, 2 * D_CONV), D_MODEL ** -0.5),
        'conv_b_glu': nrm((N_A_LAYERS, 2 * D_CONV), 0.02),
        'conv_w_dw': nrm((N_A_LAYERS, CONV_A_WIDTH, D_CONV), CONV_A_WIDTH ** -0.5),
        'conv_b_dw': nrm((N_A_LAYERS, D_CONV), 0.02),
        'conv_ln_g': gain((N_A_LAYERS, D_CONV)),
        'conv_ln_b': nrm((N_A_LAYERS, D_CONV), 0.02),
        'conv_w_out': nrm((N_A_LAYERS, D_CONV, D_MODEL), D_CONV ** -0.5),
        'conv_b_out': nrm((N_A_LAYERS, D_MODEL), 0.02),
        'kv_norm': gain((D_MODEL,)),
        'w_k': nrm((D_MODEL, hd), D_MODEL ** -0.5),
        'w_v': nrm((D_MODEL, hd), D_MODEL ** -0.5),
        'w_q': nrm((N_B_LAYERS, D_MODEL, hd), D_MODEL ** -0.5),
        'w_o': nrm((N_B_LAYERS, hd, D_MODEL), hd ** -0.5),
        'sb_bias': SB_BIAS_INIT + nrm((N_B_LAYERS, N_HEADS), 0.1),
        'ffn_w_gate': nrm((DEPTH, D_MODEL, D_FF), D_MODEL ** -0.5),
        'ffn_w_up': nrm((DEPTH, D_MODEL, D_FF), D_MODEL ** -0.5),
        'ffn_w_dw': nrm((DEPTH, FFN_CONV_WIDTH, D_FF), FFN_CONV_WIDTH ** -0.5),
        'ffn_w_down': nrm((DEPTH, D_FF, D_MODEL), D_FF ** -0.5),
    }

def reference(x_prompt, x_sample, state_conv_a, state_ffn_conv, cache_k, cache_v, page_table,
              norm_mix_pre, norm_mix_post, norm_ffn_pre, norm_ffn_post,
              conv_w_glu, conv_b_glu, conv_w_dw, conv_b_dw, conv_ln_g, conv_ln_b,
              conv_w_out, conv_b_out, kv_norm, w_k, w_v, w_q, w_o, sb_bias,
              ffn_w_gate, ffn_w_up, ffn_w_dw, ffn_w_down):
    p = dict(norm_mix_pre=norm_mix_pre, norm_mix_post=norm_mix_post,
             norm_ffn_pre=norm_ffn_pre, norm_ffn_post=norm_ffn_post,
             conv_w_glu=conv_w_glu, conv_b_glu=conv_b_glu, conv_w_dw=conv_w_dw,
             conv_b_dw=conv_b_dw, conv_ln_g=conv_ln_g, conv_ln_b=conv_ln_b,
             conv_w_out=conv_w_out, conv_b_out=conv_b_out, kv_norm=kv_norm,
             w_k=w_k, w_v=w_v, w_q=w_q, w_o=w_o, sb_bias=sb_bias, ffn_w_gate=ffn_w_gate,
             ffn_w_up=ffn_w_up, ffn_w_dw=ffn_w_dw, ffn_w_down=ffn_w_down)

    bp = x_prompt.shape[0]
    dt = x_prompt.dtype
    conv_prev_p = jnp.zeros((N_A_LAYERS, bp, CONV_A_WIDTH - 1, D_CONV), dt)
    ffn_prev_p = jnp.zeros((DEPTH, bp, FFN_CONV_WIDTH - 1, D_FF), dt)
    empty_kv = jnp.zeros((bp, 0, N_HEADS, HEAD_DIM), dt)
    y_prompt, conv_new_p, ffn_new_p, k_new_p, v_new_p = trunk(
        x_prompt, conv_prev_p, ffn_prev_p, empty_kv, empty_kv, p)

    bs = x_sample.shape[0]
    past_k = cache_k[page_table].reshape(bs, -1, N_HEADS, HEAD_DIM)
    past_v = cache_v[page_table].reshape(bs, -1, N_HEADS, HEAD_DIM)
    y_sample, conv_new_s, ffn_new_s, k_new_s, v_new_s = trunk(
        x_sample, state_conv_a, state_ffn_conv, past_k, past_v, p)

    return (y_prompt, y_sample, conv_new_p, conv_new_s, ffn_new_p, ffn_new_s,
            k_new_p, v_new_p, k_new_s, v_new_s)


_drawn_inputs = setup_inputs


def setup_inputs(seed=0):
    import zlib

    import numpy as np

    out = dict(_drawn_inputs(seed))
    spreads = {}
    factors = {'norm_ffn_post': 3.723, 'kv_norm': 2.83}
    for name, (base, spread) in spreads.items():
        noise = np.random.default_rng([zlib.crc32(name.encode()), seed]).standard_normal(out[name].shape)
        drawn = base * np.exp(spread * noise) if base else spread * noise
        out[name] = __import__('jax').numpy.asarray(drawn.astype(out[name].dtype))
    for name, factor in factors.items():
        out[name] = (out[name] * factor).astype(out[name].dtype)
    return out
```

```python
from contextlib import ExitStack

import concourse.bass as bass
from concourse import mybir

F32 = mybir.dt.float32
F32R = mybir.dt.float32r
I32 = mybir.dt.int32
ALU = mybir.AluOpType
ACT = mybir.ActivationFunctionType
ds = bass.ds

P = 128
D = 1024
KB = D // P
NP = 1024
DB, DQ = 8, 4
NS = DB * DQ
T = NP + NS
TT = NP // P
FF = 2816
FB = FF // P
CW = 31
ST = CW - 1
HEADS, HD = 16, 64
PAIRS = HEADS // 2
PAGE = 128
PAGES = 32
EPS = 1e-6
CLAMP = 40.0
NH = T // 2
HP1 = NP - NH
CH = [(0, 352), (352, 352), (704, 352)]
HCH = [(0, NH // 2), (NH // 2, NH // 2)]

(V_MIX_PRE, V_MIX_POST, V_FFN_PRE, V_FFN_POST, V_BGLU, V_BDW, V_LNG, V_LNB, V_BOUT, V_KV, V_DW) = (
    0, 2, 4, 6, 8, 10, 11, 12, 13, 14, 15)
NV = V_DW + CW

RING = 2
DVE_TAPS = 23
POOL_TAPS = CW - DVE_TAPS
KR = 8
CT = 8
CHUNKS = DB * PAGES // CT
CPB = PAGES // CT


def yoco_step(nc, ins, outs):
    A = ins
    y_p, y_s, oc_p, oc_s, of_p, of_s, ok_p, ov_p, ok_s, ov_s = outs
    k_dram = nc.dram_tensor("k_feature_major", (PAIRS, P, T), F32).ap()
    q_dram = nc.dram_tensor("q_feature_major", (PAIRS, P, T), F32).ap()

    base = (nc.sbuf_base + 63) // 64 * 64
    ROW = 4 * T
    H_AT, AR_AT = base, base + KB * ROW
    WT_AT = AR_AT + 30 * ROW
    TB_AT = WT_AT + 6 * 4096
    SM_AT = TB_AT + 4 * ROW
    small = [SM_AT]

    def at(name, shape, dt, offset):
        return nc.alloc_sbuf_tensor_at(name, shape, dt, offset=offset)

    def tiny(name, shape, dt=F32):
        n = 4
        for s in shape[1:]:
            n *= s
        t = at(name, shape, dt, small[0])
        small[0] += (n + 31) // 32 * 32
        return t

    hT = at("hT", [P, KB, T], F32, H_AT)
    xh = at("xh", [P, KB, T], F32R, AR_AT)
    xl = at("xl", [P, KB, T], F32R, AR_AT + 8 * ROW)
    mT = at("mT", [P, KB, T], F32, AR_AT + 16 * ROW)
    O2 = AR_AT + 24 * ROW
    xtok = at("xtok", [P, TT + 1, D], F32, AR_AT)
    vrow = at("vrow", [NV, D], F32, AR_AT + (TT + 1) * 4096)
    srow = at("srow", [120, 2, D], F32, AR_AT + (TT + 2) * 4096)
    UW = ST + NP + DB * (ST + DQ)
    UP = (UW + 7) // 8 * 8
    u = [at(f"u{j}", [P, UP], F32, O2 + j * 4 * UP) for j in range(2)]
    stA = at("stA", [P, KB, DB * ST], F32, O2 + 8 * UP)
    pacc = at("pacc", [P, T], F32, O2 + 8 * UP + 7680)
    ut = at("ut", [P, ST + DB * ST], F32, O2 + 8 * UP + 7680 + ROW + 1536)
    ustg = at("ustg", [120, 3, P], F32, O2 + 8 * UP + 7680 + ROW)
    xhh = at("xhh", [P, KB, NH], F32R, AR_AT)
    xlh = at("xlh", [P, KB, NH], F32R, AR_AT + 4 * ROW)
    ph = at("ph", [P, FB, NH], F32R, AR_AT + 8 * ROW)
    pl = at("pl", [P, FB, NH], F32R, AR_AT + 19 * ROW)
    mTh = at("mTh", [P, KB, NH], F32, AR_AT)
    frow = at("frow", [19, FF], F32, AR_AT + 8 * ROW)
    tok = [at(f"tok{j}", [P, TT + 1, P], F32, O2 + j * 4608) for j in range(2)]
    ytok = [at(f"ytok{j}", [P, D], F32, AR_AT + 8 * ROW + j * 4096) for j in range(2)]
    kp = [at(f"kp{j}", [P, NP], F32, AR_AT + j * 4096) for j in range(2)]
    qp = [at(f"qp{j}", [P, NP], F32, AR_AT + 8192 + j * 4096) for j in range(2)]
    vp = [at(f"vp{j}", [P, TT, P], F32, AR_AT + 16384 + j * 4096) for j in range(2)]
    eb = [at(f"eb{j}", [P, 512], F32, AR_AT + 24576 + j * 2048) for j in range(3)]
    spb = [at(f"spb{j}", [P, 512], F32, AR_AT + 30720 + j * 2048) for j in range(4)]
    sb_ = [at(f"sb{j}", [P, 512], F32, AR_AT + 38912 + j * 2048) for j in range(3)]
    wb = [at(f"wb{j}", [P, 512], F32, AR_AT + 45056 + j * 2048) for j in range(3)]
    kr = [at(f"kr{j}", [P, D], F32, AR_AT + j * 4096) for j in range(KR)]
    vr = [at(f"vr{j}", [P, D], F32, AR_AT + 32768 + j * 4096) for j in range(KR)]
    ktb = [at(f"ktb{j}", [P, PAIRS, P], F32, O2 + j * 4096) for j in range(2)]
    ceb = [at(f"ceb{j}", [P, 512], F32, O2 + 8192 + j * 2048) for j in range(2)]
    ssp = [at(f"ssp{j}", [P, 512], F32, O2 + 12288 + j * 2048) for j in range(2)]
    ssf = [at(f"ssf{j}", [P, 512], F32, O2 + 16384 + j * 2048) for j in range(2)]
    swb = [at(f"swb{j}", [P, 512], F32, O2 + 20480 + j * 2048) for j in range(2)]
    qbd = at("qbd", [P, PAIRS, DB, 8], F32, TB_AT)
    kTs = at("kTs", [P, PAIRS, NS], F32, TB_AT + 2048)
    vn = at("vn", [NS, D], F32, TB_AT + 3072)
    spn = at("spn", [P, DB, 64], F32, TB_AT + 7168)
    wn = at("wn", [NS, DB, 64], F32, TB_AT + 9216)
    brow = at("brow", [1, 512], F32, TB_AT + 11264)
    cn = at("cn", [NS, DB, 64], F32, TB_AT + 13312)
    qTs = at("qTs", [P, PAIRS, NS], F32, TB_AT + 15360)
    raw = [at(f"raw{j}", [P, KB, P], F32, WT_AT + j * 4096) for j in range(RING)]
    whi = [at(f"whi{j}", [P, KB, P], F32R, WT_AT + 8192 + j * 4096) for j in range(RING)]
    wlo = [at(f"wlo{j}", [P, KB, P], F32R, WT_AT + 16384 + j * 4096) for j in range(RING)]
    tmp = [at(f"tmp{j}", [P, T], F32, TB_AT + j * ROW) for j in range(2)]
    acc = at("acc", [P, T], F32, TB_AT + 2 * ROW)
    rs = at("rs", [P, T], F32, TB_AT + 3 * ROW)
    GW = 2 + HP1 + DB * 6
    GP = (GW + 7) // 8 * 8
    gx = [at(f"gx{j}", [P, GP], F32, TB_AT + j * 4 * GP) for j in range(2)]
    CV = TB_AT + 8 * GP
    cv = [at(f"cv{j}", [P, NH], F32, CV + j * 4 * NH) for j in range(2)]
    gel = at("gel", [P, NH], F32, CV + 8 * NH)
    pf = [at(f"pf{j}", [P, NH], F32, CV + (12 + 4 * j) * NH) for j in range(2)]
    ident = tiny("ident", [P, P])
    mean1 = tiny("mean1", [P, P])
    ninc = tiny("ninc", [P, P])
    nall = tiny("nall", [P, P])
    one1 = tiny("one1", [1, P])
    eps = tiny("eps", [P, 1])
    vec = tiny("vec", [P, KB, NV])
    fT = tiny("fT", [P, FB, 19])
    fstg = tiny("fstg", [P, FB, 18])
    gtail = tiny("gtail", [P, FB, 2])
    sbias = tiny("sbias", [P, HEADS])
    ptab = tiny("ptab", [1, DB * PAGES], I32)
    assert small[0] <= nc.sbuf_usable_end, small[0] - nc.sbuf_usable_end

    with ExitStack() as ctx:
        PS = ctx.enter_context(nc.psum_tensor("PS", [P, 8, 512], F32))

        def sem(name):
            return ctx.enter_context(nc.semaphore(name))

        fence_s = sem("stage_ends")
        ld_x, ld_v, ld_f = sem("x_landed"), sem("vectors_landed"), sem("ffn_rows_landed")
        cst = sem("constants_made")
        passed = sem("waits_passed")
        w_raw = [sem(f"weights_landed{j}") for j in range(RING)]
        w_hi, w_lo, w_used = sem("weights_hi_made"), sem("weights_lo_made"), sem("weights_used")
        ps_free = sem("psum_set_free")
        n_sq, n_add, n_mean, n_rt, n_rs = (sem(f"norm_{x}") for x in ("squares", "sums", "mean", "root", "scale"))
        n_t, n_hi, n_lo = sem("scaled"), sem("scaled_hi"), sem("scaled_lo")
        p_t, p_h = sem("post_scaled"), sem("residual_added")
        tr_pe, tr_a, tr_v = sem("transposed"), sem("transposes_read_act"), sem("transposes_read_dve")
        g_sig, g_u, g_smp, g_tap, g_pool, g_cv, g_tr, g_tre, g_dve, g_out, g_of, g_ut = (sem(f"glu_{x}") for x in (
            "sigmoid", "u", "sample_conv", "tap_products", "tap_sums", "conv", "state_transposed", "state_read",
            "vector_step", "state_stored", "state_buffer_free", "state_gathered"))
        l_s, l_m, l_xc, l_t = sem("ln_sum"), sem("ln_mean"), sem("ln_centred"), sem("ln_scaled")
        f_g, f_cv, f_gel, f_p, f_hi, f_lo, f_v, f_st = (sem(f"ffn_{x}") for x in (
            "gate_copied", "conv", "gelu", "product", "product_hi", "product_lo", "vector_step", "state_stored"))
        k_ev, k_tr, k_te, k_free, k_tf = (sem(f"proj_{x}") for x in (
            "copied", "transposed", "transposes_read", "buffer_free", "token_buffer_free"))
        k_st = [sem(f"proj_stored{j}") for j in range(2)]
        k_tst = [sem(f"proj_token_stored{j}") for j in range(2)]
        a_ld = [sem(f"att_loaded{j}") for j in range(2)]
        a_z, a_c, a_e, a_l, a_sp, a_sm, a_s, a_cum, a_w, a_wm, a_pv, a_o = (sem(f"att_{x}") for x in (
            "scores", "clamped", "exp", "log", "softplus", "masked", "suffix", "weights_ready", "weights", "weights_masked",
            "outputs", "outputs_copied"))
        s_in, s_q, s_n, s_nv, s_na, s_np = (sem("smp_loaded"), sem("smp_queries"), sem("smp_new_tensor"), sem("smp_new_vector"),
                                              sem("smp_new_scalar"), sem("smp_new_gpsimd"))
        s_k = [sem(f"k_page_landed{j}") for j in range(KR)]
        s_v = [sem(f"v_page_landed{j}") for j in range(KR)]
        s_t, s_ta, s_tv, s_qk, s_z, s_c, s_e, s_l, s_sp, s_sf, s_cum, s_w, s_pv, s_o, s_tab = (sem(f"smp_{x}") for x in (
            "page_transposed", "even_copied", "odd_copied", "tile_scored", "scores", "clamped", "exp", "log", "softplus",
            "suffix", "weights_ready", "weights", "pages_summed", "outputs_copied", "table_landed"))
        y_pe, y_a, y_v = sem("y_transposed"), sem("y_even_copied"), sem("y_odd_copied")
        y_st = [sem(f"y_stored{j}") for j in range(2)]
        fs_pe, fs_v, st_out = sem("ffn_state_transposed"), sem("ffn_state_read"), sem("ffn_tail_stored")

        block = ctx.enter_context(nc.Block())

        def fence(eng, n):
            eng.drain().then_inc(fence_s, 1)
            eng.wait_ge(fence_s, 4 * n)

        def alone(eng):
            eng.sem_inc(passed, 1)

        def ps(s, c, w):
            return PS[:, 3 * s + c, 0:w]

        first, sets, at_t, at_s = {}, {}, 0, 0
        for name, tiles, nsets in ([("glu", 16, 0), ("out", 8, 8)]
                                   + [x for h in (0, 1) for x in ((f"up0{h}", 44, 0), (f"down0{h}", 24, 8))]
                                   + [("k", 8, 8), ("v", 8, 8), ("q", 8, 8), ("o", 8, 8)]
                                   + [x for h in (0, 1) for x in ((f"up1{h}", 44, 0), (f"down1{h}", 24, 8))]):
            first[name], sets[name] = at_t, at_s
            at_t += tiles
            at_s += nsets
        TILES = at_t
        ffn_of = {"00": 0, "01": FB, "10": 2 * FB, "11": 3 * FB}
        DOWN_KB = [8, 8, FB - 16]

        def tile_no(name, per, i, q):
            return first[name] + q + per * i, (first[name] + q) // RING + (per // RING) * i

        def load_tile(sp, t, b, src, nb):
            sp.wait_ge(w_lo, t + 1)
            sp.dma_start(raw[b][:, 0:nb, :], src).then_inc(w_raw[b], 16)

        def cols(w, n, k0=0, nb=KB):
            return w[k0 * P:(k0 + nb) * P, ds(n * P, P)].rearrange("(k p) n -> p k n", p=P)

        def split_hi(act, t, turn, b):
            act.wait_ge(w_raw[b], 16 * (turn + 1))
            act.wait_ge(w_used, t + 1)
            nc.scalar.copy(whi[b][:], raw[b][:]).then_inc(w_hi, 1)

        def split_lo(dve, t, b):
            dve.wait_ge(w_hi, t + 1)
            nc.vector.tensor_tensor(wlo[b][:], raw[b][:], whi[b][:].bitcast(F32), ALU.subtract).then_inc(w_lo, 1)

        def product(pe, t, b, s, nb, k0, hi, lo, chunks, start, stop):
            pe.wait_ge(w_lo, t + 3)
            for k in range(nb):
                for wt, x in ((whi, hi), (whi, lo), (wlo, hi)):
                    for c, (c0, w) in enumerate(chunks):
                        mm = nc.tensor.matmul(ps(s, c, w), wt[b][:, k, :], x[:, k0 + k, c0:c0 + w],
                                              start=start and k == 0 and wt is whi and x is hi,
                                              stop=stop and k == nb - 1 and wt is wlo)
            mm.then_inc(w_used, 1)

        vec_rows = [(V_MIX_PRE, A["norm_mix_pre"], 2), (V_MIX_POST, A["norm_mix_post"], 2),
                    (V_FFN_PRE, A["norm_ffn_pre"], 2), (V_FFN_POST, A["norm_ffn_post"], 2),
                    (V_BGLU, A["conv_b_glu"].rearrange("a (g d) -> (a g) d", g=2), 2),
                    (V_BDW, A["conv_b_dw"], 1), (V_LNG, A["conv_ln_g"], 1), (V_LNB, A["conv_ln_b"], 1),
                    (V_BOUT, A["conv_b_out"], 1), (V_KV, A["kv_norm"].rearrange("(a d) -> a d", a=1), 1),
                    (V_DW, A["conv_w_dw"][0], CW)]

        def load_sp(sp):
            sp.dma_start(xtok[:, 0:TT, :], A["x_prompt"][0].rearrange("(t p) d -> p t d", p=P)).then_inc(ld_x, 16)
            sp.dma_start(xtok[0:NS, TT, :], A["x_sample"].rearrange("b q d -> (b q) d")).then_inc(ld_x, 16)
            for r, src, n in vec_rows:
                sp.dma_start(vrow[r:r + n, :], src).then_inc(ld_v, 16)
            st = A["state_conv_a"][0].rearrange("b s d -> (b s) d")
            for j in range(2):
                sp.dma_start(srow[:, j, :], st[120 * j:120 * j + 120, :]).then_inc(ld_v, 16)
            sp.dma_start(sbias[:, :], A["sb_bias"].broadcast_to([P, HEADS])).then_inc(ld_v, 16)
            sp.dma_start(ptab[:, :], A["page_table"].rearrange("b n -> (b n)").rearrange("(a n) -> a n", a=1)).then_inc(s_tab, 16)

        LD_V = 16 * (len(vec_rows) + 3)

        def load_pool(pool):
            for t, v in ((ident, 0.0), (mean1, 1.0 / D), (ninc, -1.0), (nall, -1.0), (one1, 1.0), (eps, EPS)):
                nc.gpsimd.memset(t[:], v)
            for j in range(2):
                nc.gpsimd.memset(u[j][:, 0:ST], 0.0)
            pool.drain().then_inc(cst, 1)
            pool.wait_ge(cst, 1)
            nc.gpsimd.affine_select(out=ident[:], in_=ident[:], compare_op=ALU.not_equal, fill=1.0, base=0,
                                    pattern=[[-1, P]], channel_multiplier=1)
            nc.gpsimd.affine_select(out=ninc[:], in_=ninc[:], compare_op=ALU.is_ge, fill=0.0, base=0,
                                    pattern=[[-1, P]], channel_multiplier=1)
            pool.drain().then_inc(cst, 1)

        def load_pe(pe):
            pe.wait_ge(cst, 2)
            pe.wait_ge(ld_x, 32)
            for k in range(KB):
                if k >= 2:
                    pe.wait_ge(tr_a, k - 1)
                    pe.wait_ge(tr_v, k - 1)
                for t in range(TT + 1):
                    n = P if t < TT else NS
                    mm = nc.tensor.transpose(PS[:, 3 * (k % 2) + t // 4, (t % 4) * P:(t % 4) * P + n],
                                             xtok[0:n, t, k * P:(k + 1) * P], ident[0:n, 0:n])
                mm.then_inc(tr_pe, 1)
            pe.wait_ge(ld_v, LD_V)
            pe.wait_ge(tr_a, KB)
            pe.wait_ge(tr_v, KB)
            for k in range(KB):
                mm = nc.tensor.transpose(PS[:, 0, k * NV:(k + 1) * NV], vrow[:, k * P:(k + 1) * P], ident[0:NV, 0:NV])
            mm.then_inc(tr_pe, 1)
            for k in range(KB):
                for j in range(2):
                    mm = nc.tensor.transpose(PS[:, 2 + k // 2, (k % 2) * 240 + j * 120:(k % 2) * 240 + j * 120 + 120],
                                             srow[:, j, k * P:(k + 1) * P], ident[0:120, 0:120])
            mm.then_inc(tr_pe, 1)

        def load_act(act):
            for k in range(KB):
                act.wait_ge(tr_pe, k + 1)
                nc.scalar.copy(hT[:, k, 0:512], PS[:, 3 * (k % 2), :]).then_inc(tr_a, 1)

        def load_dve(dve):
            for k in range(KB):
                dve.wait_ge(tr_pe, k + 1)
                nc.vector.tensor_copy(hT[:, k, 512:1024], PS[:, 3 * (k % 2) + 1, :])
                nc.vector.tensor_copy(hT[:, k, 1024:T], PS[:, 3 * (k % 2) + 2, 0:NS]).then_inc(tr_v, 1)
            dve.wait_ge(tr_pe, KB + 1)
            nc.vector.tensor_copy(vec[:, :, :], PS[:, 0, 0:KB * NV].rearrange("p (k v) -> p k v", k=KB))
            dve.wait_ge(tr_pe, KB + 2)
            for k2 in range(KB // 2):
                nc.vector.tensor_copy(stA[:, 2 * k2:2 * k2 + 2, :],
                                      PS[:, 2 + k2, 0:480].rearrange("p (k v) -> p k v", k=2))

        def stats_act(act, q, src, n, chunks):
            for k in range(KB):
                if k >= 2:
                    act.wait_ge(n_add, 7 * q + max(1, k - 2))
                nc.scalar.activation(tmp[k % 2][:, 0:n], src(k), ACT.Square).then_inc(n_sq, 1)
            act.wait_ge(n_mean, q + 1)
            for c, (c0, w) in enumerate(chunks):
                ins_ = nc.scalar.activation(rs[:, c0:c0 + w], ps(0, c, w), ACT.Sqrt, bias=eps[:, 0:1])
            ins_.then_inc(n_rt, 1)

        def stats_dve(dve, q, n):
            for k in range(1, KB):
                dve.wait_ge(n_sq, 8 * q + k + 1)
                if k == 1:
                    nc.vector.tensor_tensor(acc[:, 0:n], tmp[0][:, 0:n], tmp[1][:, 0:n], ALU.add).then_inc(n_add, 1)
                else:
                    dve.wait_ge(n_add, 7 * q + k - 1)
                    nc.vector.tensor_tensor(acc[:, 0:n], acc[:, 0:n], tmp[k % 2][:, 0:n], ALU.add).then_inc(n_add, 1)
            dve.wait_ge(n_rt, q + 1)
            nc.vector.reciprocal(rs[:, 0:n], rs[:, 0:n]).then_inc(n_rs, 1)

        def stats_pe(pe, q, chunks):
            pe.wait_ge(n_add, 7 * q + 7)
            for c, (c0, w) in enumerate(chunks):
                mm = nc.tensor.matmul(ps(0, c, w), mean1[:], acc[:, c0:c0 + w], start=True, stop=True)
            mm.then_inc(n_mean, 1)

        def apply_act(act, a, hi, n):
            for k in range(KB):
                act.wait_ge(n_t, 8 * a + k + 1)
                nc.scalar.copy(hi(k), tmp[k % 2][:, 0:n]).then_inc(n_hi, 1)

        def apply_dve(dve, a, q, src, row, hi, lo, n):
            dve.wait_ge(n_rs, q + 1)

            def low(k):
                dve.wait_ge(n_hi, 8 * a + k + 1)
                nc.vector.tensor_tensor(lo(k), tmp[k % 2][:, 0:n], hi(k).bitcast(F32), ALU.subtract).then_inc(n_lo, 1)

            for k in range(KB):
                if k >= 2:
                    dve.wait_ge(n_lo, 8 * a + k - 1)
                nc.vector.scalar_tensor_tensor(out=tmp[k % 2][:, 0:n], in0=src(k), scalar=vec[:, k, row:row + 1],
                                               in1=rs[:, 0:n], op0=ALU.mult, op1=ALU.mult).then_inc(n_t, 1)
                if k >= 1:
                    low(k - 1)
            low(KB - 1)

        def post_dve(dve, p, q, src, row, c0, n):
            dve.wait_ge(n_rs, q + 1)
            for k in range(KB + 1):
                if k < KB:
                    if k >= 2:
                        dve.wait_ge(p_h, 8 * p + k - 1)
                    nc.vector.scalar_tensor_tensor(out=tmp[k % 2][:, 0:n], in0=src(k), scalar=vec[:, k, row:row + 1],
                                                   in1=rs[:, 0:n], op0=ALU.mult, op1=ALU.mult).then_inc(p_t, 1)
                if k >= 1:
                    dve.wait_ge(p_t, 8 * p + k)
                    h = hT[:, k - 1, c0:c0 + n]
                    nc.vector.tensor_tensor(h, h, tmp[(k - 1) % 2][:, 0:n], ALU.add).then_inc(p_h, 1)

        full = lambda t: (lambda k: t[:, k, :])
        part = lambda t, c0, n: (lambda k: t[:, k, c0:c0 + n])

        w_glu = A["conv_w_glu"][0]

        def glu_sp(sp):
            with sp.Fori(0, KB // 2) as i:
                for q in range(4):
                    t, _ = tile_no("glu", 4, i, q)
                    load_tile(sp, t, q % 2, cols(w_glu, 2 * i + q // 2 + KB * (q % 2)), KB)

        def glu_pe(pe):
            with pe.Fori(0, KB // 2) as i:
                for mm_ in range(2):
                    m = 2 * i + mm_
                    pe.wait_ge(g_u, m + 1)
                    for b in range(2):
                        t, _ = tile_no("glu", 4, i, 2 * mm_ + b)
                        product(pe, t, b, b, KB, 0, xh, xl, CH, True, True)
                    pe.wait_ge(g_ut, m + 1)
                    pe.wait_ge(g_tre, m + 1)
                    nc.tensor.transpose(PS[0:ST, 6, 0:P], ut[:, 0:ST], ident[:, :])
                    for j in range(2):
                        mm = nc.tensor.transpose(PS[0:120, 6, (j + 1) * P:(j + 2) * P],
                                                 ut[:, ST + 120 * j:ST + 120 * j + 120], ident[:, :])
                    mm.then_inc(g_tr, 1)

        def glu_act(act):
            with act.Fori(0, KB // 2) as i:
                for mm_ in range(2):
                    m = 2 * i + mm_
                    t, turn = tile_no("glu", 4, i, 2 * mm_ + 1)
                    act.wait_ge(w_used, t + 3)
                    act.wait_ge(g_smp, m + 1)
                    alone(act)
                    for c, (c0, w) in enumerate(CH):
                        ins_ = nc.scalar.activation(tmp[0][:, c0:c0 + w], ps(1, c, w), ACT.Sigmoid,
                                                    bias=vec[:, ds(m, 1), V_BGLU + 1].opt())
                    ins_.then_inc(g_sig, 1)
                    for b in range(2):
                        t, turn = tile_no("glu", 4, i, 2 * mm_ + b + 2)
                        split_hi(act, t, turn, b)
                    act.wait_ge(g_u, m + 2)
                    for j in range(POOL_TAPS):
                        tap = DVE_TAPS + j
                        act.wait_ge(g_pool, POOL_TAPS * m + j + 1)
                        alone(act)
                        nc.scalar.activation((acc, rs)[j % 2][:, 0:NP], u[mm_][:, tap:tap + NP], ACT.Copy,
                                             scale=vec[:, ds(m, 1), V_DW + tap].opt()).then_inc(g_tap, 1)

        def glu_pool(pool):
            with pool.Fori(0, KB // 2) as i:
                for mm_ in range(2):
                    m = 2 * i + mm_
                    pool.wait_ge(g_cv, m + 1)
                    for j in range(POOL_TAPS):
                        pool.wait_ge(g_tap, POOL_TAPS * (m + 2) + j + 1)
                        if j == 0:
                            alone(pool)
                            nc.gpsimd.tensor_copy(pacc[:, 0:NP], acc[:, 0:NP]).then_inc(g_pool, 1)
                        else:
                            pool.wait_ge(g_pool, POOL_TAPS * m + j + 2)
                            nc.gpsimd.tensor_tensor(pacc[:, 0:NP], pacc[:, 0:NP], (acc, rs)[j % 2][:, 0:NP],
                                                    ALU.add).then_inc(g_pool, 1)
                    pool.wait_ge(g_tre, m + 2)
                    pool.dma_start(oc_p[0, 0][:, ds(m * P, P)], ustg[0:ST, 0, :]).then_inc(g_out, 16)
                    for j in range(2):
                        pool.dma_start(oc_s[0].rearrange("b s d -> (b s) d")[120 * j:120 * j + 120, ds(m * P, P)],
                                       ustg[:, j + 1, :]).then_inc(g_out, 16)
                    pool.wait_ge(g_out, 48 * m + 48)
                    pool.sem_inc(g_of, 1)

        GV = DVE_TAPS + 3

        def glu_dve(dve):
            with dve.Fori(0, KB // 2) as i:
                for mm_ in range(2):
                    m = 2 * i + mm_
                    step = [0]

                    def then(ins_):
                        step[0] += 1
                        ins_.then_inc(g_dve, 1)

                    def own(n=0):
                        dve.wait_ge(g_dve, GV * m + step[0] - n)

                    us = u[mm_]
                    usv = us[:, ST + NP:UW].rearrange("p (b w) -> p b w", b=DB)
                    dve.wait_ge(g_tap, POOL_TAPS * (m + 1))
                    nc.vector.tensor_copy(usv[:, :, 0:ST], stA[:, ds(m, 1), :].rearrange("p k (b s) -> p (k b) s", b=DB))
                    dve.wait_ge(g_sig, m + 1)
                    ba = vec[:, ds(m, 1), V_BGLU].opt()
                    for c, (c0, w) in enumerate(CH):
                        n = min(c0 + w, NP) - c0
                        nc.vector.scalar_tensor_tensor(out=us[:, ST + c0:ST + c0 + n], in0=ps(0, c, n), scalar=ba,
                                                       in1=tmp[0][:, c0:c0 + n], op0=ALU.add, op1=ALU.mult)
                    c0 = CH[2][0]
                    nc.vector.scalar_tensor_tensor(
                        out=usv[:, :, ST:ST + DQ], in0=PS[:, 2, NP - c0:T - c0].rearrange("p (b q) -> p b q", b=DB),
                        scalar=ba, in1=tmp[0][:, NP:T].rearrange("p (b q) -> p b q", b=DB),
                        op0=ALU.add, op1=ALU.mult).then_inc(g_u, 1)
                    for b in range(2):
                        t, _ = tile_no("glu", 4, i, 2 * mm_ + b + 2)
                        split_lo(dve, t, b)
                    dve.wait_ge(g_u, m + 2)
                    dve.wait_ge(g_tr, m + 2)
                    nc.vector.tensor_copy(ut[:, 0:ST], us[:, NP:NP + ST])
                    nc.vector.tensor_copy(ut[:, ST:ST + DB * ST].rearrange("p (b s) -> p b s", b=DB),
                                          usv[:, :, DQ:DQ + ST]).then_inc(g_ut, 1)
                    prod = tmp[0][:, 0:NS * CW].rearrange("p (b q w) -> p b q w", b=DB, q=DQ)
                    win = bass.AP(us, ST + NP, [(UP, P), (ST + DQ, DB), (1, DQ), (1, CW)])
                    wv = bass.AP(vec, m * NV + V_DW, [(KB * NV, P), (0, DB), (0, DQ), (1, CW)])
                    then(nc.vector.tensor_tensor(prod, win, wv, ALU.mult))
                    own()
                    smp = mT[:, ds(m, 1), NP:T].opt()
                    then(nc.vector.tensor_reduce(smp, tmp[0][:, 0:NS * CW].rearrange("p (s w) -> p s w", w=CW),
                                                 mybir.AxisListType.X, ALU.add))
                    own()
                    bdw = vec[:, ds(m, 1), V_BDW].opt()
                    nc.vector.tensor_scalar(smp, smp, bdw, None, ALU.add).then_inc(g_smp, 1)
                    sums = (mT[:, ds(m, 1), 0:NP].opt(), tmp[1][:, 0:NP])
                    for tap in range(DVE_TAPS):
                        win = us[:, tap:tap + NP]
                        wt = vec[:, ds(m, 1), V_DW + tap].opt()
                        d = sums[tap % 2]
                        if tap == 0:
                            then(nc.vector.tensor_scalar(d, win, wt, bdw, ALU.mult, ALU.add))
                        elif tap == 1:
                            dve.wait_ge(g_cv, m + 1)
                            then(nc.vector.tensor_scalar(d, win, wt, None, ALU.mult))
                        else:
                            own(1)
                            then(nc.vector.scalar_tensor_tensor(out=d, in0=win, scalar=wt, in1=d,
                                                                op0=ALU.mult, op1=ALU.add))
                    own()
                    then(nc.vector.tensor_tensor(sums[0], sums[0], sums[1], ALU.add))
                    dve.wait_ge(g_tr, m + 3)
                    dve.wait_ge(g_of, m + 1)
                    nc.vector.tensor_copy(ustg[0:ST, 0, :], PS[0:ST, 6, 0:P])
                    nc.vector.tensor_copy(ustg[:, 1:3, :],
                                          PS[0:120, 6, P:3 * P].rearrange("p (j n) -> p j n", j=2)).then_inc(g_tre, 1)
                    own()
                    dve.wait_ge(g_pool, POOL_TAPS * (m + 1) + 2)
                    nc.vector.tensor_tensor(sums[0], sums[0], pacc[:, 0:NP], ALU.add).then_inc(g_cv, 1)
                    assert step[0] == GV

        def ln_dve_sum(dve):
            for k in range(1, KB):
                if k == 1:
                    nc.vector.tensor_tensor(acc[:], mT[:, 0, :], mT[:, 1, :], ALU.add).then_inc(l_s, 1)
                else:
                    dve.wait_ge(l_s, k - 1)
                    nc.vector.tensor_tensor(acc[:], acc[:], mT[:, k, :], ALU.add).then_inc(l_s, 1)
            dve.wait_ge(l_m, 1)
            for k in range(KB):
                for c, (c0, w) in enumerate(CH):
                    ins_ = nc.vector.tensor_tensor(mT[:, k, c0:c0 + w], mT[:, k, c0:c0 + w], ps(1, c, w), ALU.subtract)
                ins_.then_inc(l_xc, 1)

        def ln_pe_mean(pe):
            pe.wait_ge(l_s, KB - 1)
            for c, (c0, w) in enumerate(CH):
                mm = nc.tensor.matmul(ps(1, c, w), mean1[:], acc[:, c0:c0 + w], start=True, stop=True)
            mm.then_inc(l_m, 1)

        def ln_dve_scale(dve, q, a):
            dve.wait_ge(n_rs, q + 1)

            def low(k):
                dve.wait_ge(n_hi, 8 * a + k + 1)
                nc.vector.tensor_tensor(xl[:, k, :], tmp[k % 2][:], xh[:, k, :].bitcast(F32), ALU.subtract).then_inc(n_lo, 1)

            for k in range(KB):
                nc.vector.tensor_tensor(mT[:, k, :], mT[:, k, :], rs[:], ALU.mult).then_inc(l_t, 1)
                if k >= 1:
                    low(k - 1)
            low(KB - 1)

        def ln_act(act, a):
            for k in range(KB):
                act.wait_ge(l_t, k + 1)
                if k >= 2:
                    act.wait_ge(n_lo, 8 * a + k - 1)
                nc.scalar.activation(tmp[k % 2][:], mT[:, k, :], ACT.Silu, bias=vec[:, k, V_LNB:V_LNB + 1],
                                     scale=vec[:, k, V_LNG:V_LNG + 1]).then_inc(n_t, 1)
                act.wait_ge(n_t, 8 * a + k + 1)
                nc.scalar.copy(xh[:, k, :], tmp[k % 2][:]).then_inc(n_hi, 1)

        def proj_sp(sp, name, w):
            with sp.Fori(0, KB // 2) as i:
                for q in range(2):
                    t, _ = tile_no(name, 2, i, q)
                    load_tile(sp, t, q, cols(w, 2 * i + q), KB)

        def proj_pe(pe, name, turned=None):
            def turn(n, b):
                pe.wait_ge(k_ev, turned * KB + n + 1)
                for g, ts_ in enumerate(((0, 1, 2, 3), (4, 5, 6, 7), (8,))):
                    if g != 1:
                        pe.wait_ge(k_te, 3 * (turned * KB + n) + g // 2 + 2)
                    for t in ts_:
                        w = P if t < TT else NS
                        mm = nc.tensor.transpose(PS[0:w, 6 + g % 2, (t % 4) * P:(t % 4) * P + P],
                                                 tmp[b][:, t * P:t * P + w], ident[:, :])
                    mm.then_inc(k_tr, 1)

            with pe.Fori(0, KB // 2) as i:
                for b in range(2):
                    t, _ = tile_no(name, 2, i, b)
                    pe.wait_ge(ps_free, sets[name] + 2 * i + b + 1)
                    product(pe, t, b, b, KB, 0, xh, xl, CH, True, True)
                    if turned is not None:
                        turn(2 * i + b, b)

        def proj_act(act, name, dest, bias=None, scale=1.0, kv=None):
            with act.Fori(0, KB // 2) as i:
                for b in range(2):
                    n = 2 * i + b
                    t, turn = tile_no(name, 2, i, b)
                    act.wait_ge(w_used, t + 3)
                    if kv is not None:
                        act.wait_ge(k_free, kv * KB + n + 1)
                    alone(act)
                    d = dest(n, b)
                    for c, (c0, w) in enumerate(CH):
                        if bias is not None:
                            ins_ = nc.scalar.activation(d[:, c0:c0 + w], ps(b, c, w), ACT.Identity,
                                                        bias=vec[:, ds(n, 1), bias].opt())
                        else:
                            ins_ = nc.scalar.activation(d[:, c0:c0 + w], ps(b, c, w), ACT.Copy, scale=scale)
                    ins_.then_inc(ps_free if kv is None else k_ev, 1)
                    if kv is not None:
                        act.wait_ge(k_ev, kv * KB + n + 1)
                        act.sem_inc(ps_free, 1)
                    t, turn = tile_no(name, 2, i, b + 2)
                    split_hi(act, t, turn, b)

        def proj_dve(dve, name, turned=None):
            with dve.Fori(0, KB // 2) as i:
                for b in range(2):
                    t, _ = tile_no(name, 2, i, b + 2)
                    split_lo(dve, t, b)
                    if turned is not None:
                        g0 = 3 * (turned * KB + 2 * i + b)
                        dve.wait_ge(k_tf, turned * KB + 2 * i + b + 1)
                        for g in range(3):
                            dve.wait_ge(k_tr, g0 + g + 1)
                            if g < 2:
                                src = PS[:, 6 + g, :].rearrange("p (t n) -> p t n", t=4)
                                nc.vector.tensor_copy(tok[b][:, 4 * g:4 * g + 4, :], src).then_inc(k_te, 1)
                            else:
                                nc.vector.tensor_copy(tok[b][0:NS, TT, :], PS[0:NS, 6, 0:P]).then_inc(k_te, 1)

        def proj_pool(pool, kv, dram, turned=None, out_p=None, out_s=None):
            with pool.Fori(0, KB // 2) as i:
                for b in range(2):
                    n = 2 * i + b
                    if dram is not None:
                        pool.wait_ge(k_ev, kv * KB + n + 1)
                        pool.dma_start(dram[ds(n, 1)].rearrange("a p t -> p (a t)"), tmp[b][:]).then_inc(k_st[b], 16)
                        done = 16 * (stored[kv] // 2 + i + 1)
                    if turned is not None:
                        pool.wait_ge(k_te, 3 * (turned * KB + n) + 3 + 2)
                        pool.dma_start(out_p[:, ds(n * P, P)].rearrange("(t p) f -> p t f", p=P),
                                       tok[b][:, 0:TT, :]).then_inc(k_tst[b], 16)
                        pool.dma_start(out_s[:, ds(n * P, P)], tok[b][0:NS, TT, :]).then_inc(k_tst[b], 16)
                    if dram is not None:
                        pool.wait_ge(k_st[b], done)
                    if turned is not None:
                        pool.wait_ge(k_tst[b], 32 * (turned * KB // 2 + i + 1))
                        pool.sem_inc(k_tf, 1)
                    pool.sem_inc(k_free, 1)
        stored = {0: 0, 1: 8, 2: 8}

        def ffn_rows_pool(pool, layer):
            pool.dma_start(frow[0:16, :], A["state_ffn_conv"][layer].rearrange("b s f -> (b s) f")).then_inc(ld_f, 16)
            pool.dma_start(frow[16:19, :], A["ffn_w_dw"][layer]).then_inc(ld_f, 16)

        def ffn_rows_pe(pe, layer):
            pe.wait_ge(ld_f, 32 * (layer + 1))
            for f in range(FB):
                mm = nc.tensor.transpose(PS[:, 6, f * 19:(f + 1) * 19], frow[:, f * P:(f + 1) * P], ident[0:19, 0:19])
            mm.then_inc(f_st, 1)

        def ffn_rows_dve(dve, layer):
            dve.wait_ge(f_st, layer + 1)
            nc.vector.tensor_copy(fT[:, :, :], PS[:, 6, 0:19 * FB].rearrange("p (f r) -> p f r", f=FB))

        def up_sp(sp, layer, half):
            with sp.Fori(0, FB // 2) as i:
                for q in range(4):
                    t, _ = tile_no(f"up{layer}{half}", 4, i, q)
                    w = A["ffn_w_gate"] if q % 2 == 0 else A["ffn_w_up"]
                    load_tile(sp, t, q % 2, cols(w[layer], 2 * i + q // 2), KB)

        def up_pe(pe, layer, half):
            f0 = ffn_of[f"{layer}{half}"]
            with pe.Fori(0, FB // 2) as i:
                for ff in range(2):
                    f = f0 + 2 * i + ff
                    for b in range(2):
                        t, _ = tile_no(f"up{layer}{half}", 4, i, 2 * ff + b)
                        pe.wait_ge((f_g, f_p)[b], f + 1)
                        product(pe, t, b, b, KB, 0, xhh, xlh, HCH, True, True)

        def up_act(act, layer, half):
            f0 = ffn_of[f"{layer}{half}"]
            name = f"up{layer}{half}"
            with act.Fori(0, FB // 2) as i:
                for ff in range(2):
                    f = f0 + 2 * i + ff
                    g = gx[ff]
                    t, _ = tile_no(name, 4, i, 2 * ff)
                    act.wait_ge(w_used, t + 3)
                    act.wait_ge(f_cv, f + 1)
                    nc.scalar.copy(g[:, 2:2 + 264], ps(0, 0, 264))
                    if half == 0:
                        ins_ = nc.scalar.copy(g[:, 2 + 264:2 + NH], ps(0, 1, 264))
                    else:
                        nc.scalar.copy(g[:, 2 + 264:2 + HP1], ps(0, 1, HP1 - 264))
                        ins_ = nc.scalar.copy(g[:, 2 + HP1:GW].rearrange("p (b w) -> p b w", b=DB)[:, :, 2:6],
                                              PS[:, 1, HP1 - 264:264].rearrange("p (b q) -> p b q", b=DB))
                    ins_.then_inc(f_g, 1)
                    t, turn = tile_no(name, 4, i, 2 * ff + 2)
                    split_hi(act, t, turn, 0)
                    act.wait_ge(f_cv, f + 3)
                    act.wait_ge(f_p, f + 1)
                    nc.scalar.activation(gel[:], cv[0][:], ACT.Gelu_apprx_tanh).then_inc(f_gel, 1)
                    t, turn = tile_no(name, 4, i, 2 * ff + 3)
                    split_hi(act, t, turn, 1)
                    act.wait_ge(f_p, f + 2)
                    nc.scalar.copy(ph[:, ds(2 * i + ff, 1), :].opt(), pf[ff][:]).then_inc(f_hi, 1)

        def up_dve(dve, layer, half):
            f0 = ffn_of[f"{layer}{half}"]
            name = f"up{layer}{half}"
            PER = (4, 10)[half]
            v0 = FB * (14 * layer + 4 * half)
            if half == 0:
                for j in range(2):
                    nc.vector.memset(gx[j][:, 0:2], 0.0)
                dve.drain().then_inc(f_lo, 1)
                dve.wait_ge(f_lo, layer + 1)
            with dve.Fori(0, FB // 2) as i:
                for ff in range(2):
                    fl = 2 * i + ff
                    f = f0 + fl
                    step = [0]

                    def then(ins_):
                        step[0] += 1
                        ins_.then_inc(f_v, 1)

                    def own(n=0):
                        dve.wait_ge(f_v, v0 + PER * fl + step[0] - n)

                    g = gx[ff]
                    gs = g[:, 2 + HP1:GW].rearrange("p (b w) -> p b w", b=DB)
                    tap = lambda j: fT[:, ds(fl, 1), 16 + j].opt()
                    n = NH if half == 0 else HP1
                    if half == 1:
                        then(nc.vector.tensor_copy(g[:, 0:2], gtail[:, ds(fl, 1), :].opt()))
                        then(nc.vector.tensor_copy(gs[:, :, 0:2], fT[:, ds(fl, 1), 0:16].rearrange(
                            "p f (b s) -> p (f b) s", b=DB)))
                        own()
                    dve.wait_ge(f_g, f + 2)
                    dve.wait_ge(f_gel, f + 1)
                    parts = [(cv[0][:, 0:n], cv[1][:, 0:n], lambda j, g=g, n=n: g[:, j:j + n])]
                    if half == 1:
                        parts.append((cv[0][:, n:NH].rearrange("p (b q) -> p b q", b=DB),
                                      cv[1][:, n:NH].rearrange("p (b q) -> p b q", b=DB),
                                      lambda j, gs=gs: gs[:, :, j:j + DQ]))
                    for j in range(3):
                        for a_, b_, win in parts:
                            if j == 0:
                                then(nc.vector.tensor_scalar(a_, win(0), tap(0), None, ALU.mult))
                            else:
                                d, s_ = (b_, a_) if j == 1 else (a_, b_)
                                own(len(parts) - 1)
                                then(nc.vector.scalar_tensor_tensor(out=d, in0=win(j), scalar=tap(j), in1=s_,
                                                                    op0=ALU.mult, op1=ALU.add))
                    if half == 0:
                        then(nc.vector.tensor_copy(gtail[:, ds(fl, 1), :].opt(), g[:, NH:NH + 2]))
                    else:
                        then(nc.vector.tensor_copy(fstg[:, ds(fl, 1), 0:2].opt(), g[:, HP1:HP1 + 2]))
                        then(nc.vector.tensor_copy(fstg[:, ds(fl, 1), 2:18].rearrange("p f (b s) -> p (f b) s", b=DB),
                                                   gs[:, :, 4:6]))
                    own()
                    dve.sem_inc(f_cv, 1)
                    t, _ = tile_no(name, 4, i, 2 * ff + 2)
                    split_lo(dve, t, 0)
                    t, _ = tile_no(name, 4, i, 2 * ff + 1)
                    dve.wait_ge(w_used, t + 3)
                    dve.wait_ge(f_gel, f + 2)
                    for c, (c0, w) in enumerate(HCH):
                        ins_ = nc.vector.tensor_tensor(pf[ff][:, c0:c0 + w], gel[:, c0:c0 + w], ps(1, c, w), ALU.mult)
                    ins_.then_inc(f_p, 1)
                    t, _ = tile_no(name, 4, i, 2 * ff + 3)
                    split_lo(dve, t, 1)
                    dve.wait_ge(f_hi, f + 1)
                    nc.vector.tensor_tensor(pl[:, ds(fl, 1), :].opt(), pf[ff][:],
                                            ph[:, ds(fl, 1), :].opt().bitcast(F32), ALU.subtract)
                    assert step[0] == PER

        def down_sp(sp, layer, half):
            with sp.Fori(0, KB // 2) as i:
                for q in range(6):
                    t, _ = tile_no(f"down{layer}{half}", 6, i, q)
                    nb = DOWN_KB[q % 3]
                    load_tile(sp, t, q % 2, cols(A["ffn_w_down"][layer], 2 * i + q // 3, 8 * (q % 3), nb), nb)

        def down_pe(pe, layer, half):
            name = f"down{layer}{half}"
            with pe.Fori(0, KB // 2) as i:
                for q in range(6):
                    t, _ = tile_no(name, 6, i, q)
                    if q % 3 == 0:
                        pe.wait_ge(ps_free, sets[name] + 2 * i + q // 3 + 1)
                    product(pe, t, q % 2, q // 3, DOWN_KB[q % 3], 8 * (q % 3), ph, pl, HCH, q % 3 == 0, q % 3 == 2)

        def loop_with_tail(eng, last, body):
            if last:
                with eng.Fori(0, KB // 2 - 1) as i:
                    body(i, False)
                body(KB // 2 - 1, True)
            else:
                with eng.Fori(0, KB // 2) as i:
                    body(i, False)

        def down_act(act, layer, half, last):
            name = f"down{layer}{half}"

            def body(i, tail):
                for q in range(6):
                    if q % 3 == 2:
                        t, _ = tile_no(name, 6, i, q)
                        act.wait_ge(w_used, t + 3)
                        for c, (c0, w) in enumerate(HCH):
                            ins_ = nc.scalar.copy(mTh[:, ds(2 * i + q // 3, 1), c0:c0 + w].opt(), ps(q // 3, c, w))
                        ins_.then_inc(ps_free, 1)
                    t, turn = tile_no(name, 6, i, q + 2)
                    if not (tail and q >= 4):
                        split_hi(act, t, turn, q % 2)
            loop_with_tail(act, last, body)

        def down_dve(dve, layer, half, last):
            name = f"down{layer}{half}"

            def body(i, tail):
                for q in range(6):
                    t, _ = tile_no(name, 6, i, q + 2)
                    if not (tail and q >= 4):
                        split_lo(dve, t, q % 2)
            loop_with_tail(dve, last, body)

        FG = [(g, min(4, FB - g)) for g in range(0, FB, 4)]

        def ffn_state_pe(pe, layer):
            for j, (g, n) in enumerate(FG):
                if j >= 2:
                    pe.wait_ge(fs_v, 6 * layer + j - 1)
                for x in range(n):
                    mm = nc.tensor.transpose(PS[0:18, 6 + j % 2, x * P:(x + 1) * P], fstg[:, g + x, :], ident[:, :])
                mm.then_inc(fs_pe, 1)

        def ffn_state_dve(dve, layer):
            for j, (g, n) in enumerate(FG):
                dve.wait_ge(fs_pe, 6 * layer + j + 1)
                nc.vector.tensor_copy(rows18[:, g * P:(g + n) * P], PS[0:18, 6 + j % 2, 0:n * P]).then_inc(fs_v, 1)

        def ffn_state_pool(pool, layer):
            pool.wait_ge(fs_v, 6 * layer + 6)
            pool.dma_start(of_p[layer, 0], rows18[0:2, :]).then_inc(st_out, 16)
            pool.dma_start(of_s[layer].rearrange("b s f -> (b s) f"), rows18[2:18, :]).then_inc(st_out, 16)
            pool.wait_ge(st_out, 32 * (layer + 1))
        rows18 = at("rows18", [18, FF], F32, TB_AT)

        UNITS = [(hh, c, j) for hh in range(2) for c in range(2) for j in range(4 * c + 3, -1, -1)]
        NU = len(UNITS)
        UN = [(pp, hh, c, j) for pp in range(2) for hh, c, j in UNITS]
        LOOPS = PAIRS // 2
        L1, L2 = 2, 3

        def span(c, j):
            t0 = max(512 * c, P * j)
            return t0 - 512 * c, 512 * (c + 1) - t0, P * j >= 512 * c

        NMASK = sum(span(c, j)[2] for _, _, c, j in UN)
        mask_no = []
        for x in UN:
            mask_no.append(sum(span(y[2], y[3])[2] for y in UN[:len(mask_no) + 1]))

        def att_sp(sp, stage):
            sp.wait_ge(fence_s, 4 * stage)
            with sp.Fori(0, LOOPS) as i:
                for pp in range(2):
                    n = 2 * i + pp
                    sp.wait_ge(a_o, 4 * n + 4)
                    sp.dma_start(kp[pp][:], k_dram[ds(n, 1), :, 0:NP].rearrange("a p t -> p (a t)")).then_inc(a_ld[pp], 16)
                    sp.dma_start(qp[pp][:], q_dram[ds(n, 1), :, 0:NP].rearrange("a p t -> p (a t)")).then_inc(a_ld[pp], 16)
                    sp.dma_start(vp[pp][:], ov_p[:, ds(n * P, P)].rearrange("(t p) f -> p t f", p=P)).then_inc(a_ld[pp], 16)

        def att_pe(pe):
            NL = len(UN)
            with pe.Fori(0, LOOPS) as i:
                u0 = NL * i
                for x in range(NL + L2):
                    if x < NL:
                        pp, hh, c, j = UN[x]
                        o, w, _ = span(c, j)
                        if (hh, c, j) == UNITS[0]:
                            pe.wait_ge(a_ld[pp], 48 * i + 48)
                        pe.wait_ge(a_w, u0 + x + 1)
                        r = slice(HD * hh, HD * hh + HD)
                        nc.tensor.matmul(PS[:, x % 4, o:o + w], kp[pp][r, j * P:(j + 1) * P],
                                         qp[pp][r, 512 * c + o:512 * c + o + w], start=True, stop=False,
                                         skip_group_check=True).then_inc(a_z, 1)
                    y = x - L1
                    if 0 <= y < NL:
                        pp, hh, c, j = UN[y]
                        o, w, diag = span(c, j)
                        top = j == 4 * c + 3
                        pe.wait_ge(a_sp, u0 + y + 1)
                        if diag:
                            pe.wait_ge(a_sm, NMASK * i + mask_no[y])
                        mm = nc.tensor.matmul(PS[:, y % 4, o:o + w], ninc[:], spb[y % 4][:, o:o + w], start=False,
                                              stop=top, skip_group_check=True)
                        if not top:
                            pe.wait_ge(a_s, u0 + y + 4)
                            mm = nc.tensor.matmul(PS[:, y % 4, o:o + w], nall[:], sb_[y % 3][:, o:o + w], start=False,
                                                  stop=True, skip_group_check=True)
                        mm.then_inc(a_cum, 1)
                    y = x - L2
                    if 0 <= y < NL:
                        pp, hh, c, j = UN[y]
                        o, w, diag = span(c, j)
                        top = j == 4 * c + 3
                        if top:
                            pe.wait_ge(a_o, 4 * (2 * i + pp) + 2 * hh + c + 5)
                        pe.wait_ge(a_w, u0 + y + 5)
                        if diag:
                            pe.wait_ge(a_wm, NMASK * i + mask_no[y])
                        nc.tensor.matmul(PS[HD * hh:HD * hh + HD, 4 + c, o:o + w], vp[pp][:, j, HD * hh:HD * hh + HD],
                                         wb[y % 3][:, o:o + w], start=top, stop=j == 0,
                                         skip_group_check=True).then_inc(a_pv, 1)

        def att_act(act):
            NL = len(UN)
            with act.Fori(0, LOOPS) as i:
                u0 = NL * i
                for x in range(NL + L1 + 1):
                    if x < NL:
                        pp, hh, c, j = UN[x]
                        o, w, _ = span(c, j)
                        e = eb[x % 3][:, o:o + w]
                        act.wait_ge(a_c, u0 + x + 1)
                        nc.scalar.activation(e, e, ACT.Exp).then_inc(a_e, 1)
                        act.wait_ge(a_e, u0 + x + 1)
                        nc.scalar.activation(e, e, ACT.Ln, bias=1.0).then_inc(a_l, 1)
                    y = x - L1
                    if 0 <= y < NL:
                        pp, hh, c, j = UN[y]
                        o, w, _ = span(c, j)
                        act.wait_ge(a_cum, u0 + y + 5)
                        act.wait_ge(a_pv, u0 + y + 1)
                        alone(act)
                        nc.scalar.activation(wb[y % 3][:, o:o + w], PS[:, y % 4, o:o + w], ACT.Exp,
                                             bias=sbias[:, ds(4 * i + 2 * pp + hh, 1)]).then_inc(a_w, 1)

        def att_dve(dve):
            NL = len(UN)
            with dve.Fori(0, LOOPS) as i:
                u0 = NL * i
                for x in range(NL + L2 + 1):
                    if x < NL:
                        pp, hh, c, j = UN[x]
                        o, w, _ = span(c, j)
                        bias = sbias[:, ds(4 * i + 2 * pp + hh, 1)]
                        dve.wait_ge(a_z, u0 + x + 1)
                        nc.vector.tensor_scalar(eb[x % 3][:, o:o + w], PS[:, x % 4, o:o + w], bias, CLAMP,
                                                ALU.add, ALU.min).then_inc(a_c, 1)
                    y = x - 1
                    if 0 <= y < NL:
                        pp, hh, c, j = UN[y]
                        o, w, _ = span(c, j)
                        bias = sbias[:, ds(4 * i + 2 * pp + hh, 1)]
                        dve.wait_ge(a_l, u0 + y + 1)
                        dve.wait_ge(a_s, u0 + y + 1)
                        dve.wait_ge(a_cum, u0 + y + 1)
                        nc.vector.scalar_tensor_tensor(out=spb[y % 4][:, o:o + w], in0=PS[:, y % 4, o:o + w], scalar=bias,
                                                       in1=eb[y % 3][:, o:o + w], op0=ALU.add,
                                                       op1=ALU.max).then_inc(a_sp, 1)
                    y = x - L2 - 1
                    if 0 <= y < NL and UN[y][3] == 0:
                        pp, hh, c, j = UN[y]
                        dve.wait_ge(a_pv, u0 + y + 4)
                        r = slice(HD * hh, HD * hh + HD)
                        nc.vector.tensor_copy(mT[r, ds(2 * i + pp, 1), 512 * c:512 * c + 512].opt(),
                                              PS[r, 4 + c, :]).then_inc(a_o, 1)

        def att_pool(pool):
            NL = len(UN)

            def mask(t, semaphore):
                alone(pool)
                nc.gpsimd.affine_select(out=t, in_=t, compare_op=ALU.is_ge, fill=0.0, base=-1,
                                        pattern=[[1, P]], channel_multiplier=-1).then_inc(semaphore, 1)

            with pool.Fori(0, LOOPS) as i:
                u0 = NL * i
                for x in range(NL + L1 + 1):
                    y = x - L1 - 1
                    if 0 <= y < NL and span(UN[y][2], UN[y][3])[2]:
                        o = span(UN[y][2], UN[y][3])[0]
                        pool.wait_ge(a_w, u0 + y + 5)
                        mask(wb[y % 3][:, o:o + P], a_wm)
                    if x < NL:
                        pp, hh, c, j = UN[x]
                        o, w, diag = span(c, j)
                        pool.wait_ge(a_sp, u0 + x + 1)
                        if diag:
                            mask(spb[x % 4][:, o:o + P], a_sm)
                            pool.wait_ge(a_sm, NMASK * i + mask_no[x])
                        pool.wait_ge(a_s, u0 + x + 4)
                        if j > 0:
                            d = sb_[(x + 1) % 3]
                            pool.wait_ge(a_cum, u0 + x + 3)
                            no = span(c, j - 1)[0]
                            alone(pool)
                            if no < o:
                                nc.gpsimd.memset(d[:, no:o], 0.0)
                            if j == 4 * c + 3:
                                ins_ = nc.gpsimd.tensor_copy(d[:, o:o + w], spb[x % 4][:, o:o + w])
                            else:
                                ins_ = nc.gpsimd.tensor_tensor(d[:, o:o + w], sb_[x % 3][:, o:o + w],
                                                               spb[x % 4][:, o:o + w], ALU.add)
                            ins_.then_inc(a_s, 1)
                        else:
                            pool.sem_inc(a_s, 1)

        TPB = PAGES

        def smp_in_pool(pool):
            pool.dma_start(kTs[:], k_dram[:, :, NP:T].rearrange("a p t -> p a t")).then_inc(s_in, 16)
            pool.dma_start(qTs[:], q_dram[:, :, NP:T].rearrange("a p t -> p a t")).then_inc(s_in, 16)
            pool.dma_start(vn[:], ov_s).then_inc(s_in, 16)

        def smp_new_dve(dve):
            nc.vector.memset(qbd[:], 0.0)
            nc.vector.memset(spn[:], 0.0)
            dve.drain().then_inc(s_nv, 1)
            dve.wait_ge(s_nv, 1)
            dve.wait_ge(s_in, 48)
            for hh in range(2):
                r = slice(HD * hh, HD * hh + HD)
                for a in range(PAIRS):
                    nc.vector.tensor_copy(qbd[r, a, :, 4 * hh:4 * hh + 4], qTs[r, a, :].rearrange("p (b q) -> p b q", b=DB))
            nc.vector.tensor_copy(brow[0:1, :].rearrange("p (t h q) -> p t h q", t=CT, h=HEADS),
                                  bass.AP(sbias, 0, [(HEADS, 1), (0, CT), (1, HEADS), (0, DQ)]))
            dve.drain().then_inc(s_q, 1)
            dve.wait_ge(s_n, 1)
            zn = PS[0:NS, 7, :].rearrange("p (b c) -> p b c", b=DB)
            nc.vector.tensor_scalar(cn[:], zn, CLAMP, None, ALU.min).then_inc(s_nv, 1)
            dve.wait_ge(s_na, 2)
            nc.vector.tensor_tensor(spn[0:NS], zn, cn[:], ALU.max).then_inc(s_nv, 1)

        def smp_new_act(act):
            act.wait_ge(s_nv, 2)
            nc.scalar.activation(cn[:], cn[:], ACT.Exp).then_inc(s_na, 1)
            act.wait_ge(s_na, 1)
            nc.scalar.activation(cn[:], cn[:], ACT.Ln, bias=1.0).then_inc(s_na, 1)
            act.wait_ge(s_n, 2)
            nc.scalar.activation(wn[:], PS[0:NS, 7, :].rearrange("p (b c) -> p b c", b=DB), ACT.Exp).then_inc(s_na, 1)

        def smp_new_pool(pool):
            def mask(t):
                v = t.rearrange("p b (h q) -> p b h q", h=HEADS)
                nc.gpsimd.affine_select(out=v, in_=v, compare_op=ALU.is_ge, fill=0.0, base=0,
                                        pattern=[[-DQ, DB], [0, HEADS], [0, DQ]], channel_multiplier=1)
                pool.drain().then_inc(s_np, 1)
                mask.n += 1
                pool.wait_ge(s_np, mask.n)
                nc.gpsimd.affine_select(out=v, in_=v, compare_op=ALU.is_ge, fill=0.0, base=-1,
                                        pattern=[[DQ, DB], [0, HEADS], [1, DQ]], channel_multiplier=-1)
                pool.drain().then_inc(s_np, 1)
                mask.n += 1
            mask.n = 0
            pool.wait_ge(s_nv, 3)
            mask(spn[0:NS])
            pool.wait_ge(s_na, 3)
            mask(wn[:])

        def smp_new_pe(pe):
            pe.wait_ge(s_q, 1)
            nc.tensor.matmul(PS[0:NS, 7, :], one1[0:1, 0:NS], brow[:], start=True, stop=False, skip_group_check=True)
            zn = PS[0:NS, 7, :].rearrange("p (b c) -> p b c", b=DB)
            for a in range(PAIRS):
                mm = nc.tensor.matmul(zn[:, :, 8 * a:8 * a + 8], kTs[:, a, :], qbd[:, a, :, :], start=False,
                                      stop=False, skip_group_check=True)
            mm.then_inc(s_n, 1)
            pe.wait_ge(s_np, 2)
            nc.tensor.matmul(PS[0:NS, 7, :], ninc[0:NS, 0:NS], spn[0:NS].rearrange("p b c -> p (b c)"), start=False,
                             stop=True, skip_group_check=True).then_inc(s_n, 1)

        def pages(eng, cache, ring, landed, freed, credit):
            eng.wait_ge(s_tab, 16)
            with eng.Fori(0, DB) as b:
                for j in range(TPB):
                    page = eng.value_load(ptab[0:1, ds(TPB * b + (TPB - 1 - j), 1)], min_val=0,
                                          max_val=cache.shape[0] - 1)
                    eng.wait_ge(freed, TPB * b + j + 1 + credit - KR)
                    eng.dma_start(ring[j % KR][:], cache[ds(page, 1)].rearrange("a s h d -> (a s) (h d)")).then_inc(
                        landed[j % KR], 16)

        def smp_sp(sp, stage):
            sp.wait_ge(fence_s, 4 * stage)
            pages(sp, A["cache_k"], kr, s_k, s_t, 8)

        def smp_pool(pool):
            pages(pool, A["cache_v"], vr, s_v, s_pv, 16)

        def by_sequence(eng, body):
            with eng.Fori(0, DB - 1) as b:
                for c in range(CPB):
                    body(b, c, True)
            for c in range(CPB):
                body(DB - 1, c, c < CPB - 1)

        def smp_pe(pe):
            def scores(b, c, g):
                z = c % 2
                pe.wait_ge(s_w, g + 1)
                nc.tensor.matmul(PS[:, z, :], one1[:], brow[:], start=True, stop=False, skip_group_check=True)
                for x in range(CT + 1):
                    if x < CT:
                        n = CT * g + x
                        pe.wait_ge(s_k[x], 16 * g + 16)
                        pe.wait_ge(s_ta, n + 1)
                        pe.wait_ge(s_tv, n + 1)
                        for a in range(PAIRS):
                            mm = nc.tensor.transpose(PS[:, 3 + 2 * (x % 2) + a // 4, (a % 4) * P:(a % 4) * P + P],
                                                     kr[x][:, a * P:(a + 1) * P], ident[:])
                        mm.then_inc(s_t, 1)
                    if x >= 1:
                        n = CT * g + x - 1
                        pe.wait_ge(s_ta, n + 3)
                        pe.wait_ge(s_tv, n + 3)
                        for a in range(PAIRS):
                            o = 64 * (x - 1) + 8 * a
                            mm = nc.tensor.matmul(PS[:, z, o:o + 8], ktb[(x - 1) % 2][:, a, :],
                                                  qbd[:, a, ds(b, 1), :].rearrange("p b c -> p (b c)"), start=False,
                                                  stop=False, skip_group_check=True)
                        mm.then_inc(s_qk, 1)

            def body(b, c, more):
                g = CPB * b + c
                if more:
                    scores(b if c < CPB - 1 else b + 1, (c + 1) % CPB, g + 1)
                pe.wait_ge(s_sp, g + 1)
                pe.wait_ge(s_sf, CT * g + CT)
                nc.tensor.matmul(PS[:, c % 2, :], ninc[:], ssp[c % 2][:], start=False, stop=False, skip_group_check=True)
                nc.tensor.matmul(PS[:, c % 2, :], nall[:], ssf[c % 2][:], start=False, stop=True,
                                 skip_group_check=True).then_inc(s_cum, 1)
                if c == 0:
                    pe.wait_ge(s_o, b + 1)
                    for a in range(PAIRS):
                        nc.tensor.matmul(PS[:, 2, 8 * a:8 * a + 8], vn[:, a * P:(a + 1) * P],
                                         wn[:, ds(b, 1), 8 * a:8 * a + 8].rearrange("p b c -> p (b c)"),
                                         start=a == 0, stop=False, skip_group_check=True)
                pe.wait_ge(s_w, g + 3)
                for x in range(CT):
                    pe.wait_ge(s_v[x], 16 * g + 16)
                    for a in range(PAIRS):
                        mm = nc.tensor.matmul(PS[:, 2, 8 * a:8 * a + 8], vr[x][:, a * P:(a + 1) * P],
                                              swb[c % 2][:, 64 * x + 8 * a:64 * x + 8 * a + 8], start=False,
                                              stop=c == CPB - 1 and x == CT - 1, skip_group_check=True)
                    mm.then_inc(s_pv, 1)

            pe.wait_ge(s_np, 4)
            scores(0, 0, 0)
            by_sequence(pe, body)

        def smp_act(act):
            def turned(g):
                for x in range(CT):
                    n = CT * g + x
                    act.wait_ge(s_t, n + 9)
                    act.wait_ge(s_qk, n + 1)
                    nc.scalar.copy(ktb[x % 2][:, 0:4, :], PS[:, 3 + 2 * (x % 2), :].rearrange("p (a s) -> p a s", a=4)
                                   ).then_inc(s_ta, 1)

            def soft(c, g):
                e = ceb[c % 2][:]
                act.wait_ge(s_c, g + 1)
                nc.scalar.activation(e, e, ACT.Exp).then_inc(s_e, 1)
                act.wait_ge(s_e, g + 1)
                nc.scalar.activation(e, e, ACT.Ln, bias=1.0).then_inc(s_l, 1)

            def body(b, c, more):
                g = CPB * b + c
                if more:
                    turned(g + 1)
                act.wait_ge(s_cum, g + 3)
                act.wait_ge(s_pv, CT * g + CT)
                nc.scalar.activation(swb[c % 2][:], PS[:, c % 2, :], ACT.Exp).then_inc(s_w, 1)
                if more:
                    soft(c + 1, g + 1)

            turned(0)
            soft(0, 0)
            by_sequence(act, body)

        def smp_dve(dve):
            def chunk(b, c, g):
                for x in range(CT):
                    n = CT * g + x
                    dve.wait_ge(s_t, n + 9)
                    dve.wait_ge(s_qk, n + 1)
                    nc.vector.tensor_copy(ktb[x % 2][:, 4:8, :], PS[:, 4 + 2 * (x % 2), :].rearrange(
                        "p (a s) -> p a s", a=4)).then_inc(s_tv, 1)
                z, e = PS[:, c % 2, :], ceb[c % 2][:]
                dve.wait_ge(s_qk, CT * g + CT + 2)
                nc.vector.tensor_scalar(e, z, CLAMP, None, ALU.min).then_inc(s_c, 1)
                dve.wait_ge(s_l, g + 1)
                dve.wait_ge(s_cum, g + 1)
                nc.vector.tensor_tensor(ssp[c % 2][:], z, e, ALU.max).then_inc(s_sp, 1)
                for x in range(CT):
                    d = ssf[c % 2][:, 64 * x:64 * x + 64]
                    if x == 0 and c == 0:
                        nc.vector.tensor_copy(d, spn[:, ds(b, 1), :].rearrange("p b c -> p (b c)")).then_inc(s_sf, 1)
                        continue
                    dve.wait_ge(s_sf, CT * g + x)
                    if x == 1:
                        dve.wait_ge(s_sp, g + 1)
                    pc, px = ((c - 1) % 2, CT - 1) if x == 0 else (c % 2, x - 1)
                    nc.vector.tensor_tensor(d, ssf[pc][:, 64 * px:64 * px + 64], ssp[pc][:, 64 * px:64 * px + 64],
                                            ALU.add).then_inc(s_sf, 1)

            def body(b, c, more):
                g = CPB * b + c
                if more:
                    chunk(b if c < CPB - 1 else b + 1, (c + 1) % CPB, g + 1)
                if c == CPB - 1:
                    dve.wait_ge(s_pv, TPB * b + TPB + 16)
                    for hh in range(2):
                        r = slice(HD * hh, HD * hh + HD)
                        ins_ = nc.vector.tensor_copy(
                            mT[r, :, ds(NP + DQ * b, DQ)],
                            PS[r, 2, 0:64].rearrange("p (a c) -> p a c", a=PAIRS)[:, :, 4 * hh:4 * hh + 4])
                    ins_.then_inc(s_o, 1)

            dve.wait_ge(s_np, 4)
            chunk(0, 0, 0)
            by_sequence(dve, body)

        def split_act(act, a):
            for k in range(KB):
                nc.scalar.copy(xh[:, k, :], mT[:, k, :]).then_inc(n_hi, 1)

        def split_dve(dve, a):
            for k in range(KB):
                dve.wait_ge(n_hi, 8 * a + k + 1)
                nc.vector.tensor_tensor(xl[:, k, :], mT[:, k, :], xh[:, k, :].bitcast(F32), ALU.subtract).then_inc(n_lo, 1)
            dve.sem_inc(n_t, KB)

        def y_rows(t):
            return (P, y_p[0][t * P:(t + 1) * P, :]) if t < TT else (NS, y_s.rearrange("b q d -> (b q) d"))

        def out_pe(pe):
            for t in range(TT + 1):
                w = y_rows(t)[0]
                if t >= 2:
                    pe.wait_ge(y_a, t - 1)
                    pe.wait_ge(y_v, t - 1)
                for k in range(KB):
                    mm = nc.tensor.transpose(PS[0:w, 2 * (t % 2) + k // 4, (k % 4) * P:(k % 4) * P + P],
                                             hT[:, k, t * P:t * P + w], ident[:, :])
                mm.then_inc(y_pe, 1)

        def out_copy(eng, copy, b, done):
            for t in range(TT + 1):
                w = y_rows(t)[0]
                eng.wait_ge(y_pe, t + 1)
                if t >= 2:
                    eng.wait_ge(y_st[t % 2], 16 * (t // 2))
                copy(ytok[t % 2][0:w, 512 * b:512 * b + 512], PS[0:w, 2 * (t % 2) + b, :]).then_inc(done, 1)

        def out_sp(sp):
            for t in range(TT + 1):
                w, dst = y_rows(t)
                sp.wait_ge(y_a, t + 1)
                sp.wait_ge(y_v, t + 1)
                sp.dma_start(dst, ytok[t % 2][0:w, :]).then_inc(y_st[t % 2], 16)
            for j in range(2):
                sp.wait_ge(y_st[j], 16 * ((TT + 1 - j + 1) // 2))

        hsrc = [part(hT, 0, NH), part(hT, NH, NH)]

        (F_LOAD, F_NORM0, F_GLU, F_LN, F_OUT, F_POST0, F_FFN0) = range(1, 8)
        FFN_FENCES = 8
        F_KVN = F_FFN0 + FFN_FENCES
        F_KV, F_QN, S_ATT, S_SMP, F_SMP, F_SPLIT, F_O, F_POST1 = range(F_KVN + 1, F_KVN + 9)
        F_FFN1 = F_POST1 + 1

        def ffn(stage0, layer, q0, a0, p0, parts):
            for half in range(2):
                parts[0](half, q0 + 2 * half, a0 + half)
                yield stage0 + 4 * half
                parts[1](half)
                yield stage0 + 4 * half + 1
                parts[2](half)
                yield stage0 + 4 * half + 2
                parts[3](half, q0 + 2 * half + 1, p0 + half)
                yield stage0 + 4 * half + 3


        @block.sync
        def _(sp):
            load_sp(sp)
            glu_sp(sp)
            proj_sp(sp, "out", A["conv_w_out"][0])
            for half in range(2):
                up_sp(sp, 0, half)
                down_sp(sp, 0, half)
            proj_sp(sp, "k", A["w_k"])
            proj_sp(sp, "v", A["w_v"])
            proj_sp(sp, "q", A["w_q"][0])
            for q in range(2):
                load_tile(sp, first["o"] + q, q, cols(A["w_o"][0], q), KB)
            att_sp(sp, S_ATT)
            smp_sp(sp, S_SMP)
            with sp.Fori(1, KB // 2) as i:
                for q in range(2):
                    t, _ = tile_no("o", 2, i, q)
                    load_tile(sp, t, q, cols(A["w_o"][0], 2 * i + q), KB)
            for half in range(2):
                up_sp(sp, 1, half)
                down_sp(sp, 1, half)
            out_sp(sp)

        @block.tensor
        def _(pe):
            pe.sem_inc(w_used, 2)
            pe.sem_inc(g_tr, 2)
            pe.sem_inc(a_cum, 4)
            pe.sem_inc(a_pv, 3)
            pe.sem_inc(s_t, 8)
            pe.sem_inc(s_qk, 2)
            pe.sem_inc(s_cum, 2)
            pe.sem_inc(s_pv, 16)
            load_pe(pe)
            fence(pe, F_LOAD)
            stats_pe(pe, 0, CH)
            fence(pe, F_NORM0)
            glu_pe(pe)
            fence(pe, F_GLU)
            ln_pe_mean(pe)
            stats_pe(pe, 1, CH)
            fence(pe, F_LN)
            proj_pe(pe, "out")
            fence(pe, F_OUT)
            stats_pe(pe, 2, CH)
            fence(pe, F_POST0)

            def run_ffn(layer, stage0, q0, a0, p0):
                def inp(half, q, a):
                    if half == 0:
                        ffn_rows_pe(pe, layer)
                    stats_pe(pe, q, HCH)

                def down(half):
                    if half == 1:
                        ffn_state_pe(pe, layer)
                    down_pe(pe, layer, half)
                for n in ffn(stage0, layer, q0, a0, p0, (inp, lambda half: up_pe(pe, layer, half), down,
                                                         lambda half, q, p: stats_pe(pe, q, HCH))):
                    fence(pe, n)
            run_ffn(0, F_FFN0, 3, 2, 1)
            stats_pe(pe, 7, CH)
            fence(pe, F_KVN)
            proj_pe(pe, "k", 0)
            proj_pe(pe, "v", 1)
            fence(pe, F_KV)
            fence(pe, F_QN)
            proj_pe(pe, "q")
            fence(pe, S_ATT)
            att_pe(pe)
            fence(pe, S_SMP)
            smp_new_pe(pe)
            smp_pe(pe)
            fence(pe, F_SMP)
            fence(pe, F_SPLIT)
            proj_pe(pe, "o")
            fence(pe, F_O)
            stats_pe(pe, 8, CH)
            fence(pe, F_POST1)
            run_ffn(1, F_FFN1, 9, 7, 4)
            out_pe(pe)

        @block.scalar
        def _(act):
            act.sem_inc(ps_free, 2)
            act.sem_inc(f_g, 1)
            act.sem_inc(f_gel, 1)
            act.sem_inc(g_tap, 16)
            act.sem_inc(a_w, 4)
            act.sem_inc(s_ta, 2)
            act.sem_inc(s_w, 2)
            load_act(act)
            for b in range(2):
                split_hi(act, b, 0, b)
            fence(act, F_LOAD)
            stats_act(act, 0, full(hT), T, CH)
            apply_act(act, 0, full(xh), T)
            fence(act, F_NORM0)
            glu_act(act)
            fence(act, F_GLU)
            act.wait_ge(l_xc, KB)
            stats_act(act, 1, full(mT), T, CH)
            ln_act(act, 1)
            fence(act, F_LN)
            proj_act(act, "out", lambda n, b: mT[:, ds(n, 1), :].opt(), bias=V_BOUT)
            fence(act, F_OUT)
            stats_act(act, 2, full(mT), T, CH)
            fence(act, F_POST0)

            def run_ffn(layer, stage0, q0, a0, p0):
                def inp(half, q, a):
                    stats_act(act, q, hsrc[half], NH, HCH)
                    apply_act(act, a, full(xhh), NH)
                for n in ffn(stage0, layer, q0, a0, p0, (
                        inp, lambda half: up_act(act, layer, half),
                        lambda half: down_act(act, layer, half, layer == 1 and half == 1),
                        lambda half, q, p: stats_act(act, q, full(mTh), NH, HCH))):
                    fence(act, n)
            run_ffn(0, F_FFN0, 3, 2, 1)
            stats_act(act, 7, full(hT), T, CH)
            apply_act(act, 4, full(xh), T)
            fence(act, F_KVN)
            proj_act(act, "k", lambda n, b: tmp[b], kv=0)
            proj_act(act, "v", lambda n, b: tmp[b], kv=1)
            fence(act, F_KV)
            apply_act(act, 5, full(xh), T)
            fence(act, F_QN)
            proj_act(act, "q", lambda n, b: tmp[b], scale=HD ** -0.5, kv=2)
            fence(act, S_ATT)
            att_act(act)
            fence(act, S_SMP)
            smp_new_act(act)
            smp_act(act)
            fence(act, F_SMP)
            split_act(act, 6)
            fence(act, F_SPLIT)
            proj_act(act, "o", lambda n, b: mT[:, ds(n, 1), :].opt())
            fence(act, F_O)
            stats_act(act, 8, full(mT), T, CH)
            fence(act, F_POST1)
            run_ffn(1, F_FFN1, 9, 7, 4)
            out_copy(act, nc.scalar.copy, 0, y_a)

        @block.vector
        def _(dve):
            dve.sem_inc(w_lo, 2)
            for s_, n in ((g_u, 1), (g_smp, 1), (g_cv, 1), (g_tre, 1), (k_te, 2), (f_cv, 2), (f_p, 1), (a_o, 8),
                          (s_tv, 2), (s_o, 1)):
                dve.sem_inc(s_, n)
            load_dve(dve)
            for b in range(2):
                split_lo(dve, b, b)
            fence(dve, F_LOAD)
            stats_dve(dve, 0, T)
            apply_dve(dve, 0, 0, full(hT), V_MIX_PRE, full(xh), full(xl), T)
            fence(dve, F_NORM0)
            glu_dve(dve)
            fence(dve, F_GLU)
            ln_dve_sum(dve)
            stats_dve(dve, 1, T)
            ln_dve_scale(dve, 1, 1)
            fence(dve, F_LN)
            proj_dve(dve, "out")
            fence(dve, F_OUT)
            stats_dve(dve, 2, T)
            post_dve(dve, 0, 2, full(mT), V_MIX_POST, 0, T)
            fence(dve, F_POST0)

            def run_ffn(layer, stage0, q0, a0, p0):
                def inp(half, q, a):
                    if half == 0:
                        ffn_rows_dve(dve, layer)
                    stats_dve(dve, q, NH)
                    apply_dve(dve, a, q, hsrc[half], V_FFN_PRE + layer, full(xhh), full(xlh), NH)

                def down(half):
                    if half == 1:
                        ffn_state_dve(dve, layer)
                    down_dve(dve, layer, half, layer == 1 and half == 1)

                def post(half, q, p):
                    stats_dve(dve, q, NH)
                    post_dve(dve, p, q, full(mTh), V_FFN_POST + layer, NH * half, NH)
                for n in ffn(stage0, layer, q0, a0, p0, (inp, lambda half: up_dve(dve, layer, half), down, post)):
                    fence(dve, n)
            run_ffn(0, F_FFN0, 3, 2, 1)
            stats_dve(dve, 7, T)
            apply_dve(dve, 4, 7, full(hT), V_KV, full(xh), full(xl), T)
            fence(dve, F_KVN)
            proj_dve(dve, "k", 0)
            proj_dve(dve, "v", 1)
            fence(dve, F_KV)
            apply_dve(dve, 5, 7, full(hT), V_MIX_PRE + 1, full(xh), full(xl), T)
            fence(dve, F_QN)
            proj_dve(dve, "q")
            fence(dve, S_ATT)
            att_dve(dve)
            fence(dve, S_SMP)
            smp_new_dve(dve)
            smp_dve(dve)
            fence(dve, F_SMP)
            split_dve(dve, 6)
            fence(dve, F_SPLIT)
            proj_dve(dve, "o")
            fence(dve, F_O)
            stats_dve(dve, 8, T)
            post_dve(dve, 3, 8, full(mT), V_MIX_POST + 1, 0, T)
            fence(dve, F_POST1)
            run_ffn(1, F_FFN1, 9, 7, 4)
            out_copy(dve, nc.vector.tensor_copy, 1, y_v)

        @block.gpsimd
        def _(pool):
            for s_, n in ((g_pool, 2), (g_of, 1), (k_free, 2), (k_tf, 2), (a_s, 4)):
                pool.sem_inc(s_, n)
            load_pool(pool)
            for n in (F_LOAD, F_NORM0):
                fence(pool, n)
            glu_pool(pool)
            for n in (F_GLU, F_LN, F_OUT, F_POST0):
                fence(pool, n)

            def run_ffn(layer, stage0, q0, a0, p0):
                def inp(half, q, a):
                    if half == 0:
                        ffn_rows_pool(pool, layer)

                def down(half):
                    if half == 1:
                        ffn_state_pool(pool, layer)
                for n in ffn(stage0, layer, q0, a0, p0, (inp, lambda half: None, down, lambda half, q, p: None)):
                    fence(pool, n)
            run_ffn(0, F_FFN0, 3, 2, 1)
            fence(pool, F_KVN)
            proj_pool(pool, 0, k_dram, 0, ok_p, ok_s)
            proj_pool(pool, 1, None, 1, ov_p, ov_s)
            fence(pool, F_KV)
            fence(pool, F_QN)
            proj_pool(pool, 2, q_dram)
            fence(pool, S_ATT)
            att_pool(pool)
            fence(pool, S_SMP)
            smp_in_pool(pool)
            smp_new_pool(pool)
            smp_pool(pool)
            for n in (F_SMP, F_SPLIT, F_O, F_POST1):
                fence(pool, n)
            run_ffn(1, F_FFN1, 9, 7, 4)


_INS = ["x_prompt", "x_sample", "state_conv_a", "state_ffn_conv", "cache_k", "cache_v", "page_table",
        "norm_mix_pre", "norm_mix_post", "norm_ffn_pre", "norm_ffn_post", "conv_w_glu", "conv_b_glu", "conv_w_dw",
        "conv_b_dw", "conv_ln_g", "conv_ln_b", "conv_w_out", "conv_b_out", "kv_norm", "w_k", "w_v", "w_q", "w_o",
        "sb_bias", "ffn_w_gate", "ffn_w_up", "ffn_w_dw", "ffn_w_down"]
_OUTS = [(1, NP, D), (DB, DQ, D), (1, 1, ST, D), (1, DB, ST, D), (2, 1, 2, FF), (2, DB, 2, FF),
         (NP, D), (NP, D), (NS, D), (NS, D)]
_RETURNED = _OUTS[:6] + [(1, NP, HEADS, HD)] * 2 + [(DB, DQ, HEADS, HD)] * 2


def build(nc, shapes):
    ins = {n: nc.dram_tensor(f"in_{n}", s, dt, kind="ExternalInput").ap() for n, (s, dt) in shapes.items()}
    outs = [nc.dram_tensor(f"out_{i}", s, F32, kind="ExternalOutput").ap() for i, s in enumerate(_OUTS)]
    yoco_step(nc, ins, outs)


def kernel(**inputs):
    import numpy as np
    import concourse.bacc as bacc
    from concourse.bass_utils import run_bass_kernel_spmd

    nc = bacc.Bacc("TRN2", target_bir_lowering=False, num_devices=1)
    arrays = {n: np.ascontiguousarray(inputs[n]) for n in _INS}
    build(nc, {n: (a.shape, mybir.dt.from_np(a.dtype)) for n, a in arrays.items()})
    r = run_bass_kernel_spmd(nc, [{f"in_{n}": a for n, a in arrays.items()}], core_ids=[0])
    return tuple(r.results[0][f"out_{i}"].reshape(s) for i, s in enumerate(_RETURNED))
```

```python
from contextlib import ExitStack

import concourse.bass as bass
from concourse import mybir

F32 = mybir.dt.float32
F32R = mybir.dt.float32r
I32 = mybir.dt.int32
ALU = mybir.AluOpType
ACT = mybir.ActivationFunctionType
ds = bass.ds

P = 128
D = 1024
KB = D // P
NP = 1024
DB, DQ = 8, 4
NS = DB * DQ
T = NP + NS
TT = NP // P
FF = 2816
FB = FF // P
CW = 31
ST = CW - 1
HEADS, HD = 16, 64
PAIRS = HEADS // 2
PAGE = 128
PAGES = 32
EPS = 1e-6
CLAMP = 40.0
NH = T // 2
HP1 = NP - NH
CH = [(0, 352), (352, 352), (704, 352)]
HCH = [(0, NH // 2), (NH // 2, NH // 2)]

(V_MIX_PRE, V_MIX_POST, V_FFN_PRE, V_FFN_POST, V_BGLU, V_BDW, V_LNG, V_LNB, V_BOUT, V_KV, V_DW) = (
    0, 2, 4, 6, 8, 10, 11, 12, 13, 14, 15)
NV = V_DW + CW

RING = 2
DVE_TAPS = 23
POOL_TAPS = CW - DVE_TAPS
KR, VR = 4, 8
CT = 8
CHUNKS = DB * PAGES // CT
CPB = PAGES // CT


def yoco_step(nc, ins, outs):
    A = ins
    y_p, y_s, oc_p, oc_s, of_p, of_s, ok_p, ov_p, ok_s, ov_s = outs
    k_dram = nc.dram_tensor("k_feature_major", (PAIRS, P, T), F32).ap()
    q_dram = nc.dram_tensor("q_feature_major", (PAIRS, P, T), F32).ap()

    base = (nc.sbuf_base + 63) // 64 * 64
    ROW = 4 * T
    H_AT, AR_AT = base, base + KB * ROW
    WT_AT = AR_AT + 30 * ROW
    TB_AT = WT_AT + 6 * 4096
    SM_AT = TB_AT + 4 * ROW
    small = [SM_AT]

    def at(name, shape, dt, offset):
        return nc.alloc_sbuf_tensor_at(name, shape, dt, offset=offset)

    def tiny(name, shape, dt=F32):
        n = 4
        for s in shape[1:]:
            n *= s
        t = at(name, shape, dt, small[0])
        small[0] += (n + 31) // 32 * 32
        return t

    hT = at("hT", [P, KB, T], F32, H_AT)
    xh = at("xh", [P, KB, T], F32R, AR_AT)
    xl = at("xl", [P, KB, T], F32R, AR_AT + 8 * ROW)
    mT = at("mT", [P, KB, T], F32, AR_AT + 16 * ROW)
    O2 = AR_AT + 24 * ROW
    xtok = at("xtok", [P, TT + 1, D], F32, AR_AT)
    vrow = at("vrow", [NV, D], F32, AR_AT + (TT + 1) * 4096)
    srow = at("srow", [120, 2, D], F32, AR_AT + (TT + 2) * 4096)
    UW = ST + NP + DB * (ST + DQ)
    UP = (UW + 7) // 8 * 8
    u = [at(f"u{j}", [P, UP], F32, O2 + j * 4 * UP) for j in range(2)]
    stA = at("stA", [P, KB, DB * ST], F32, O2 + 8 * UP)
    pacc = at("pacc", [P, T], F32, O2 + 8 * UP + 7680)
    ut = at("ut", [P, ST + DB * ST], F32, O2 + 8 * UP + 7680 + ROW + 1536)
    ustg = at("ustg", [120, 3, P], F32, O2 + 8 * UP + 7680 + ROW)
    xhh = at("xhh", [P, KB, NH], F32R, AR_AT)
    xlh = at("xlh", [P, KB, NH], F32R, AR_AT + 4 * ROW)
    ph = at("ph", [P, FB, NH], F32R, AR_AT + 8 * ROW)
    pl = at("pl", [P, FB, NH], F32R, AR_AT + 19 * ROW)
    mTh = at("mTh", [P, KB, NH], F32, AR_AT)
    frow = at("frow", [19, FF], F32, AR_AT + 8 * ROW)
    tok = [at(f"tok{j}", [P, TT + 1, P], F32, O2 + j * 4608) for j in range(2)]
    ytok = [at(f"ytok{j}", [P, D], F32, AR_AT + 8 * ROW + j * 4096) for j in range(2)]
    kp = [at(f"kp{j}", [P, NP], F32, AR_AT + j * 4096) for j in range(2)]
    qp = [at(f"qp{j}", [P, NP], F32, AR_AT + 8192 + j * 4096) for j in range(2)]
    vp = [at(f"vp{j}", [P, TT, P], F32, AR_AT + 16384 + j * 4096) for j in range(2)]
    eb = [at(f"eb{j}", [P, 512], F32, AR_AT + 24576 + j * 2048) for j in range(3)]
    spb = [at(f"spb{j}", [P, 512], F32, AR_AT + 30720 + j * 2048) for j in range(4)]
    sb_ = [at(f"sb{j}", [P, 512], F32, AR_AT + 38912 + j * 2048) for j in range(3)]
    wb = [at(f"wb{j}", [P, 512], F32, AR_AT + 45056 + j * 2048) for j in range(3)]
    kr = [at(f"kr{j}", [P, D], F32, AR_AT + j * 4096) for j in range(KR)]
    vr = [at(f"vr{j}", [P, D], F32, AR_AT + 16384 + j * 4096) for j in range(VR)]
    vl = [at(f"vl{j}", [P, D], F32R, AR_AT + 16384 + j * 4096) for j in range(VR)]
    vh = [at(f"vh{j}", [P, D], F32R, AR_AT + 49152 + j * 4096) for j in range(4)]
    kth = [at(f"kth{j}", [P, PAIRS, 2 * P], F32R, AR_AT + 65536 + j * 8192) for j in range(2)]
    ktl = [at(f"ktl{j}", [P, PAIRS, 2 * P], F32R, AR_AT + 81920 + j * 8192) for j in range(2)]
    wst = [at(f"wst{j}", [P, CT, P], F32R, AR_AT + 98304 + j * 4096) for j in range(2)]
    zsb = [at(f"zsb{j}", [P, 2 * P], F32, AR_AT + 106496 + j * 1024) for j in range(2)]
    om = at("om", [P, D], F32, AR_AT + 108544)
    qst = at("qst", [P, PAIRS, P], F32R, AR_AT + 112640)
    oc = at("oc", [P, DB, HD], F32, AR_AT + 116736)
    ssp = at("ssp", [P, 512], F32, AR_AT + 118784)
    ssf = at("ssf", [P, 512], F32, AR_AT + 120832)
    wns = at("wns", [NS, P], F32, AR_AT + 122880)
    both = at("both", [P, 64], F32, AR_AT + 123392)
    own_head = at("own_head", [P, HEADS], F32, AR_AT + 123648)
    carry = at("carry", [P, 64], F32, AR_AT + 123712)
    ceb = at("ceb", [P, 512], F32, TB_AT)
    swb = at("swb", [P, 512], F32, TB_AT + 13312)
    qbd = at("qbd", [P, PAIRS, DB, 8], F32, TB_AT)
    kTs = at("kTs", [P, PAIRS, NS], F32, TB_AT + 2048)
    vn = at("vn", [NS, D], F32, TB_AT + 3072)
    spn = at("spn", [P, DB, 64], F32, TB_AT + 7168)
    wn = at("wn", [NS, DB, 64], F32, TB_AT + 9216)
    brow = at("brow", [1, 512], F32, TB_AT + 11264)
    cn = at("cn", [NS, DB, 64], F32, TB_AT + 13312)
    qTs = at("qTs", [P, PAIRS, NS], F32, TB_AT + 15360)
    raw = [at(f"raw{j}", [P, KB, P], F32, WT_AT + j * 4096) for j in range(RING)]
    whi = [at(f"whi{j}", [P, KB, P], F32R, WT_AT + 8192 + j * 4096) for j in range(RING)]
    wlo = [at(f"wlo{j}", [P, KB, P], F32R, WT_AT + 16384 + j * 4096) for j in range(RING)]
    tmp = [at(f"tmp{j}", [P, T], F32, TB_AT + j * ROW) for j in range(2)]
    acc = at("acc", [P, T], F32, TB_AT + 2 * ROW)
    rs = at("rs", [P, T], F32, TB_AT + 3 * ROW)
    GW = 2 + HP1 + DB * 6
    GP = (GW + 7) // 8 * 8
    gx = [at(f"gx{j}", [P, GP], F32, TB_AT + j * 4 * GP) for j in range(2)]
    CV = TB_AT + 8 * GP
    cv = [at(f"cv{j}", [P, NH], F32, CV + j * 4 * NH) for j in range(2)]
    gel = at("gel", [P, NH], F32, CV + 8 * NH)
    pf = [at(f"pf{j}", [P, NH], F32, CV + (12 + 4 * j) * NH) for j in range(2)]
    ident = tiny("ident", [P, P])
    mean1 = tiny("mean1", [P, P])
    ninc = tiny("ninc", [P, P])
    nall = tiny("nall", [P, P])
    one1 = tiny("one1", [1, P])
    eps = tiny("eps", [P, 1])
    vec = tiny("vec", [P, KB, NV])
    fT = tiny("fT", [P, FB, 19])
    fstg = tiny("fstg", [P, FB, 18])
    gtail = tiny("gtail", [P, FB, 2])
    sbias = tiny("sbias", [P, HEADS])
    ptab = tiny("ptab", [1, DB * PAGES], I32)
    assert small[0] <= nc.sbuf_usable_end, small[0] - nc.sbuf_usable_end

    with ExitStack() as ctx:
        PS = ctx.enter_context(nc.psum_tensor("PS", [P, 8, 512], F32))

        def sem(name):
            return ctx.enter_context(nc.semaphore(name))

        fence_s = sem("stage_ends")
        ld_x, ld_v, ld_f = sem("x_landed"), sem("vectors_landed"), sem("ffn_rows_landed")
        cst = sem("constants_made")
        passed = sem("waits_passed")
        w_raw = [sem(f"weights_landed{j}") for j in range(RING)]
        w_hi, w_lo, w_used = sem("weights_hi_made"), sem("weights_lo_made"), sem("weights_used")
        ps_free = sem("psum_set_free")
        n_sq, n_add, n_mean, n_rt, n_rs = (sem(f"norm_{x}") for x in ("squares", "sums", "mean", "root", "scale"))
        n_t, n_hi, n_lo = sem("scaled"), sem("scaled_hi"), sem("scaled_lo")
        p_t, p_h = sem("post_scaled"), sem("residual_added")
        tr_pe, tr_a, tr_v = sem("transposed"), sem("transposes_read_act"), sem("transposes_read_dve")
        g_sig, g_u, g_smp, g_tap, g_pool, g_cv, g_tr, g_tre, g_dve, g_out, g_of, g_ut = (sem(f"glu_{x}") for x in (
            "sigmoid", "u", "sample_conv", "tap_products", "tap_sums", "conv", "state_transposed", "state_read",
            "vector_step", "state_stored", "state_buffer_free", "state_gathered"))
        l_s, l_m, l_xc, l_t = sem("ln_sum"), sem("ln_mean"), sem("ln_centred"), sem("ln_scaled")
        f_g, f_cv, f_gel, f_p, f_hi, f_lo, f_v, f_st = (sem(f"ffn_{x}") for x in (
            "gate_copied", "conv", "gelu", "product", "product_hi", "product_lo", "vector_step", "state_stored"))
        k_ev, k_tr, k_te, k_free, k_tf = (sem(f"proj_{x}") for x in (
            "copied", "transposed", "transposes_read", "buffer_free", "token_buffer_free"))
        k_st = [sem(f"proj_stored{j}") for j in range(2)]
        k_tst = [sem(f"proj_token_stored{j}") for j in range(2)]
        a_ld = [sem(f"att_loaded{j}") for j in range(2)]
        a_z, a_c, a_e, a_l, a_sp, a_sm, a_s, a_cum, a_w, a_wm, a_pv, a_o = (sem(f"att_{x}") for x in (
            "scores", "clamped", "exp", "log", "softplus", "masked", "suffix", "weights_ready", "weights", "weights_masked",
            "outputs", "outputs_copied"))
        s_in, s_q, s_n, s_nv, s_na, s_np, s_nm, s_tab = (sem(f"smp_{x}") for x in (
            "loaded", "queries", "new_tensor", "new_vector", "new_scalar", "new_gpsimd", "new_masked", "table_landed"))
        s_k = [sem(f"k_page_landed{j}") for j in range(KR)]
        s_v = [sem(f"v_page_landed{j}") for j in range(VR)]
        s_t, s_kh, s_kl, s_qk, s_zc, s_c1, s_m, s_e, s_l, s_sp, s_sf, s_cum, s_w, s_wh, s_wl = (sem(f"smp_{x}") for x in (
            "k_turned", "k_hi", "k_lo", "scored", "scores_copied", "scores_combined", "clamped", "exp", "log", "softplus",
            "page_sums", "weights_ready", "weights", "weights_hi", "weights_lo"))
        s_vh, s_vl0, s_vl1, s_pv, s_o, s_oc, s_qh, s_qst, s_wn = (sem(f"smp_{x}") for x in (
            "v_hi", "v_lo_even", "v_lo_odd", "v_summed", "outputs_read", "own_features", "queries_hi", "queries_placed",
            "new_weights_placed"))
        y_pe, y_a, y_v = sem("y_transposed"), sem("y_even_copied"), sem("y_odd_copied")
        y_st = [sem(f"y_stored{j}") for j in range(2)]
        fs_pe, fs_v, st_out = sem("ffn_state_transposed"), sem("ffn_state_read"), sem("ffn_tail_stored")

        block = ctx.enter_context(nc.Block())

        def fence(eng, n):
            eng.drain().then_inc(fence_s, 1)
            eng.wait_ge(fence_s, 4 * n)

        def alone(eng):
            eng.sem_inc(passed, 1)

        def ps(s, c, w):
            return PS[:, 3 * s + c, 0:w]

        first, sets, at_t, at_s = {}, {}, 0, 0
        for name, tiles, nsets in ([("glu", 16, 0), ("out", 8, 8)]
                                   + [x for h in (0, 1) for x in ((f"up0{h}", 44, 0), (f"down0{h}", 24, 8))]
                                   + [("k", 8, 8), ("v", 8, 8), ("q", 8, 8), ("o", 8, 8)]
                                   + [x for h in (0, 1) for x in ((f"up1{h}", 44, 0), (f"down1{h}", 24, 8))]):
            first[name], sets[name] = at_t, at_s
            at_t += tiles
            at_s += nsets
        TILES = at_t
        ffn_of = {"00": 0, "01": FB, "10": 2 * FB, "11": 3 * FB}
        DOWN_KB = [8, 8, FB - 16]

        def tile_no(name, per, i, q):
            return first[name] + q + per * i, (first[name] + q) // RING + (per // RING) * i

        def load_tile(sp, t, b, src, nb):
            sp.wait_ge(w_lo, t + 1)
            sp.dma_start(raw[b][:, 0:nb, :], src).then_inc(w_raw[b], 16)

        def cols(w, n, k0=0, nb=KB):
            return w[k0 * P:(k0 + nb) * P, ds(n * P, P)].rearrange("(k p) n -> p k n", p=P)

        def split_hi(act, t, turn, b):
            act.wait_ge(w_raw[b], 16 * (turn + 1))
            act.wait_ge(w_used, t + 1)
            nc.scalar.copy(whi[b][:], raw[b][:]).then_inc(w_hi, 1)

        def split_lo(dve, t, b):
            dve.wait_ge(w_hi, t + 1)
            nc.vector.tensor_tensor(wlo[b][:], raw[b][:], whi[b][:].bitcast(F32), ALU.subtract).then_inc(w_lo, 1)

        def product(pe, t, b, s, nb, k0, hi, lo, chunks, start, stop):
            pe.wait_ge(w_lo, t + 3)
            for k in range(nb):
                for wt, x in ((whi, hi), (whi, lo), (wlo, hi)):
                    for c, (c0, w) in enumerate(chunks):
                        mm = nc.tensor.matmul(ps(s, c, w), wt[b][:, k, :], x[:, k0 + k, c0:c0 + w],
                                              start=start and k == 0 and wt is whi and x is hi,
                                              stop=stop and k == nb - 1 and wt is wlo)
            mm.then_inc(w_used, 1)

        vec_rows = [(V_MIX_PRE, A["norm_mix_pre"], 2), (V_MIX_POST, A["norm_mix_post"], 2),
                    (V_FFN_PRE, A["norm_ffn_pre"], 2), (V_FFN_POST, A["norm_ffn_post"], 2),
                    (V_BGLU, A["conv_b_glu"].rearrange("a (g d) -> (a g) d", g=2), 2),
                    (V_BDW, A["conv_b_dw"], 1), (V_LNG, A["conv_ln_g"], 1), (V_LNB, A["conv_ln_b"], 1),
                    (V_BOUT, A["conv_b_out"], 1), (V_KV, A["kv_norm"].rearrange("(a d) -> a d", a=1), 1),
                    (V_DW, A["conv_w_dw"][0], CW)]

        def load_sp(sp):
            sp.dma_start(xtok[:, 0:TT, :], A["x_prompt"][0].rearrange("(t p) d -> p t d", p=P)).then_inc(ld_x, 16)
            sp.dma_start(xtok[0:NS, TT, :], A["x_sample"].rearrange("b q d -> (b q) d")).then_inc(ld_x, 16)
            for r, src, n in vec_rows:
                sp.dma_start(vrow[r:r + n, :], src).then_inc(ld_v, 16)
            st = A["state_conv_a"][0].rearrange("b s d -> (b s) d")
            for j in range(2):
                sp.dma_start(srow[:, j, :], st[120 * j:120 * j + 120, :]).then_inc(ld_v, 16)
            sp.dma_start(sbias[:, :], A["sb_bias"].broadcast_to([P, HEADS])).then_inc(ld_v, 16)
            sp.dma_start(ptab[:, :], A["page_table"].rearrange("b n -> (b n)").rearrange("(a n) -> a n", a=1)).then_inc(s_tab, 16)

        LD_V = 16 * (len(vec_rows) + 3)

        def load_pool(pool):
            for t, v in ((ident, 0.0), (mean1, 1.0 / D), (ninc, -1.0), (nall, -1.0), (one1, 1.0), (eps, EPS)):
                nc.gpsimd.memset(t[:], v)
            for j in range(2):
                nc.gpsimd.memset(u[j][:, 0:ST], 0.0)
            pool.drain().then_inc(cst, 1)
            pool.wait_ge(cst, 1)
            nc.gpsimd.affine_select(out=ident[:], in_=ident[:], compare_op=ALU.not_equal, fill=1.0, base=0,
                                    pattern=[[-1, P]], channel_multiplier=1)
            nc.gpsimd.affine_select(out=ninc[:], in_=ninc[:], compare_op=ALU.is_ge, fill=0.0, base=0,
                                    pattern=[[-1, P]], channel_multiplier=1)
            pool.drain().then_inc(cst, 1)

        def load_pe(pe):
            pe.wait_ge(cst, 2)
            pe.wait_ge(ld_x, 32)
            for k in range(KB):
                if k >= 2:
                    pe.wait_ge(tr_a, k - 1)
                    pe.wait_ge(tr_v, k - 1)
                for t in range(TT + 1):
                    n = P if t < TT else NS
                    mm = nc.tensor.transpose(PS[:, 3 * (k % 2) + t // 4, (t % 4) * P:(t % 4) * P + n],
                                             xtok[0:n, t, k * P:(k + 1) * P], ident[0:n, 0:n])
                mm.then_inc(tr_pe, 1)
            pe.wait_ge(ld_v, LD_V)
            pe.wait_ge(tr_a, KB)
            pe.wait_ge(tr_v, KB)
            for k in range(KB):
                mm = nc.tensor.transpose(PS[:, 0, k * NV:(k + 1) * NV], vrow[:, k * P:(k + 1) * P], ident[0:NV, 0:NV])
            mm.then_inc(tr_pe, 1)
            for k in range(KB):
                for j in range(2):
                    mm = nc.tensor.transpose(PS[:, 2 + k // 2, (k % 2) * 240 + j * 120:(k % 2) * 240 + j * 120 + 120],
                                             srow[:, j, k * P:(k + 1) * P], ident[0:120, 0:120])
            mm.then_inc(tr_pe, 1)

        def load_act(act):
            for k in range(KB):
                act.wait_ge(tr_pe, k + 1)
                nc.scalar.copy(hT[:, k, 0:512], PS[:, 3 * (k % 2), :]).then_inc(tr_a, 1)

        def load_dve(dve):
            for k in range(KB):
                dve.wait_ge(tr_pe, k + 1)
                nc.vector.tensor_copy(hT[:, k, 512:1024], PS[:, 3 * (k % 2) + 1, :])
                nc.vector.tensor_copy(hT[:, k, 1024:T], PS[:, 3 * (k % 2) + 2, 0:NS]).then_inc(tr_v, 1)
            dve.wait_ge(tr_pe, KB + 1)
            nc.vector.tensor_copy(vec[:, :, :], PS[:, 0, 0:KB * NV].rearrange("p (k v) -> p k v", k=KB))
            dve.wait_ge(tr_pe, KB + 2)
            for k2 in range(KB // 2):
                nc.vector.tensor_copy(stA[:, 2 * k2:2 * k2 + 2, :],
                                      PS[:, 2 + k2, 0:480].rearrange("p (k v) -> p k v", k=2))

        def stats_act(act, q, src, n, chunks):
            for k in range(KB):
                if k >= 2:
                    act.wait_ge(n_add, 7 * q + max(1, k - 2))
                nc.scalar.activation(tmp[k % 2][:, 0:n], src(k), ACT.Square).then_inc(n_sq, 1)
            act.wait_ge(n_mean, q + 1)
            for c, (c0, w) in enumerate(chunks):
                ins_ = nc.scalar.activation(rs[:, c0:c0 + w], ps(0, c, w), ACT.Sqrt, bias=eps[:, 0:1])
            ins_.then_inc(n_rt, 1)

        def stats_dve(dve, q, n):
            for k in range(1, KB):
                dve.wait_ge(n_sq, 8 * q + k + 1)
                if k == 1:
                    nc.vector.tensor_tensor(acc[:, 0:n], tmp[0][:, 0:n], tmp[1][:, 0:n], ALU.add).then_inc(n_add, 1)
                else:
                    dve.wait_ge(n_add, 7 * q + k - 1)
                    nc.vector.tensor_tensor(acc[:, 0:n], acc[:, 0:n], tmp[k % 2][:, 0:n], ALU.add).then_inc(n_add, 1)
            dve.wait_ge(n_rt, q + 1)
            nc.vector.reciprocal(rs[:, 0:n], rs[:, 0:n]).then_inc(n_rs, 1)

        def stats_pe(pe, q, chunks):
            pe.wait_ge(n_add, 7 * q + 7)
            for c, (c0, w) in enumerate(chunks):
                mm = nc.tensor.matmul(ps(0, c, w), mean1[:], acc[:, c0:c0 + w], start=True, stop=True)
            mm.then_inc(n_mean, 1)

        def apply_act(act, a, hi, n):
            for k in range(KB):
                act.wait_ge(n_t, 8 * a + k + 1)
                nc.scalar.copy(hi(k), tmp[k % 2][:, 0:n]).then_inc(n_hi, 1)

        def apply_dve(dve, a, q, src, row, hi, lo, n):
            dve.wait_ge(n_rs, q + 1)

            def low(k):
                dve.wait_ge(n_hi, 8 * a + k + 1)
                nc.vector.tensor_tensor(lo(k), tmp[k % 2][:, 0:n], hi(k).bitcast(F32), ALU.subtract).then_inc(n_lo, 1)

            for k in range(KB):
                if k >= 2:
                    dve.wait_ge(n_lo, 8 * a + k - 1)
                nc.vector.scalar_tensor_tensor(out=tmp[k % 2][:, 0:n], in0=src(k), scalar=vec[:, k, row:row + 1],
                                               in1=rs[:, 0:n], op0=ALU.mult, op1=ALU.mult).then_inc(n_t, 1)
                if k >= 1:
                    low(k - 1)
            low(KB - 1)

        def post_dve(dve, p, q, src, row, c0, n):
            dve.wait_ge(n_rs, q + 1)
            for k in range(KB + 1):
                if k < KB:
                    if k >= 2:
                        dve.wait_ge(p_h, 8 * p + k - 1)
                    nc.vector.scalar_tensor_tensor(out=tmp[k % 2][:, 0:n], in0=src(k), scalar=vec[:, k, row:row + 1],
                                                   in1=rs[:, 0:n], op0=ALU.mult, op1=ALU.mult).then_inc(p_t, 1)
                if k >= 1:
                    dve.wait_ge(p_t, 8 * p + k)
                    h = hT[:, k - 1, c0:c0 + n]
                    nc.vector.tensor_tensor(h, h, tmp[(k - 1) % 2][:, 0:n], ALU.add).then_inc(p_h, 1)

        full = lambda t: (lambda k: t[:, k, :])
        part = lambda t, c0, n: (lambda k: t[:, k, c0:c0 + n])

        w_glu = A["conv_w_glu"][0]

        def glu_sp(sp):
            with sp.Fori(0, KB // 2) as i:
                for q in range(4):
                    t, _ = tile_no("glu", 4, i, q)
                    load_tile(sp, t, q % 2, cols(w_glu, 2 * i + q // 2 + KB * (q % 2)), KB)

        def glu_pe(pe):
            with pe.Fori(0, KB // 2) as i:
                for mm_ in range(2):
                    m = 2 * i + mm_
                    pe.wait_ge(g_u, m + 1)
                    for b in range(2):
                        t, _ = tile_no("glu", 4, i, 2 * mm_ + b)
                        product(pe, t, b, b, KB, 0, xh, xl, CH, True, True)
                    pe.wait_ge(g_ut, m + 1)
                    pe.wait_ge(g_tre, m + 1)
                    nc.tensor.transpose(PS[0:ST, 6, 0:P], ut[:, 0:ST], ident[:, :])
                    for j in range(2):
                        mm = nc.tensor.transpose(PS[0:120, 6, (j + 1) * P:(j + 2) * P],
                                                 ut[:, ST + 120 * j:ST + 120 * j + 120], ident[:, :])
                    mm.then_inc(g_tr, 1)

        def glu_act(act):
            with act.Fori(0, KB // 2) as i:
                for mm_ in range(2):
                    m = 2 * i + mm_
                    t, turn = tile_no("glu", 4, i, 2 * mm_ + 1)
                    act.wait_ge(w_used, t + 3)
                    act.wait_ge(g_smp, m + 1)
                    alone(act)
                    for c, (c0, w) in enumerate(CH):
                        ins_ = nc.scalar.activation(tmp[0][:, c0:c0 + w], ps(1, c, w), ACT.Sigmoid,
                                                    bias=vec[:, ds(m, 1), V_BGLU + 1].opt())
                    ins_.then_inc(g_sig, 1)
                    for b in range(2):
                        t, turn = tile_no("glu", 4, i, 2 * mm_ + b + 2)
                        split_hi(act, t, turn, b)
                    act.wait_ge(g_u, m + 2)
                    for j in range(POOL_TAPS):
                        tap = DVE_TAPS + j
                        act.wait_ge(g_pool, POOL_TAPS * m + j + 1)
                        alone(act)
                        nc.scalar.activation((acc, rs)[j % 2][:, 0:NP], u[mm_][:, tap:tap + NP], ACT.Copy,
                                             scale=vec[:, ds(m, 1), V_DW + tap].opt()).then_inc(g_tap, 1)

        def glu_pool(pool):
            with pool.Fori(0, KB // 2) as i:
                for mm_ in range(2):
                    m = 2 * i + mm_
                    pool.wait_ge(g_cv, m + 1)
                    for j in range(POOL_TAPS):
                        pool.wait_ge(g_tap, POOL_TAPS * (m + 2) + j + 1)
                        if j == 0:
                            alone(pool)
                            nc.gpsimd.tensor_copy(pacc[:, 0:NP], acc[:, 0:NP]).then_inc(g_pool, 1)
                        else:
                            pool.wait_ge(g_pool, POOL_TAPS * m + j + 2)
                            nc.gpsimd.tensor_tensor(pacc[:, 0:NP], pacc[:, 0:NP], (acc, rs)[j % 2][:, 0:NP],
                                                    ALU.add).then_inc(g_pool, 1)
                    pool.wait_ge(g_tre, m + 2)
                    pool.dma_start(oc_p[0, 0][:, ds(m * P, P)], ustg[0:ST, 0, :]).then_inc(g_out, 16)
                    for j in range(2):
                        pool.dma_start(oc_s[0].rearrange("b s d -> (b s) d")[120 * j:120 * j + 120, ds(m * P, P)],
                                       ustg[:, j + 1, :]).then_inc(g_out, 16)
                    pool.wait_ge(g_out, 48 * m + 48)
                    pool.sem_inc(g_of, 1)

        GV = DVE_TAPS + 3

        def glu_dve(dve):
            with dve.Fori(0, KB // 2) as i:
                for mm_ in range(2):
                    m = 2 * i + mm_
                    step = [0]

                    def then(ins_):
                        step[0] += 1
                        ins_.then_inc(g_dve, 1)

                    def own(n=0):
                        dve.wait_ge(g_dve, GV * m + step[0] - n)

                    us = u[mm_]
                    usv = us[:, ST + NP:UW].rearrange("p (b w) -> p b w", b=DB)
                    dve.wait_ge(g_tap, POOL_TAPS * (m + 1))
                    nc.vector.tensor_copy(usv[:, :, 0:ST], stA[:, ds(m, 1), :].rearrange("p k (b s) -> p (k b) s", b=DB))
                    dve.wait_ge(g_sig, m + 1)
                    ba = vec[:, ds(m, 1), V_BGLU].opt()
                    for c, (c0, w) in enumerate(CH):
                        n = min(c0 + w, NP) - c0
                        nc.vector.scalar_tensor_tensor(out=us[:, ST + c0:ST + c0 + n], in0=ps(0, c, n), scalar=ba,
                                                       in1=tmp[0][:, c0:c0 + n], op0=ALU.add, op1=ALU.mult)
                    c0 = CH[2][0]
                    nc.vector.scalar_tensor_tensor(
                        out=usv[:, :, ST:ST + DQ], in0=PS[:, 2, NP - c0:T - c0].rearrange("p (b q) -> p b q", b=DB),
                        scalar=ba, in1=tmp[0][:, NP:T].rearrange("p (b q) -> p b q", b=DB),
                        op0=ALU.add, op1=ALU.mult).then_inc(g_u, 1)
                    for b in range(2):
                        t, _ = tile_no("glu", 4, i, 2 * mm_ + b + 2)
                        split_lo(dve, t, b)
                    dve.wait_ge(g_u, m + 2)
                    dve.wait_ge(g_tr, m + 2)
                    nc.vector.tensor_copy(ut[:, 0:ST], us[:, NP:NP + ST])
                    nc.vector.tensor_copy(ut[:, ST:ST + DB * ST].rearrange("p (b s) -> p b s", b=DB),
                                          usv[:, :, DQ:DQ + ST]).then_inc(g_ut, 1)
                    prod = tmp[0][:, 0:NS * CW].rearrange("p (b q w) -> p b q w", b=DB, q=DQ)
                    win = bass.AP(us, ST + NP, [(UP, P), (ST + DQ, DB), (1, DQ), (1, CW)])
                    wv = bass.AP(vec, m * NV + V_DW, [(KB * NV, P), (0, DB), (0, DQ), (1, CW)])
                    then(nc.vector.tensor_tensor(prod, win, wv, ALU.mult))
                    own()
                    smp = mT[:, ds(m, 1), NP:T].opt()
                    then(nc.vector.tensor_reduce(smp, tmp[0][:, 0:NS * CW].rearrange("p (s w) -> p s w", w=CW),
                                                 mybir.AxisListType.X, ALU.add))
                    own()
                    bdw = vec[:, ds(m, 1), V_BDW].opt()
                    nc.vector.tensor_scalar(smp, smp, bdw, None, ALU.add).then_inc(g_smp, 1)
                    sums = (mT[:, ds(m, 1), 0:NP].opt(), tmp[1][:, 0:NP])
                    for tap in range(DVE_TAPS):
                        win = us[:, tap:tap + NP]
                        wt = vec[:, ds(m, 1), V_DW + tap].opt()
                        d = sums[tap % 2]
                        if tap == 0:
                            then(nc.vector.tensor_scalar(d, win, wt, bdw, ALU.mult, ALU.add))
                        elif tap == 1:
                            dve.wait_ge(g_cv, m + 1)
                            then(nc.vector.tensor_scalar(d, win, wt, None, ALU.mult))
                        else:
                            own(1)
                            then(nc.vector.scalar_tensor_tensor(out=d, in0=win, scalar=wt, in1=d,
                                                                op0=ALU.mult, op1=ALU.add))
                    own()
                    then(nc.vector.tensor_tensor(sums[0], sums[0], sums[1], ALU.add))
                    dve.wait_ge(g_tr, m + 3)
                    dve.wait_ge(g_of, m + 1)
                    nc.vector.tensor_copy(ustg[0:ST, 0, :], PS[0:ST, 6, 0:P])
                    nc.vector.tensor_copy(ustg[:, 1:3, :],
                                          PS[0:120, 6, P:3 * P].rearrange("p (j n) -> p j n", j=2)).then_inc(g_tre, 1)
                    own()
                    dve.wait_ge(g_pool, POOL_TAPS * (m + 1) + 2)
                    nc.vector.tensor_tensor(sums[0], sums[0], pacc[:, 0:NP], ALU.add).then_inc(g_cv, 1)
                    assert step[0] == GV

        def ln_dve_sum(dve):
            for k in range(1, KB):
                if k == 1:
                    nc.vector.tensor_tensor(acc[:], mT[:, 0, :], mT[:, 1, :], ALU.add).then_inc(l_s, 1)
                else:
                    dve.wait_ge(l_s, k - 1)
                    nc.vector.tensor_tensor(acc[:], acc[:], mT[:, k, :], ALU.add).then_inc(l_s, 1)
            dve.wait_ge(l_m, 1)
            for k in range(KB):
                for c, (c0, w) in enumerate(CH):
                    ins_ = nc.vector.tensor_tensor(mT[:, k, c0:c0 + w], mT[:, k, c0:c0 + w], ps(1, c, w), ALU.subtract)
                ins_.then_inc(l_xc, 1)

        def ln_pe_mean(pe):
            pe.wait_ge(l_s, KB - 1)
            for c, (c0, w) in enumerate(CH):
                mm = nc.tensor.matmul(ps(1, c, w), mean1[:], acc[:, c0:c0 + w], start=True, stop=True)
            mm.then_inc(l_m, 1)

        def ln_dve_scale(dve, q, a):
            dve.wait_ge(n_rs, q + 1)

            def low(k):
                dve.wait_ge(n_hi, 8 * a + k + 1)
                nc.vector.tensor_tensor(xl[:, k, :], tmp[k % 2][:], xh[:, k, :].bitcast(F32), ALU.subtract).then_inc(n_lo, 1)

            for k in range(KB):
                nc.vector.tensor_tensor(mT[:, k, :], mT[:, k, :], rs[:], ALU.mult).then_inc(l_t, 1)
                if k >= 1:
                    low(k - 1)
            low(KB - 1)

        def ln_act(act, a):
            for k in range(KB):
                act.wait_ge(l_t, k + 1)
                if k >= 2:
                    act.wait_ge(n_lo, 8 * a + k - 1)
                nc.scalar.activation(tmp[k % 2][:], mT[:, k, :], ACT.Silu, bias=vec[:, k, V_LNB:V_LNB + 1],
                                     scale=vec[:, k, V_LNG:V_LNG + 1]).then_inc(n_t, 1)
                act.wait_ge(n_t, 8 * a + k + 1)
                nc.scalar.copy(xh[:, k, :], tmp[k % 2][:]).then_inc(n_hi, 1)

        def proj_sp(sp, name, w):
            with sp.Fori(0, KB // 2) as i:
                for q in range(2):
                    t, _ = tile_no(name, 2, i, q)
                    load_tile(sp, t, q, cols(w, 2 * i + q), KB)

        def proj_pe(pe, name, turned=None):
            def turn(n, b):
                pe.wait_ge(k_ev, turned * KB + n + 1)
                for g, ts_ in enumerate(((0, 1, 2, 3), (4, 5, 6, 7), (8,))):
                    if g != 1:
                        pe.wait_ge(k_te, 3 * (turned * KB + n) + g // 2 + 2)
                    for t in ts_:
                        w = P if t < TT else NS
                        mm = nc.tensor.transpose(PS[0:w, 6 + g % 2, (t % 4) * P:(t % 4) * P + P],
                                                 tmp[b][:, t * P:t * P + w], ident[:, :])
                    mm.then_inc(k_tr, 1)

            with pe.Fori(0, KB // 2) as i:
                for b in range(2):
                    t, _ = tile_no(name, 2, i, b)
                    pe.wait_ge(ps_free, sets[name] + 2 * i + b + 1)
                    product(pe, t, b, b, KB, 0, xh, xl, CH, True, True)
                    if turned is not None:
                        turn(2 * i + b, b)

        def proj_act(act, name, dest, bias=None, scale=1.0, kv=None):
            with act.Fori(0, KB // 2) as i:
                for b in range(2):
                    n = 2 * i + b
                    t, turn = tile_no(name, 2, i, b)
                    act.wait_ge(w_used, t + 3)
                    if kv is not None:
                        act.wait_ge(k_free, kv * KB + n + 1)
                    alone(act)
                    d = dest(n, b)
                    for c, (c0, w) in enumerate(CH):
                        if bias is not None:
                            ins_ = nc.scalar.activation(d[:, c0:c0 + w], ps(b, c, w), ACT.Identity,
                                                        bias=vec[:, ds(n, 1), bias].opt())
                        else:
                            ins_ = nc.scalar.activation(d[:, c0:c0 + w], ps(b, c, w), ACT.Copy, scale=scale)
                    ins_.then_inc(ps_free if kv is None else k_ev, 1)
                    if kv is not None:
                        act.wait_ge(k_ev, kv * KB + n + 1)
                        act.sem_inc(ps_free, 1)
                    t, turn = tile_no(name, 2, i, b + 2)
                    split_hi(act, t, turn, b)

        def proj_dve(dve, name, turned=None):
            with dve.Fori(0, KB // 2) as i:
                for b in range(2):
                    t, _ = tile_no(name, 2, i, b + 2)
                    split_lo(dve, t, b)
                    if turned is not None:
                        g0 = 3 * (turned * KB + 2 * i + b)
                        dve.wait_ge(k_tf, turned * KB + 2 * i + b + 1)
                        for g in range(3):
                            dve.wait_ge(k_tr, g0 + g + 1)
                            if g < 2:
                                src = PS[:, 6 + g, :].rearrange("p (t n) -> p t n", t=4)
                                nc.vector.tensor_copy(tok[b][:, 4 * g:4 * g + 4, :], src).then_inc(k_te, 1)
                            else:
                                nc.vector.tensor_copy(tok[b][0:NS, TT, :], PS[0:NS, 6, 0:P]).then_inc(k_te, 1)

        def proj_pool(pool, kv, dram, turned=None, out_p=None, out_s=None):
            with pool.Fori(0, KB // 2) as i:
                for b in range(2):
                    n = 2 * i + b
                    if dram is not None:
                        pool.wait_ge(k_ev, kv * KB + n + 1)
                        pool.dma_start(dram[ds(n, 1)].rearrange("a p t -> p (a t)"), tmp[b][:]).then_inc(k_st[b], 16)
                        done = 16 * (stored[kv] // 2 + i + 1)
                    if turned is not None:
                        pool.wait_ge(k_te, 3 * (turned * KB + n) + 3 + 2)
                        pool.dma_start(out_p[:, ds(n * P, P)].rearrange("(t p) f -> p t f", p=P),
                                       tok[b][:, 0:TT, :]).then_inc(k_tst[b], 16)
                        pool.dma_start(out_s[:, ds(n * P, P)], tok[b][0:NS, TT, :]).then_inc(k_tst[b], 16)
                    if dram is not None:
                        pool.wait_ge(k_st[b], done)
                    if turned is not None:
                        pool.wait_ge(k_tst[b], 32 * (turned * KB // 2 + i + 1))
                        pool.sem_inc(k_tf, 1)
                    pool.sem_inc(k_free, 1)
        stored = {0: 0, 1: 8, 2: 8}

        def ffn_rows_pool(pool, layer):
            pool.dma_start(frow[0:16, :], A["state_ffn_conv"][layer].rearrange("b s f -> (b s) f")).then_inc(ld_f, 16)
            pool.dma_start(frow[16:19, :], A["ffn_w_dw"][layer]).then_inc(ld_f, 16)

        def ffn_rows_pe(pe, layer):
            pe.wait_ge(ld_f, 32 * (layer + 1))
            for f in range(FB):
                mm = nc.tensor.transpose(PS[:, 6, f * 19:(f + 1) * 19], frow[:, f * P:(f + 1) * P], ident[0:19, 0:19])
            mm.then_inc(f_st, 1)

        def ffn_rows_dve(dve, layer):
            dve.wait_ge(f_st, layer + 1)
            nc.vector.tensor_copy(fT[:, :, :], PS[:, 6, 0:19 * FB].rearrange("p (f r) -> p f r", f=FB))

        def up_sp(sp, layer, half):
            with sp.Fori(0, FB // 2) as i:
                for q in range(4):
                    t, _ = tile_no(f"up{layer}{half}", 4, i, q)
                    w = A["ffn_w_gate"] if q % 2 == 0 else A["ffn_w_up"]
                    load_tile(sp, t, q % 2, cols(w[layer], 2 * i + q // 2), KB)

        def up_pe(pe, layer, half):
            f0 = ffn_of[f"{layer}{half}"]
            with pe.Fori(0, FB // 2) as i:
                for ff in range(2):
                    f = f0 + 2 * i + ff
                    for b in range(2):
                        t, _ = tile_no(f"up{layer}{half}", 4, i, 2 * ff + b)
                        pe.wait_ge((f_g, f_p)[b], f + 1)
                        product(pe, t, b, b, KB, 0, xhh, xlh, HCH, True, True)

        def up_act(act, layer, half):
            f0 = ffn_of[f"{layer}{half}"]
            name = f"up{layer}{half}"
            with act.Fori(0, FB // 2) as i:
                for ff in range(2):
                    f = f0 + 2 * i + ff
                    g = gx[ff]
                    t, _ = tile_no(name, 4, i, 2 * ff)
                    act.wait_ge(w_used, t + 3)
                    act.wait_ge(f_cv, f + 1)
                    nc.scalar.copy(g[:, 2:2 + 264], ps(0, 0, 264))
                    if half == 0:
                        ins_ = nc.scalar.copy(g[:, 2 + 264:2 + NH], ps(0, 1, 264))
                    else:
                        nc.scalar.copy(g[:, 2 + 264:2 + HP1], ps(0, 1, HP1 - 264))
                        ins_ = nc.scalar.copy(g[:, 2 + HP1:GW].rearrange("p (b w) -> p b w", b=DB)[:, :, 2:6],
                                              PS[:, 1, HP1 - 264:264].rearrange("p (b q) -> p b q", b=DB))
                    ins_.then_inc(f_g, 1)
                    t, turn = tile_no(name, 4, i, 2 * ff + 2)
                    split_hi(act, t, turn, 0)
                    act.wait_ge(f_cv, f + 3)
                    act.wait_ge(f_p, f + 1)
                    nc.scalar.activation(gel[:], cv[0][:], ACT.Gelu_apprx_tanh).then_inc(f_gel, 1)
                    t, turn = tile_no(name, 4, i, 2 * ff + 3)
                    split_hi(act, t, turn, 1)
                    act.wait_ge(f_p, f + 2)
                    nc.scalar.copy(ph[:, ds(2 * i + ff, 1), :].opt(), pf[ff][:]).then_inc(f_hi, 1)

        def up_dve(dve, layer, half):
            f0 = ffn_of[f"{layer}{half}"]
            name = f"up{layer}{half}"
            PER = (4, 10)[half]
            v0 = FB * (14 * layer + 4 * half)
            if half == 0:
                for j in range(2):
                    nc.vector.memset(gx[j][:, 0:2], 0.0)
                dve.drain().then_inc(f_lo, 1)
                dve.wait_ge(f_lo, layer + 1)
            with dve.Fori(0, FB // 2) as i:
                for ff in range(2):
                    fl = 2 * i + ff
                    f = f0 + fl
                    step = [0]

                    def then(ins_):
                        step[0] += 1
                        ins_.then_inc(f_v, 1)

                    def own(n=0):
                        dve.wait_ge(f_v, v0 + PER * fl + step[0] - n)

                    g = gx[ff]
                    gs = g[:, 2 + HP1:GW].rearrange("p (b w) -> p b w", b=DB)
                    tap = lambda j: fT[:, ds(fl, 1), 16 + j].opt()
                    n = NH if half == 0 else HP1
                    if half == 1:
                        then(nc.vector.tensor_copy(g[:, 0:2], gtail[:, ds(fl, 1), :].opt()))
                        then(nc.vector.tensor_copy(gs[:, :, 0:2], fT[:, ds(fl, 1), 0:16].rearrange(
                            "p f (b s) -> p (f b) s", b=DB)))
                        own()
                    dve.wait_ge(f_g, f + 2)
                    dve.wait_ge(f_gel, f + 1)
                    parts = [(cv[0][:, 0:n], cv[1][:, 0:n], lambda j, g=g, n=n: g[:, j:j + n])]
                    if half == 1:
                        parts.append((cv[0][:, n:NH].rearrange("p (b q) -> p b q", b=DB),
                                      cv[1][:, n:NH].rearrange("p (b q) -> p b q", b=DB),
                                      lambda j, gs=gs: gs[:, :, j:j + DQ]))
                    for j in range(3):
                        for a_, b_, win in parts:
                            if j == 0:
                                then(nc.vector.tensor_scalar(a_, win(0), tap(0), None, ALU.mult))
                            else:
                                d, s_ = (b_, a_) if j == 1 else (a_, b_)
                                own(len(parts) - 1)
                                then(nc.vector.scalar_tensor_tensor(out=d, in0=win(j), scalar=tap(j), in1=s_,
                                                                    op0=ALU.mult, op1=ALU.add))
                    if half == 0:
                        then(nc.vector.tensor_copy(gtail[:, ds(fl, 1), :].opt(), g[:, NH:NH + 2]))
                    else:
                        then(nc.vector.tensor_copy(fstg[:, ds(fl, 1), 0:2].opt(), g[:, HP1:HP1 + 2]))
                        then(nc.vector.tensor_copy(fstg[:, ds(fl, 1), 2:18].rearrange("p f (b s) -> p (f b) s", b=DB),
                                                   gs[:, :, 4:6]))
                    own()
                    dve.sem_inc(f_cv, 1)
                    t, _ = tile_no(name, 4, i, 2 * ff + 2)
                    split_lo(dve, t, 0)
                    t, _ = tile_no(name, 4, i, 2 * ff + 1)
                    dve.wait_ge(w_used, t + 3)
                    dve.wait_ge(f_gel, f + 2)
                    for c, (c0, w) in enumerate(HCH):
                        ins_ = nc.vector.tensor_tensor(pf[ff][:, c0:c0 + w], gel[:, c0:c0 + w], ps(1, c, w), ALU.mult)
                    ins_.then_inc(f_p, 1)
                    t, _ = tile_no(name, 4, i, 2 * ff + 3)
                    split_lo(dve, t, 1)
                    dve.wait_ge(f_hi, f + 1)
                    nc.vector.tensor_tensor(pl[:, ds(fl, 1), :].opt(), pf[ff][:],
                                            ph[:, ds(fl, 1), :].opt().bitcast(F32), ALU.subtract)
                    assert step[0] == PER

        def down_sp(sp, layer, half):
            with sp.Fori(0, KB // 2) as i:
                for q in range(6):
                    t, _ = tile_no(f"down{layer}{half}", 6, i, q)
                    nb = DOWN_KB[q % 3]
                    load_tile(sp, t, q % 2, cols(A["ffn_w_down"][layer], 2 * i + q // 3, 8 * (q % 3), nb), nb)

        def down_pe(pe, layer, half):
            name = f"down{layer}{half}"
            with pe.Fori(0, KB // 2) as i:
                for q in range(6):
                    t, _ = tile_no(name, 6, i, q)
                    if q % 3 == 0:
                        pe.wait_ge(ps_free, sets[name] + 2 * i + q // 3 + 1)
                    product(pe, t, q % 2, q // 3, DOWN_KB[q % 3], 8 * (q % 3), ph, pl, HCH, q % 3 == 0, q % 3 == 2)

        def loop_with_tail(eng, last, body):
            if last:
                with eng.Fori(0, KB // 2 - 1) as i:
                    body(i, False)
                body(KB // 2 - 1, True)
            else:
                with eng.Fori(0, KB // 2) as i:
                    body(i, False)

        def down_act(act, layer, half, last):
            name = f"down{layer}{half}"

            def body(i, tail):
                for q in range(6):
                    if q % 3 == 2:
                        t, _ = tile_no(name, 6, i, q)
                        act.wait_ge(w_used, t + 3)
                        for c, (c0, w) in enumerate(HCH):
                            ins_ = nc.scalar.copy(mTh[:, ds(2 * i + q // 3, 1), c0:c0 + w].opt(), ps(q // 3, c, w))
                        ins_.then_inc(ps_free, 1)
                    t, turn = tile_no(name, 6, i, q + 2)
                    if not (tail and q >= 4):
                        split_hi(act, t, turn, q % 2)
            loop_with_tail(act, last, body)

        def down_dve(dve, layer, half, last):
            name = f"down{layer}{half}"

            def body(i, tail):
                for q in range(6):
                    t, _ = tile_no(name, 6, i, q + 2)
                    if not (tail and q >= 4):
                        split_lo(dve, t, q % 2)
            loop_with_tail(dve, last, body)

        FG = [(g, min(4, FB - g)) for g in range(0, FB, 4)]

        def ffn_state_pe(pe, layer):
            for j, (g, n) in enumerate(FG):
                if j >= 2:
                    pe.wait_ge(fs_v, 6 * layer + j - 1)
                for x in range(n):
                    mm = nc.tensor.transpose(PS[0:18, 6 + j % 2, x * P:(x + 1) * P], fstg[:, g + x, :], ident[:, :])
                mm.then_inc(fs_pe, 1)

        def ffn_state_dve(dve, layer):
            for j, (g, n) in enumerate(FG):
                dve.wait_ge(fs_pe, 6 * layer + j + 1)
                nc.vector.tensor_copy(rows18[:, g * P:(g + n) * P], PS[0:18, 6 + j % 2, 0:n * P]).then_inc(fs_v, 1)

        def ffn_state_pool(pool, layer):
            pool.wait_ge(fs_v, 6 * layer + 6)
            pool.dma_start(of_p[layer, 0], rows18[0:2, :]).then_inc(st_out, 16)
            pool.dma_start(of_s[layer].rearrange("b s f -> (b s) f"), rows18[2:18, :]).then_inc(st_out, 16)
            pool.wait_ge(st_out, 32 * (layer + 1))
        rows18 = at("rows18", [18, FF], F32, TB_AT)

        UNITS = [(hh, c, j) for hh in range(2) for c in range(2) for j in range(4 * c + 3, -1, -1)]
        NU = len(UNITS)
        UN = [(pp, hh, c, j) for pp in range(2) for hh, c, j in UNITS]
        LOOPS = PAIRS // 2
        L1, L2 = 2, 3

        def span(c, j):
            t0 = max(512 * c, P * j)
            return t0 - 512 * c, 512 * (c + 1) - t0, P * j >= 512 * c

        NMASK = sum(span(c, j)[2] for _, _, c, j in UN)
        mask_no = []
        for x in UN:
            mask_no.append(sum(span(y[2], y[3])[2] for y in UN[:len(mask_no) + 1]))

        def att_sp(sp, stage):
            sp.wait_ge(fence_s, 4 * stage)
            with sp.Fori(0, LOOPS) as i:
                for pp in range(2):
                    n = 2 * i + pp
                    sp.wait_ge(a_o, 4 * n + 4)
                    sp.dma_start(kp[pp][:], k_dram[ds(n, 1), :, 0:NP].rearrange("a p t -> p (a t)")).then_inc(a_ld[pp], 16)
                    sp.dma_start(qp[pp][:], q_dram[ds(n, 1), :, 0:NP].rearrange("a p t -> p (a t)")).then_inc(a_ld[pp], 16)
                    sp.dma_start(vp[pp][:], ov_p[:, ds(n * P, P)].rearrange("(t p) f -> p t f", p=P)).then_inc(a_ld[pp], 16)

        def att_pe(pe):
            NL = len(UN)
            with pe.Fori(0, LOOPS) as i:
                u0 = NL * i
                for x in range(NL + L2):
                    if x < NL:
                        pp, hh, c, j = UN[x]
                        o, w, _ = span(c, j)
                        if (hh, c, j) == UNITS[0]:
                            pe.wait_ge(a_ld[pp], 48 * i + 48)
                        pe.wait_ge(a_w, u0 + x + 1)
                        r = slice(HD * hh, HD * hh + HD)
                        nc.tensor.matmul(PS[:, x % 4, o:o + w], kp[pp][r, j * P:(j + 1) * P],
                                         qp[pp][r, 512 * c + o:512 * c + o + w], start=True, stop=False,
                                         skip_group_check=True).then_inc(a_z, 1)
                    y = x - L1
                    if 0 <= y < NL:
                        pp, hh, c, j = UN[y]
                        o, w, diag = span(c, j)
                        top = j == 4 * c + 3
                        pe.wait_ge(a_sp, u0 + y + 1)
                        if diag:
                            pe.wait_ge(a_sm, NMASK * i + mask_no[y])
                        mm = nc.tensor.matmul(PS[:, y % 4, o:o + w], ninc[:], spb[y % 4][:, o:o + w], start=False,
                                              stop=top, skip_group_check=True)
                        if not top:
                            pe.wait_ge(a_s, u0 + y + 4)
                            mm = nc.tensor.matmul(PS[:, y % 4, o:o + w], nall[:], sb_[y % 3][:, o:o + w], start=False,
                                                  stop=True, skip_group_check=True)
                        mm.then_inc(a_cum, 1)
                    y = x - L2
                    if 0 <= y < NL:
                        pp, hh, c, j = UN[y]
                        o, w, diag = span(c, j)
                        top = j == 4 * c + 3
                        if top:
                            pe.wait_ge(a_o, 4 * (2 * i + pp) + 2 * hh + c + 5)
                        pe.wait_ge(a_w, u0 + y + 5)
                        if diag:
                            pe.wait_ge(a_wm, NMASK * i + mask_no[y])
                        nc.tensor.matmul(PS[HD * hh:HD * hh + HD, 4 + c, o:o + w], vp[pp][:, j, HD * hh:HD * hh + HD],
                                         wb[y % 3][:, o:o + w], start=top, stop=j == 0,
                                         skip_group_check=True).then_inc(a_pv, 1)

        def att_act(act):
            NL = len(UN)
            with act.Fori(0, LOOPS) as i:
                u0 = NL * i
                for x in range(NL + L1 + 1):
                    if x < NL:
                        pp, hh, c, j = UN[x]
                        o, w, _ = span(c, j)
                        e = eb[x % 3][:, o:o + w]
                        act.wait_ge(a_c, u0 + x + 1)
                        nc.scalar.activation(e, e, ACT.Exp).then_inc(a_e, 1)
                        act.wait_ge(a_e, u0 + x + 1)
                        nc.scalar.activation(e, e, ACT.Ln, bias=1.0).then_inc(a_l, 1)
                    y = x - L1
                    if 0 <= y < NL:
                        pp, hh, c, j = UN[y]
                        o, w, _ = span(c, j)
                        act.wait_ge(a_cum, u0 + y + 5)
                        act.wait_ge(a_pv, u0 + y + 1)
                        alone(act)
                        nc.scalar.activation(wb[y % 3][:, o:o + w], PS[:, y % 4, o:o + w], ACT.Exp,
                                             bias=sbias[:, ds(4 * i + 2 * pp + hh, 1)]).then_inc(a_w, 1)

        def att_dve(dve):
            NL = len(UN)
            with dve.Fori(0, LOOPS) as i:
                u0 = NL * i
                for x in range(NL + L2 + 1):
                    if x < NL:
                        pp, hh, c, j = UN[x]
                        o, w, _ = span(c, j)
                        bias = sbias[:, ds(4 * i + 2 * pp + hh, 1)]
                        dve.wait_ge(a_z, u0 + x + 1)
                        nc.vector.tensor_scalar(eb[x % 3][:, o:o + w], PS[:, x % 4, o:o + w], bias, CLAMP,
                                                ALU.add, ALU.min).then_inc(a_c, 1)
                    y = x - 1
                    if 0 <= y < NL:
                        pp, hh, c, j = UN[y]
                        o, w, _ = span(c, j)
                        bias = sbias[:, ds(4 * i + 2 * pp + hh, 1)]
                        dve.wait_ge(a_l, u0 + y + 1)
                        dve.wait_ge(a_s, u0 + y + 1)
                        dve.wait_ge(a_cum, u0 + y + 1)
                        nc.vector.scalar_tensor_tensor(out=spb[y % 4][:, o:o + w], in0=PS[:, y % 4, o:o + w], scalar=bias,
                                                       in1=eb[y % 3][:, o:o + w], op0=ALU.add,
                                                       op1=ALU.max).then_inc(a_sp, 1)
                    y = x - L2 - 1
                    if 0 <= y < NL and UN[y][3] == 0:
                        pp, hh, c, j = UN[y]
                        dve.wait_ge(a_pv, u0 + y + 4)
                        r = slice(HD * hh, HD * hh + HD)
                        nc.vector.tensor_copy(mT[r, ds(2 * i + pp, 1), 512 * c:512 * c + 512].opt(),
                                              PS[r, 4 + c, :]).then_inc(a_o, 1)

        def att_pool(pool):
            NL = len(UN)

            def mask(t, semaphore):
                alone(pool)
                nc.gpsimd.affine_select(out=t, in_=t, compare_op=ALU.is_ge, fill=0.0, base=-1,
                                        pattern=[[1, P]], channel_multiplier=-1).then_inc(semaphore, 1)

            with pool.Fori(0, LOOPS) as i:
                u0 = NL * i
                for x in range(NL + L1 + 1):
                    y = x - L1 - 1
                    if 0 <= y < NL and span(UN[y][2], UN[y][3])[2]:
                        o = span(UN[y][2], UN[y][3])[0]
                        pool.wait_ge(a_w, u0 + y + 5)
                        mask(wb[y % 3][:, o:o + P], a_wm)
                    if x < NL:
                        pp, hh, c, j = UN[x]
                        o, w, diag = span(c, j)
                        pool.wait_ge(a_sp, u0 + x + 1)
                        if diag:
                            mask(spb[x % 4][:, o:o + P], a_sm)
                            pool.wait_ge(a_sm, NMASK * i + mask_no[x])
                        pool.wait_ge(a_s, u0 + x + 4)
                        if j > 0:
                            d = sb_[(x + 1) % 3]
                            pool.wait_ge(a_cum, u0 + x + 3)
                            no = span(c, j - 1)[0]
                            alone(pool)
                            if no < o:
                                nc.gpsimd.memset(d[:, no:o], 0.0)
                            if j == 4 * c + 3:
                                ins_ = nc.gpsimd.tensor_copy(d[:, o:o + w], spb[x % 4][:, o:o + w])
                            else:
                                ins_ = nc.gpsimd.tensor_tensor(d[:, o:o + w], sb_[x % 3][:, o:o + w],
                                                               spb[x % 4][:, o:o + w], ALU.add)
                            ins_.then_inc(a_s, 1)
                        else:
                            pool.sem_inc(a_s, 1)

        SEQ_PAIRS = PAGES // 2
        CHUNK_PAIRS = CT // 2
        LAG = 8

        def steps(eng, body):
            for s in range(LAG):
                body(0, lambda lag, s=s: s - lag if s >= lag else None)
            with eng.Fori(0, DB - 1) as b:
                for s in range(SEQ_PAIRS):
                    body(b, lambda lag, s=s: LAG + s - lag)
            for s in range(SEQ_PAIRS):
                body(DB - 1, lambda lag, s=s: LAG + s - lag if LAG + s - lag < SEQ_PAIRS else None)

        def chunk_of(b, o):
            return CPB * b + o // CHUNK_PAIRS, (o // CHUNK_PAIRS) % 2

        def is_first(o):
            return o is not None and o % CHUNK_PAIRS == 0

        def is_start(o):
            return o is not None and o % SEQ_PAIRS == 0

        def seq(b, o):
            return b + o // SEQ_PAIRS if o >= SEQ_PAIRS else b

        def smp_in_pool(pool):
            pool.dma_start(kTs[:], k_dram[:, :, NP:T].rearrange("a p t -> p a t")).then_inc(s_in, 16)
            pool.dma_start(qTs[:], q_dram[:, :, NP:T].rearrange("a p t -> p a t")).then_inc(s_in, 16)
            pool.dma_start(vn[:], ov_s).then_inc(s_in, 16)

        def smp_new_dve(dve):
            nc.vector.memset(qbd[:], 0.0)
            nc.vector.memset(spn[:], 0.0)
            nc.vector.memset(qst[:].bitcast(F32), 0.0)
            nc.vector.memset(wns[:], 0.0)
            dve.drain().then_inc(s_nv, 1)
            dve.wait_ge(s_nv, 1)
            dve.wait_ge(s_in, 48)
            for hh in range(2):
                r = slice(HD * hh, HD * hh + HD)
                for a in range(PAIRS):
                    nc.vector.tensor_copy(qbd[r, a, :, 4 * hh:4 * hh + 4], qTs[r, a, :].rearrange("p (b q) -> p b q", b=DB))
            nc.vector.tensor_copy(brow[0:1, :].rearrange("p (t h q) -> p t h q", t=CT, h=HEADS),
                                  bass.AP(sbias, 0, [(HEADS, 1), (0, CT), (1, HEADS), (0, DQ)]))
            dve.drain().then_inc(s_q, 1)
            dve.wait_ge(s_n, 1)
            zn = PS[0:NS, 7, :].rearrange("p (b c) -> p b c", b=DB)
            nc.vector.tensor_scalar(cn[:], zn, CLAMP, None, ALU.min).then_inc(s_nv, 1)
            dve.wait_ge(s_na, 2)
            nc.vector.tensor_tensor(spn[0:NS], zn, cn[:], ALU.max).then_inc(s_nv, 1)

        def smp_new_act(act):
            act.wait_ge(s_nv, 2)
            nc.scalar.activation(cn[:], cn[:], ACT.Exp).then_inc(s_na, 1)
            act.wait_ge(s_na, 1)
            nc.scalar.activation(cn[:], cn[:], ACT.Ln, bias=1.0).then_inc(s_na, 1)
            act.wait_ge(s_n, 2)
            nc.scalar.activation(wn[:], PS[0:NS, 7, :].rearrange("p (b c) -> p b c", b=DB), ACT.Exp).then_inc(s_na, 1)

        def smp_new_pool(pool):
            count = [0]

            def done():
                pool.drain().then_inc(s_np, 1)
                count[0] += 1
                pool.wait_ge(s_np, count[0])

            nc.gpsimd.memset(both[:], 0.0)
            nc.gpsimd.memset(own_head[:], 0.0)
            done()
            for g in range(2):
                nc.gpsimd.affine_select(out=both[:], in_=both[:], compare_op=ALU.not_equal, fill=1.0, base=-64 * g,
                                        pattern=[[-1, 64]], channel_multiplier=1)
                for q in range(DQ):
                    nc.gpsimd.affine_select(out=own_head[:], in_=own_head[:], compare_op=ALU.not_equal, fill=1.0,
                                            base=-64 * g - q, pattern=[[-DQ, HEADS]], channel_multiplier=1)
                    done()

            def mask(t):
                v = t.rearrange("p b (h q) -> p b h q", h=HEADS)
                nc.gpsimd.affine_select(out=v, in_=v, compare_op=ALU.is_ge, fill=0.0, base=0,
                                        pattern=[[-DQ, DB], [0, HEADS], [0, DQ]], channel_multiplier=1)
                done()
                nc.gpsimd.affine_select(out=v, in_=v, compare_op=ALU.is_ge, fill=0.0, base=-1,
                                        pattern=[[DQ, DB], [0, HEADS], [1, DQ]], channel_multiplier=-1)
                done()
            pool.wait_ge(s_nv, 3)
            mask(spn[0:NS])
            pool.sem_inc(s_nm, 1)
            pool.wait_ge(s_na, 3)
            mask(wn[:])

        def smp_new_pe(pe):
            pe.wait_ge(s_q, 1)
            nc.tensor.matmul(PS[0:NS, 7, :], one1[0:1, 0:NS], brow[:], start=True, stop=False, skip_group_check=True)
            zn = PS[0:NS, 7, :].rearrange("p (b c) -> p b c", b=DB)
            for a in range(PAIRS):
                mm = nc.tensor.matmul(zn[:, :, 8 * a:8 * a + 8], kTs[:, a, :], qbd[:, a, :, :], start=False,
                                      stop=False, skip_group_check=True)
            mm.then_inc(s_n, 1)
            pe.wait_ge(s_nm, 1)
            nc.tensor.matmul(PS[0:NS, 7, :], ninc[0:NS, 0:NS], spn[0:NS].rearrange("p b c -> p (b c)"), start=False,
                             stop=True, skip_group_check=True).then_inc(s_n, 1)

        def smp_sp(sp, stage):
            sp.wait_ge(fence_s, 4 * stage)
            sp.wait_ge(s_tab, 16)

            def load(b, o, cache, ring, landed, freed, count):
                first_entry = PAGES * seq(b, o) + PAGES - 1 - 2 * (o % SEQ_PAIRS)
                numbers = [sp.value_load(ptab[0:1, ds(first_entry - e, 1)], min_val=0, max_val=cache.shape[0] - 1)
                           for e in range(2)]
                sp.wait_ge(freed, count)
                for e, number in enumerate(numbers):
                    slot = (2 * o + e) % len(ring)
                    sp.dma_start(ring[slot][:], cache[ds(number, 1)].rearrange("a s h d -> (a s) (h d)")).then_inc(
                        landed[slot], 16)

            def body(b, at):
                k, v = at(0), at(6)
                if k is not None:
                    load(b, k, A["cache_k"], kr, s_k, s_t, 4 * (SEQ_PAIRS * b + k) + 1)
                if v is not None:
                    load(b, v, A["cache_v"], vr, s_v, s_pv, SEQ_PAIRS * b + v + 5)
            steps(sp, body)

        def smp_pe(pe):
            def turn(b, o, hf):
                e, h, unit = hf // 2, hf % 2, 4 * (SEQ_PAIRS * b + o) + hf
                slot = (2 * o + e) % KR
                if h == 0:
                    pe.wait_ge(s_k[slot], 16 * (PAGES // KR * b + (2 * o + e) // KR + 1))
                pe.wait_ge(s_kl, unit + 1)
                for j in range(4):
                    a = 4 * h + j
                    mm = nc.tensor.transpose(PS[:, 4 + hf % 2, j * P:(j + 1) * P], kr[slot][:, a * P:(a + 1) * P], ident[:])
                mm.then_inc(s_t, 1)

            def scores(b, o, h):
                pair = SEQ_PAIRS * b + o
                if h == 0:
                    pe.wait_ge(s_kl, 4 * pair + 6)
                    pe.wait_ge(s_zc, pair + 1)
                    if is_start(o):
                        pe.wait_ge(s_qst, seq(b, o) + 1)
                for a in range(4 * h, 4 * h + 4):
                    for part_ in (kth, ktl):
                        mm = nc.tensor.matmul(PS[:, 6 + o % 2, 0:2 * P], qst[:, a, :], part_[o % 2][:, a, :],
                                              start=a == 0 and part_ is kth, stop=a == PAIRS - 1 and part_ is ktl)
                if h == 1:
                    mm.then_inc(s_qk, 1)

            def combine(b, o):
                g, z = chunk_of(b, o)
                if is_first(o):
                    pe.wait_ge(s_w, g + 1)
                    nc.tensor.matmul(PS[:, z, :], one1[:], brow[:], start=True, stop=False, skip_group_check=True)
                pe.wait_ge(s_zc, SEQ_PAIRS * b + o + 3)
                for e in range(2):
                    c = 64 * (2 * (o % CHUNK_PAIRS) + e)
                    mm = nc.tensor.matmul(PS[:, z, c:c + 64], zsb[o % 2][:, e * P:(e + 1) * P], both[:], start=False,
                                          stop=False, skip_group_check=True)
                mm.then_inc(s_c1, 1)

            def sums(b, o):
                g, z = chunk_of(b, o)
                pe.wait_ge(s_sp, g + 2)
                nc.tensor.matmul(PS[:, z, :], ninc[:], ssp[:], start=False, stop=False, skip_group_check=True)
                pe.wait_ge(s_sf, (CT + 1) * g + CT + 1)
                nc.tensor.matmul(PS[:, z, :], nall[:], ssf[:], start=False, stop=True,
                                 skip_group_check=True).then_inc(s_cum, 1)

            def outputs(b, o, e):
                pair, (g, par) = SEQ_PAIRS * b + o, chunk_of(b, o)
                if e == 0:
                    if is_start(o):
                        pe.wait_ge(s_wn, seq(b, o) + 1)
                        pe.wait_ge(s_o, seq(b, o) + 1)
                        for h in range(2):
                            nc.tensor.matmul(PS[:, 2 + h, :], wns[:], vn[:, 512 * h:512 * h + 512], start=True, stop=False,
                                             skip_group_check=True)
                    if is_first(o):
                        pe.wait_ge(s_wl, g + 2)
                    pe.wait_ge(s_vl0, pair + 1)
                else:
                    pe.wait_ge(s_vl1, pair + 1)
                x, slot = (2 * o + e) % CT, (2 * o + e) % VR
                for v in (vh[(2 * o + e) % 4], vl[slot]):
                    for h in range(2):
                        mm = nc.tensor.matmul(PS[:, 2 + h, :], wst[par][:, x, :], v[:, 512 * h:512 * h + 512], start=False,
                                              stop=o % SEQ_PAIRS == SEQ_PAIRS - 1 and e == 1 and v is vl[slot],
                                              skip_group_check=True)
                if e == 1:
                    mm.then_inc(s_pv, 1)

            def body(b, at):
                k, s, c, u, o = at(0), at(1), at(2), at(6), at(8)
                if k is not None:
                    turn(b, k, 0)
                    turn(b, k, 1)
                if s is not None:
                    scores(b, s, 0)
                if k is not None:
                    turn(b, k, 2)
                if s is not None:
                    scores(b, s, 1)
                if k is not None:
                    turn(b, k, 3)
                if o is not None:
                    outputs(b, o, 0)
                if c is not None:
                    combine(b, c)
                if is_first(u):
                    sums(b, u)
                if o is not None:
                    outputs(b, o, 1)
            steps(pe, body)
            for b in range(DB):
                pe.wait_ge(s_oc, b + 2)
                for hh in range(2):
                    mm = nc.tensor.matmul(PS[HD * hh:HD * hh + HD, 4 + hh, 64 * b:64 * b + 64], oc[:, b, :], both[:],
                                          start=True, stop=True)
            mm.then_inc(s_n, 1)

        def smp_act(act):
            def k_hi(b, o, hf):
                e, h, unit = hf // 2, hf % 2, 4 * (SEQ_PAIRS * b + o) + hf
                act.wait_ge(s_t, unit + 6)
                if hf == 0:
                    act.wait_ge(s_qk, SEQ_PAIRS * b + o + 1)
                nc.scalar.copy(kth[o % 2][:, 4 * h:4 * h + 4, e * P:(e + 1) * P],
                               PS[:, 4 + hf % 2, :].rearrange("p (a s) -> p a s", a=4)).then_inc(s_kh, 1)

            def v_hi(b, o, e):
                slot = (2 * o + e) % VR
                act.wait_ge(s_v[slot], 16 * (PAGES // VR * b + (2 * o + e) // VR + 1))
                if e == 0:
                    act.wait_ge(s_pv, SEQ_PAIRS * b + o + 7)
                nc.scalar.copy(vh[(2 * o + e) % 4][:], vr[slot][:]).then_inc(s_vh, 1)

            def soft(b, o):
                g, _ = chunk_of(b, o)
                act.wait_ge(s_m, g + 1)
                nc.scalar.activation(ceb[:], ceb[:], ACT.Exp).then_inc(s_e, 1)
                act.wait_ge(s_e, g + 1)
                nc.scalar.activation(ceb[:], ceb[:], ACT.Ln, bias=1.0).then_inc(s_l, 1)

            def weights(b, o):
                g, z = chunk_of(b, o)
                act.wait_ge(s_cum, g + 2)
                act.wait_ge(s_wl, g + 1)
                nc.scalar.activation(swb[:], PS[:, z, :], ACT.Exp).then_inc(s_w, 1)
                act.wait_ge(s_w, g + 3)
                act.wait_ge(s_pv, CHUNK_PAIRS * g + 4)
                nc.scalar.copy(wst[z][:, :, 0:64], swb[:].rearrange("p (x c) -> p x c", x=CT)).then_inc(s_wh, 1)

            def body(b, at):
                k, e, w, v = at(0), at(6), at(7), at(7)
                if is_first(w):
                    weights(b, w)
                if is_first(e):
                    soft(b, e)
                for hf in range(4):
                    if k is not None:
                        k_hi(b, k, hf)
                    if v is not None and hf % 2 == 1:
                        v_hi(b, v, hf // 2)
            steps(act, body)

        def smp_dve(dve):
            def queries(b, o):
                dve.wait_ge(s_qk, SEQ_PAIRS * b + o + 2)
                for lo in range(2):
                    for hh in range(2):
                        r = slice(HD * hh, HD * hh + HD)
                        q = qTs[r, :, ds(DQ * seq(b, o), DQ)]
                        hi = bass.AP(qst, HD * hh * PAIRS * P + 4 * hh, [(PAIRS * P, HD), (P + 8, PAIRS), (1, DQ)])
                        if lo == 0:
                            nc.vector.tensor_copy(hi, q).then_inc(s_qh, 1)
                        else:
                            low = bass.AP(qst, HD * hh * PAIRS * P + 4 * hh + 64, [(PAIRS * P, HD), (P + 8, PAIRS), (1, DQ)])
                            dve.wait_ge(s_qh, 2 * seq(b, o) + 2)
                            ins_ = nc.vector.tensor_tensor(low, q, hi.bitcast(F32), ALU.subtract)
                ins_.then_inc(s_qst, 1)

            def k_lo(b, o, hf):
                e, h, unit = hf // 2, hf % 2, 4 * (SEQ_PAIRS * b + o) + hf
                dve.wait_ge(s_kh, unit + 1)
                part_ = lambda t: t[o % 2][:, 4 * h:4 * h + 4, e * P:(e + 1) * P]
                nc.vector.tensor_tensor(part_(ktl), PS[:, 4 + hf % 2, :].rearrange("p (a s) -> p a s", a=4),
                                        part_(kth).bitcast(F32), ALU.subtract).then_inc(s_kl, 1)

            def copy_scores(b, o):
                pair = SEQ_PAIRS * b + o
                dve.wait_ge(s_qk, pair + 3)
                dve.wait_ge(s_c1, pair + 1)
                nc.vector.tensor_copy(zsb[o % 2][:], PS[:, 6 + o % 2, 0:2 * P]).then_inc(s_zc, 1)

            def clamp(b, o):
                g, z = chunk_of(b, o)
                dve.wait_ge(s_c1, CHUNK_PAIRS * g + 6)
                dve.wait_ge(s_sp, g + 1)
                nc.vector.tensor_scalar(ceb[:], PS[:, z, :], CLAMP, None, ALU.min).then_inc(s_m, 1)

            def softplus(b, o):
                g, z = chunk_of(b, o)
                dve.wait_ge(s_l, g + 1)
                dve.wait_ge(s_cum, g + 1)
                dve.wait_ge(s_sf, (CT + 1) * g + 1)
                nc.vector.tensor_tensor(ssp[:], PS[:, z, :], ceb[:], ALU.max).then_inc(s_sp, 1)

            def page_sums(b, o):
                g, _ = chunk_of(b, o)
                for x in range(CT + 1):
                    d = ssf[:, 64 * x:64 * x + 64] if x < CT else carry[:]
                    dve.wait_ge(s_sf, (CT + 1) * g + x + 1)
                    if x == 0 and o % SEQ_PAIRS == 0:
                        nc.vector.tensor_copy(d, spn[:, ds(seq(b, o), 1), :].rearrange("p b c -> p (b c)")).then_inc(s_sf, 1)
                    elif x == 0:
                        nc.vector.tensor_copy(d, carry[:]).then_inc(s_sf, 1)
                    else:
                        if x == 1:
                            dve.wait_ge(s_sp, g + 2)
                        nc.vector.tensor_tensor(d, ssf[:, 64 * x - 64:64 * x], ssp[:, 64 * x - 64:64 * x],
                                                ALU.add).then_inc(s_sf, 1)

            def w_lo(b, o):
                g, par = chunk_of(b, o)
                dve.wait_ge(s_wh, g + 1)
                nc.vector.tensor_tensor(wst[par][:, :, 64:128], swb[:].rearrange("p (x c) -> p x c", x=CT),
                                        wst[par][:, :, 0:64].bitcast(F32), ALU.subtract).then_inc(s_wl, 1)

            def new_weights(b, o):
                dve.wait_ge(s_pv, SEQ_PAIRS * b + o + 1)
                nc.vector.tensor_copy(wns[:, 0:64], wn[:, ds(seq(b, o), 1), :].rearrange("p b c -> p (b c)")
                                      ).then_inc(s_wn, 1)

            def own_features(b, o):
                n = seq(b, o)
                dve.wait_ge(s_pv, SEQ_PAIRS * b + o + 9)
                dve.wait_ge(s_oc, n + 1)
                for h in range(2):
                    own = bass.AP(own_head, 8 * h, [(HEADS, P), (1, 8), (0, HD)])
                    ins_ = nc.vector.tensor_tensor(om[:, 512 * h:512 * h + 512].rearrange("p (h d) -> p h d", d=HD),
                                                   PS[:, 2 + h, :].rearrange("p (h d) -> p h d", d=HD), own, ALU.mult)
                ins_.then_inc(s_o, 1)
                dve.wait_ge(s_o, n + 2)
                nc.vector.tensor_reduce(oc[:, ds(n, 1), :].rearrange("p b d -> p (b d)"),
                                        om[:].rearrange("p (h d) -> p d h", d=HD), mybir.AxisListType.X,
                                        ALU.add).then_inc(s_oc, 1)

            def body(b, at):
                k, s, c, l, w, v, o = at(0), at(1), at(5), at(6), at(7), at(7), at(8)
                if is_start(s):
                    queries(b, s)
                if is_first(w):
                    w_lo(b, w)
                if is_start(w):
                    new_weights(b, w)
                if k is not None:
                    k_lo(b, k, 0)
                if is_first(l):
                    softplus(b, l)
                if k is not None:
                    k_lo(b, k, 1)
                if is_first(l):
                    page_sums(b, l)
                if k is not None:
                    k_lo(b, k, 2)
                    k_lo(b, k, 3)
                if v is not None:
                    v_lo(dve, nc.vector, b, v, 0, s_vl0)
                if s is not None:
                    copy_scores(b, s)
                if is_first(c):
                    clamp(b, c)
                if o is not None and o % SEQ_PAIRS == SEQ_PAIRS - 1:
                    own_features(b, o)
            steps(dve, body)
            dve.wait_ge(s_n, 3)
            for hh in range(2):
                r = slice(HD * hh, HD * hh + HD)
                src = PS[r, 4 + hh, :].rearrange("p (b a c) -> p a b c", b=DB, a=PAIRS)
                nc.vector.tensor_copy(mT[r, :, NP:T].rearrange("p a (b q) -> p a b q", b=DB),
                                      src[:, :, :, 4 * hh:4 * hh + 4])

        def v_lo(eng, unit, b, o, e, done):
            slot = (2 * o + e) % VR
            eng.wait_ge(s_vh, 2 * (SEQ_PAIRS * b + o) + e + 1)
            unit.tensor_tensor(vl[slot][:], vr[slot][:], vh[(2 * o + e) % 4][:].bitcast(F32), ALU.subtract).then_inc(done, 1)

        def smp_pool(pool):
            def body(b, at):
                if at(7) is not None:
                    v_lo(pool, nc.gpsimd, b, at(7), 1, s_vl1)
            steps(pool, body)

        def split_act(act, a):
            for k in range(KB):
                nc.scalar.copy(xh[:, k, :], mT[:, k, :]).then_inc(n_hi, 1)

        def split_dve(dve, a):
            for k in range(KB):
                dve.wait_ge(n_hi, 8 * a + k + 1)
                nc.vector.tensor_tensor(xl[:, k, :], mT[:, k, :], xh[:, k, :].bitcast(F32), ALU.subtract).then_inc(n_lo, 1)
            dve.sem_inc(n_t, KB)

        def y_rows(t):
            return (P, y_p[0][t * P:(t + 1) * P, :]) if t < TT else (NS, y_s.rearrange("b q d -> (b q) d"))

        def out_pe(pe):
            for t in range(TT + 1):
                w = y_rows(t)[0]
                if t >= 2:
                    pe.wait_ge(y_a, t - 1)
                    pe.wait_ge(y_v, t - 1)
                for k in range(KB):
                    mm = nc.tensor.transpose(PS[0:w, 2 * (t % 2) + k // 4, (k % 4) * P:(k % 4) * P + P],
                                             hT[:, k, t * P:t * P + w], ident[:, :])
                mm.then_inc(y_pe, 1)

        def out_copy(eng, copy, b, done):
            for t in range(TT + 1):
                w = y_rows(t)[0]
                eng.wait_ge(y_pe, t + 1)
                if t >= 2:
                    eng.wait_ge(y_st[t % 2], 16 * (t // 2))
                copy(ytok[t % 2][0:w, 512 * b:512 * b + 512], PS[0:w, 2 * (t % 2) + b, :]).then_inc(done, 1)

        def out_sp(sp):
            for t in range(TT + 1):
                w, dst = y_rows(t)
                sp.wait_ge(y_a, t + 1)
                sp.wait_ge(y_v, t + 1)
                sp.dma_start(dst, ytok[t % 2][0:w, :]).then_inc(y_st[t % 2], 16)
            for j in range(2):
                sp.wait_ge(y_st[j], 16 * ((TT + 1 - j + 1) // 2))

        hsrc = [part(hT, 0, NH), part(hT, NH, NH)]

        (F_LOAD, F_NORM0, F_GLU, F_LN, F_OUT, F_POST0, F_FFN0) = range(1, 8)
        FFN_FENCES = 8
        F_KVN = F_FFN0 + FFN_FENCES
        F_KV, F_QN, S_NEW, S_SMP, S_ATT, F_ATT, F_SPLIT, F_O, F_POST1 = range(F_KVN + 1, F_KVN + 10)
        F_FFN1 = F_POST1 + 1

        def ffn(stage0, layer, q0, a0, p0, parts):
            for half in range(2):
                parts[0](half, q0 + 2 * half, a0 + half)
                yield stage0 + 4 * half
                parts[1](half)
                yield stage0 + 4 * half + 1
                parts[2](half)
                yield stage0 + 4 * half + 2
                parts[3](half, q0 + 2 * half + 1, p0 + half)
                yield stage0 + 4 * half + 3


        @block.sync
        def _(sp):
            load_sp(sp)
            glu_sp(sp)
            proj_sp(sp, "out", A["conv_w_out"][0])
            for half in range(2):
                up_sp(sp, 0, half)
                down_sp(sp, 0, half)
            proj_sp(sp, "k", A["w_k"])
            proj_sp(sp, "v", A["w_v"])
            proj_sp(sp, "q", A["w_q"][0])
            for q in range(2):
                load_tile(sp, first["o"] + q, q, cols(A["w_o"][0], q), KB)
            smp_sp(sp, S_NEW)
            att_sp(sp, S_ATT)
            with sp.Fori(1, KB // 2) as i:
                for q in range(2):
                    t, _ = tile_no("o", 2, i, q)
                    load_tile(sp, t, q, cols(A["w_o"][0], 2 * i + q), KB)
            for half in range(2):
                up_sp(sp, 1, half)
                down_sp(sp, 1, half)
            out_sp(sp)

        @block.tensor
        def _(pe):
            pe.sem_inc(w_used, 2)
            pe.sem_inc(g_tr, 2)
            pe.sem_inc(a_cum, 4)
            pe.sem_inc(a_pv, 3)
            pe.sem_inc(s_t, 5)
            pe.sem_inc(s_qk, 2)
            pe.sem_inc(s_c1, 2)
            pe.sem_inc(s_cum, 1)
            pe.sem_inc(s_pv, 8)
            load_pe(pe)
            fence(pe, F_LOAD)
            stats_pe(pe, 0, CH)
            fence(pe, F_NORM0)
            glu_pe(pe)
            fence(pe, F_GLU)
            ln_pe_mean(pe)
            stats_pe(pe, 1, CH)
            fence(pe, F_LN)
            proj_pe(pe, "out")
            fence(pe, F_OUT)
            stats_pe(pe, 2, CH)
            fence(pe, F_POST0)

            def run_ffn(layer, stage0, q0, a0, p0):
                def inp(half, q, a):
                    if half == 0:
                        ffn_rows_pe(pe, layer)
                    stats_pe(pe, q, HCH)

                def down(half):
                    if half == 1:
                        ffn_state_pe(pe, layer)
                    down_pe(pe, layer, half)
                for n in ffn(stage0, layer, q0, a0, p0, (inp, lambda half: up_pe(pe, layer, half), down,
                                                         lambda half, q, p: stats_pe(pe, q, HCH))):
                    fence(pe, n)
            run_ffn(0, F_FFN0, 3, 2, 1)
            stats_pe(pe, 7, CH)
            fence(pe, F_KVN)
            proj_pe(pe, "k", 0)
            proj_pe(pe, "v", 1)
            fence(pe, F_KV)
            fence(pe, F_QN)
            proj_pe(pe, "q")
            fence(pe, S_NEW)
            smp_new_pe(pe)
            fence(pe, S_SMP)
            smp_pe(pe)
            fence(pe, S_ATT)
            att_pe(pe)
            fence(pe, F_ATT)
            fence(pe, F_SPLIT)
            proj_pe(pe, "o")
            fence(pe, F_O)
            stats_pe(pe, 8, CH)
            fence(pe, F_POST1)
            run_ffn(1, F_FFN1, 9, 7, 4)
            out_pe(pe)

        @block.scalar
        def _(act):
            act.sem_inc(ps_free, 2)
            act.sem_inc(f_g, 1)
            act.sem_inc(f_gel, 1)
            act.sem_inc(g_tap, 16)
            act.sem_inc(a_w, 4)
            act.sem_inc(s_w, 2)
            load_act(act)
            for b in range(2):
                split_hi(act, b, 0, b)
            fence(act, F_LOAD)
            stats_act(act, 0, full(hT), T, CH)
            apply_act(act, 0, full(xh), T)
            fence(act, F_NORM0)
            glu_act(act)
            fence(act, F_GLU)
            act.wait_ge(l_xc, KB)
            stats_act(act, 1, full(mT), T, CH)
            ln_act(act, 1)
            fence(act, F_LN)
            proj_act(act, "out", lambda n, b: mT[:, ds(n, 1), :].opt(), bias=V_BOUT)
            fence(act, F_OUT)
            stats_act(act, 2, full(mT), T, CH)
            fence(act, F_POST0)

            def run_ffn(layer, stage0, q0, a0, p0):
                def inp(half, q, a):
                    stats_act(act, q, hsrc[half], NH, HCH)
                    apply_act(act, a, full(xhh), NH)
                for n in ffn(stage0, layer, q0, a0, p0, (
                        inp, lambda half: up_act(act, layer, half),
                        lambda half: down_act(act, layer, half, layer == 1 and half == 1),
                        lambda half, q, p: stats_act(act, q, full(mTh), NH, HCH))):
                    fence(act, n)
            run_ffn(0, F_FFN0, 3, 2, 1)
            stats_act(act, 7, full(hT), T, CH)
            apply_act(act, 4, full(xh), T)
            fence(act, F_KVN)
            proj_act(act, "k", lambda n, b: tmp[b], kv=0)
            proj_act(act, "v", lambda n, b: tmp[b], kv=1)
            fence(act, F_KV)
            apply_act(act, 5, full(xh), T)
            fence(act, F_QN)
            proj_act(act, "q", lambda n, b: tmp[b], scale=HD ** -0.5, kv=2)
            fence(act, S_NEW)
            nc.scalar.preload_act_table_set("natural_log_exp_and_others")
            smp_new_act(act)
            fence(act, S_SMP)
            smp_act(act)
            fence(act, S_ATT)
            att_act(act)
            fence(act, F_ATT)
            split_act(act, 6)
            fence(act, F_SPLIT)
            proj_act(act, "o", lambda n, b: mT[:, ds(n, 1), :].opt())
            fence(act, F_O)
            stats_act(act, 8, full(mT), T, CH)
            fence(act, F_POST1)
            run_ffn(1, F_FFN1, 9, 7, 4)
            out_copy(act, nc.scalar.copy, 0, y_a)

        @block.vector
        def _(dve):
            dve.sem_inc(w_lo, 2)
            for s_, n in ((g_u, 1), (g_smp, 1), (g_cv, 1), (g_tre, 1), (k_te, 2), (f_cv, 2), (f_p, 1), (a_o, 8),
                          (s_kl, 2), (s_zc, 2), (s_sp, 1), (s_sf, 1), (s_wl, 1), (s_o, 1), (s_oc, 1)):
                dve.sem_inc(s_, n)
            load_dve(dve)
            for b in range(2):
                split_lo(dve, b, b)
            fence(dve, F_LOAD)
            stats_dve(dve, 0, T)
            apply_dve(dve, 0, 0, full(hT), V_MIX_PRE, full(xh), full(xl), T)
            fence(dve, F_NORM0)
            glu_dve(dve)
            fence(dve, F_GLU)
            ln_dve_sum(dve)
            stats_dve(dve, 1, T)
            ln_dve_scale(dve, 1, 1)
            fence(dve, F_LN)
            proj_dve(dve, "out")
            fence(dve, F_OUT)
            stats_dve(dve, 2, T)
            post_dve(dve, 0, 2, full(mT), V_MIX_POST, 0, T)
            fence(dve, F_POST0)

            def run_ffn(layer, stage0, q0, a0, p0):
                def inp(half, q, a):
                    if half == 0:
                        ffn_rows_dve(dve, layer)
                    stats_dve(dve, q, NH)
                    apply_dve(dve, a, q, hsrc[half], V_FFN_PRE + layer, full(xhh), full(xlh), NH)

                def down(half):
                    if half == 1:
                        ffn_state_dve(dve, layer)
                    down_dve(dve, layer, half, layer == 1 and half == 1)

                def post(half, q, p):
                    stats_dve(dve, q, NH)
                    post_dve(dve, p, q, full(mTh), V_FFN_POST + layer, NH * half, NH)
                for n in ffn(stage0, layer, q0, a0, p0, (inp, lambda half: up_dve(dve, layer, half), down, post)):
                    fence(dve, n)
            run_ffn(0, F_FFN0, 3, 2, 1)
            stats_dve(dve, 7, T)
            apply_dve(dve, 4, 7, full(hT), V_KV, full(xh), full(xl), T)
            fence(dve, F_KVN)
            proj_dve(dve, "k", 0)
            proj_dve(dve, "v", 1)
            fence(dve, F_KV)
            apply_dve(dve, 5, 7, full(hT), V_MIX_PRE + 1, full(xh), full(xl), T)
            fence(dve, F_QN)
            proj_dve(dve, "q")
            fence(dve, S_NEW)
            smp_new_dve(dve)
            fence(dve, S_SMP)
            smp_dve(dve)
            fence(dve, S_ATT)
            att_dve(dve)
            fence(dve, F_ATT)
            split_dve(dve, 6)
            fence(dve, F_SPLIT)
            proj_dve(dve, "o")
            fence(dve, F_O)
            stats_dve(dve, 8, T)
            post_dve(dve, 3, 8, full(mT), V_MIX_POST + 1, 0, T)
            fence(dve, F_POST1)
            run_ffn(1, F_FFN1, 9, 7, 4)
            out_copy(dve, nc.vector.tensor_copy, 1, y_v)

        @block.gpsimd
        def _(pool):
            for s_, n in ((g_pool, 2), (g_of, 1), (k_free, 2), (k_tf, 2), (a_s, 4)):
                pool.sem_inc(s_, n)
            load_pool(pool)
            for n in (F_LOAD, F_NORM0):
                fence(pool, n)
            glu_pool(pool)
            for n in (F_GLU, F_LN, F_OUT, F_POST0):
                fence(pool, n)

            def run_ffn(layer, stage0, q0, a0, p0):
                def inp(half, q, a):
                    if half == 0:
                        ffn_rows_pool(pool, layer)

                def down(half):
                    if half == 1:
                        ffn_state_pool(pool, layer)
                for n in ffn(stage0, layer, q0, a0, p0, (inp, lambda half: None, down, lambda half, q, p: None)):
                    fence(pool, n)
            run_ffn(0, F_FFN0, 3, 2, 1)
            fence(pool, F_KVN)
            proj_pool(pool, 0, k_dram, 0, ok_p, ok_s)
            proj_pool(pool, 1, None, 1, ov_p, ov_s)
            fence(pool, F_KV)
            fence(pool, F_QN)
            proj_pool(pool, 2, q_dram)
            fence(pool, S_NEW)
            smp_in_pool(pool)
            smp_new_pool(pool)
            fence(pool, S_SMP)
            smp_pool(pool)
            fence(pool, S_ATT)
            att_pool(pool)
            for n in (F_ATT, F_SPLIT, F_O, F_POST1):
                fence(pool, n)
            run_ffn(1, F_FFN1, 9, 7, 4)


_INS = ["x_prompt", "x_sample", "state_conv_a", "state_ffn_conv", "cache_k", "cache_v", "page_table",
        "norm_mix_pre", "norm_mix_post", "norm_ffn_pre", "norm_ffn_post", "conv_w_glu", "conv_b_glu", "conv_w_dw",
        "conv_b_dw", "conv_ln_g", "conv_ln_b", "conv_w_out", "conv_b_out", "kv_norm", "w_k", "w_v", "w_q", "w_o",
        "sb_bias", "ffn_w_gate", "ffn_w_up", "ffn_w_dw", "ffn_w_down"]
_OUTS = [(1, NP, D), (DB, DQ, D), (1, 1, ST, D), (1, DB, ST, D), (2, 1, 2, FF), (2, DB, 2, FF),
         (NP, D), (NP, D), (NS, D), (NS, D)]
_RETURNED = _OUTS[:6] + [(1, NP, HEADS, HD)] * 2 + [(DB, DQ, HEADS, HD)] * 2


def build(nc, shapes):
    ins = {n: nc.dram_tensor(f"in_{n}", s, dt, kind="ExternalInput").ap() for n, (s, dt) in shapes.items()}
    outs = [nc.dram_tensor(f"out_{i}", s, F32, kind="ExternalOutput").ap() for i, s in enumerate(_OUTS)]
    yoco_step(nc, ins, outs)


def kernel(**inputs):
    import numpy as np
    import concourse.bacc as bacc
    from concourse.bass_utils import run_bass_kernel_spmd

    nc = bacc.Bacc("TRN2", target_bir_lowering=False, num_devices=1)
    arrays = {n: np.ascontiguousarray(inputs[n]) for n in _INS}
    build(nc, {n: (a.shape, mybir.dt.from_np(a.dtype)) for n, a in arrays.items()})
    r = run_bass_kernel_spmd(nc, [{f"in_{n}": a for n, a in arrays.items()}], core_ids=[0])
    return tuple(r.results[0][f"out_{i}"].reshape(s) for i, s in enumerate(_RETURNED))
```

```python
from contextlib import ExitStack

import concourse.bass as bass
from concourse import mybir

F32 = mybir.dt.float32
F32R = mybir.dt.float32r
I32 = mybir.dt.int32
ALU = mybir.AluOpType
ACT = mybir.ActivationFunctionType
ds = bass.ds

P = 128
D = 1024
KB = D // P
NP = 1024
DB, DQ = 8, 4
NS = DB * DQ
T = NP + NS
TT = NP // P
FF = 2816
FB = FF // P
CW = 31
ST = CW - 1
HEADS, HD = 16, 64
PAIRS = HEADS // 2
PAGE = 128
PAGES = 32
EPS = 1e-6
CLAMP = 40.0
NH = T // 2
HP1 = NP - NH
CH = [(0, 352), (352, 352), (704, 352)]
HCH = [(0, NH // 2), (NH // 2, NH // 2)]

(V_MIX_PRE, V_MIX_POST, V_FFN_PRE, V_FFN_POST, V_BGLU, V_BDW, V_LNG, V_LNB, V_BOUT, V_KV, V_DW) = (
    0, 2, 4, 6, 8, 10, 11, 12, 13, 14, 15)
NV = V_DW + CW

RING = 2
DVE_TAPS = 19
POOL_TAPS = CW - DVE_TAPS
KR, VR = 4, 8
UR = 6
CT = 8
CHUNKS = DB * PAGES // CT
CPB = PAGES // CT


def yoco_step(nc, ins, outs):
    A = ins
    y_p, y_s, oc_p, oc_s, of_p, of_s, ok_p, ov_p, ok_s, ov_s = outs
    k_dram = nc.dram_tensor("k_feature_major", (PAIRS, P, T), F32).ap()
    q_dram = nc.dram_tensor("q_feature_major", (PAIRS, P, T), F32).ap()

    base = (nc.sbuf_base + 63) // 64 * 64
    ROW = 4 * T
    H_AT, AR_AT = base, base + KB * ROW
    WT_AT = AR_AT + 30 * ROW
    TB_AT = WT_AT + 6 * 4096
    SM_AT = TB_AT + 4 * ROW
    small = [SM_AT]

    def at(name, shape, dt, offset):
        return nc.alloc_sbuf_tensor_at(name, shape, dt, offset=offset)

    def tiny(name, shape, dt=F32):
        n = 4
        for s in shape[1:]:
            n *= s
        t = at(name, shape, dt, small[0])
        small[0] += (n + 31) // 32 * 32
        return t

    hT = at("hT", [P, KB, T], F32, H_AT)
    xh = at("xh", [P, KB, T], F32R, AR_AT)
    xl = at("xl", [P, KB, T], F32R, AR_AT + 8 * ROW)
    mT = at("mT", [P, KB, T], F32, AR_AT + 16 * ROW)
    O2 = AR_AT + 24 * ROW
    xtok = at("xtok", [P, TT + 1, D], F32, AR_AT)
    vrow = at("vrow", [NV, D], F32, AR_AT + (TT + 1) * 4096)
    srow = at("srow", [120, 2, D], F32, AR_AT + (TT + 2) * 4096)
    UW = ST + NP + DB * (ST + DQ)
    UP = (UW + 7) // 8 * 8
    u = [at(f"u{j}", [P, UP], F32, O2 + j * 4 * UP) for j in range(2)]
    stA = at("stA", [P, KB, DB * ST], F32, O2 + 8 * UP)
    pacc = at("pacc", [P, T], F32, O2 + 8 * UP + 7680)
    ut = at("ut", [P, ST + DB * ST], F32, O2 + 8 * UP + 7680 + ROW + 1536)
    ustg = at("ustg", [120, 3, P], F32, O2 + 8 * UP + 7680 + ROW)
    xhh = at("xhh", [P, KB, NH], F32R, AR_AT)
    xlh = at("xlh", [P, KB, NH], F32R, AR_AT + 4 * ROW)
    ph = at("ph", [P, FB, NH], F32R, AR_AT + 8 * ROW)
    pl = at("pl", [P, FB, NH], F32R, AR_AT + 19 * ROW)
    mTh = at("mTh", [P, KB, NH], F32, AR_AT)
    frow = at("frow", [19, FF], F32, AR_AT + 24 * ROW)
    tok = [at(f"tok{j}", [P, TT + 1, P], F32, O2 + j * 4608) for j in range(2)]
    ytok = [at(f"ytok{j}", [P, D], F32, AR_AT + 8 * ROW + j * 4096) for j in range(2)]
    kp = [at(f"kp{j}", [P, NP], F32, AR_AT + j * 4096) for j in range(2)]
    qp = [at(f"qp{j}", [P, NP], F32, AR_AT + 8192 + j * 4096) for j in range(2)]
    vp = [at(f"vp{j}", [P, TT, P], F32, AR_AT + 16384 + j * 4096) for j in range(2)]
    eb = [at(f"eb{j}", [P, 512], F32, AR_AT + 24576 + j * 2048) for j in range(3)]
    spb = [at(f"spb{j}", [P, 512], F32, AR_AT + 30720 + j * 2048) for j in range(UR)]
    sb_ = [at(f"sb{j}", [P, 512], F32, AR_AT + 43008 + j * 2048) for j in range(UR)]
    wb = [at(f"wb{j}", [P, 512], F32, AR_AT + 55296 + j * 2048) for j in range(4)]
    kr = [at(f"kr{j}", [P, D], F32, AR_AT + j * 4096) for j in range(KR)]
    vr = [at(f"vr{j}", [P, D], F32, AR_AT + 16384 + j * 4096) for j in range(VR)]
    vl = [at(f"vl{j}", [P, D], F32R, AR_AT + 16384 + j * 4096) for j in range(VR)]
    vh = [at(f"vh{j}", [P, D], F32R, AR_AT + 49152 + j * 4096) for j in range(4)]
    kth = [at(f"kth{j}", [P, PAIRS, 2 * P], F32R, AR_AT + 65536 + j * 8192) for j in range(2)]
    ktl = [at(f"ktl{j}", [P, PAIRS, 2 * P], F32R, AR_AT + 81920 + j * 8192) for j in range(2)]
    wst = [at(f"wst{j}", [P, CT, P], F32R, AR_AT + 98304 + j * 4096) for j in range(2)]
    zsb = [at(f"zsb{j}", [P, 2 * P], F32, AR_AT + 106496 + j * 1024) for j in range(2)]
    om = at("om", [P, D], F32, AR_AT + 108544)
    qst = at("qst", [P, PAIRS, P], F32R, AR_AT + 112640)
    oc = at("oc", [P, DB, HD], F32, AR_AT + 116736)
    ssp = at("ssp", [P, 512], F32, AR_AT + 118784)
    ssf = at("ssf", [P, 512], F32, AR_AT + 120832)
    wns = at("wns", [NS, P], F32, AR_AT + 122880)
    both = at("both", [P, 64], F32, AR_AT + 123392)
    own_head = at("own_head", [P, HEADS], F32, AR_AT + 123648)
    carry = at("carry", [P, 64], F32, AR_AT + 123712)
    ceb = at("ceb", [P, 512], F32, TB_AT)
    swb = at("swb", [P, 512], F32, TB_AT + 13312)
    qbd = at("qbd", [P, PAIRS, DB, 8], F32, TB_AT)
    kTs = at("kTs", [P, PAIRS, NS], F32, TB_AT + 2048)
    vn = at("vn", [NS, D], F32, TB_AT + 3072)
    spn = at("spn", [P, DB, 64], F32, TB_AT + 7168)
    wn = at("wn", [NS, DB, 64], F32, TB_AT + 9216)
    brow = at("brow", [1, 512], F32, TB_AT + 11264)
    cn = at("cn", [NS, DB, 64], F32, TB_AT + 13312)
    qTs = at("qTs", [P, PAIRS, NS], F32, TB_AT + 15360)
    sq = [at(f"sq{k}", [P, T], F32, AR_AT + (8 + k) * ROW) for k in range(KB)]
    sqh = [at(f"sqh{k}", [P, NH], F32, AR_AT + 4 * ROW + k * 4 * NH) for k in range(2)]
    acch = at("acch", [P, NH], F32, TB_AT + 11264)
    raw = [at(f"raw{j}", [P, KB, P], F32, WT_AT + j * 4096) for j in range(RING)]
    whi = [at(f"whi{j}", [P, KB, P], F32R, WT_AT + 8192 + j * 4096) for j in range(RING)]
    wlo = [at(f"wlo{j}", [P, KB, P], F32R, WT_AT + 16384 + j * 4096) for j in range(RING)]
    tmp = [at(f"tmp{j}", [P, T], F32, TB_AT + j * ROW) for j in range(2)]
    acc = at("acc", [P, T], F32, TB_AT + 2 * ROW)
    rs = at("rs", [P, T], F32, TB_AT + 3 * ROW)
    GW = 2 + HP1 + DB * 6
    GP = (GW + 7) // 8 * 8
    gx = [at(f"gx{j}", [P, GP], F32, TB_AT + j * 4 * GP) for j in range(2)]
    CV = TB_AT + 8 * GP
    cv = [at(f"cv{j}", [P, NH], F32, CV + j * 4 * NH) for j in range(2)]
    gel = at("gel", [P, NH], F32, CV + 8 * NH)
    pf = [at(f"pf{j}", [P, NH], F32, CV + (12 + 4 * j) * NH) for j in range(2)]
    ident = tiny("ident", [P, P])
    mean1 = tiny("mean1", [P, P])
    ninc = tiny("ninc", [P, P])
    nall = tiny("nall", [P, P])
    one1 = tiny("one1", [1, P])
    eps = tiny("eps", [P, 1])
    vec = tiny("vec", [P, KB, NV])
    fT = tiny("fT", [P, FB, 19])
    fstg = tiny("fstg", [P, FB, 18])
    gtail = tiny("gtail", [P, FB, 2])
    sbias = tiny("sbias", [P, HEADS])
    ptab = tiny("ptab", [1, DB * PAGES], I32)
    assert small[0] <= nc.sbuf_usable_end, small[0] - nc.sbuf_usable_end

    with ExitStack() as ctx:
        PS = ctx.enter_context(nc.psum_tensor("PS", [P, 8, 512], F32))

        def sem(name):
            return ctx.enter_context(nc.semaphore(name))

        fence_s = sem("stage_ends")
        ld_x, ld_v, ld_f = sem("x_landed"), sem("vectors_landed"), sem("ffn_rows_landed")
        cst = sem("constants_made")
        passed = sem("waits_passed")
        w_raw = [sem(f"weights_landed{j}") for j in range(RING)]
        w_hi, w_lo, w_used = sem("weights_hi_made"), sem("weights_lo_made"), sem("weights_used")
        ps_free = sem("psum_set_free")
        n_sq, n_add, n_mean, n_rt, n_rs = (sem(f"norm_{x}") for x in ("squares", "sums", "mean", "root", "scale"))
        m_sq, m_add = sem("output_squares"), sem("output_square_sums")
        n_t, n_hi, n_lo = sem("scaled"), sem("scaled_hi"), sem("scaled_lo")
        p_t, p_h = sem("post_scaled"), sem("residual_added")
        tr_pe, tr_a, tr_v = sem("transposed"), sem("transposes_read_act"), sem("transposes_read_dve")
        g_sig, g_u, g_smp, g_tap, g_pool, g_cv, g_tr, g_tre, g_dve, g_out, g_of, g_ut = (sem(f"glu_{x}") for x in (
            "sigmoid", "u", "sample_conv", "tap_products", "tap_sums", "conv", "state_transposed", "state_read",
            "vector_step", "state_stored", "state_buffer_free", "state_gathered"))
        l_s, l_m, l_xc, l_t = sem("ln_sum"), sem("ln_mean"), sem("ln_centred"), sem("ln_scaled")
        f_g, f_cv, f_gel, f_p, f_hi, f_lo, f_v, f_st, f_ft = (sem(f"ffn_{x}") for x in (
            "gate_copied", "conv", "gelu", "product", "product_hi", "product_lo", "vector_step", "rows_transposed", "rows_read"))
        k_ev, k_tr, k_te, k_free, k_tf = (sem(f"proj_{x}") for x in (
            "copied", "transposed", "transposes_read", "buffer_free", "token_buffer_free"))
        k_st = [sem(f"proj_stored{j}") for j in range(2)]
        k_tst = [sem(f"proj_token_stored{j}") for j in range(2)]
        a_ld = [sem(f"att_loaded{j}") for j in range(2)]
        a_z, a_c, a_e, a_l, a_sp, a_sm, a_s, a_cum, a_w, a_wm, a_pv, a_o = (sem(f"att_{x}") for x in (
            "scores", "clamped", "exp", "log", "softplus", "masked", "suffix", "weights_ready", "weights", "weights_masked",
            "outputs", "outputs_copied"))
        s_in, s_q, s_n, s_nv, s_na, s_np, s_nm, s_tab = (sem(f"smp_{x}") for x in (
            "loaded", "queries", "new_tensor", "new_vector", "new_scalar", "new_gpsimd", "new_masked", "table_landed"))
        s_k = [sem(f"k_page_landed{j}") for j in range(KR)]
        s_v = [sem(f"v_page_landed{j}") for j in range(VR)]
        s_t, s_kh, s_kl, s_qk, s_zc, s_c1, s_m, s_e, s_l, s_sp, s_sf, s_cum, s_w, s_wh, s_wl = (sem(f"smp_{x}") for x in (
            "k_turned", "k_hi", "k_lo", "scored", "scores_copied", "scores_combined", "clamped", "exp", "log", "softplus",
            "page_sums", "weights_ready", "weights", "weights_hi", "weights_lo"))
        s_vh, s_vl0, s_vl1, s_pv, s_o, s_oc, s_qh, s_qst, s_wn = (sem(f"smp_{x}") for x in (
            "v_hi", "v_lo_even", "v_lo_odd", "v_summed", "outputs_read", "own_features", "queries_hi", "queries_placed",
            "new_weights_placed"))
        y_pe, y_a, y_v = sem("y_transposed"), sem("y_even_copied"), sem("y_odd_copied")
        y_st = [sem(f"y_stored{j}") for j in range(2)]
        fs_pe, fs_v, st_out = sem("ffn_state_transposed"), sem("ffn_state_read"), sem("ffn_tail_stored")

        block = ctx.enter_context(nc.Block())

        def fence(eng, n):
            eng.drain().then_inc(fence_s, 1)
            eng.wait_ge(fence_s, 4 * n)

        def alone(eng):
            eng.sem_inc(passed, 1)

        def ps(s, c, w):
            return PS[:, 3 * s + c, 0:w]

        first, sets, at_t, at_s = {}, {}, 0, 0
        for name, tiles, nsets in ([("glu", 16, 0), ("out", 8, 8)]
                                   + [x for h in (0, 1) for x in ((f"up0{h}", 44, 0), (f"down0{h}", 24, 8))]
                                   + [("k", 8, 8), ("v", 8, 8), ("q", 8, 8), ("o", 8, 8)]
                                   + [x for h in (0, 1) for x in ((f"up1{h}", 44, 0), (f"down1{h}", 24, 8))]):
            first[name], sets[name] = at_t, at_s
            at_t += tiles
            at_s += nsets
        TILES = at_t
        ffn_of = {"00": 0, "01": FB, "10": 2 * FB, "11": 3 * FB}
        DOWN_KB = [8, 8, FB - 16]

        def tile_no(name, per, i, q):
            return first[name] + q + per * i, (first[name] + q) // RING + (per // RING) * i

        def load_tile(sp, t, b, src, nb):
            sp.wait_ge(w_lo, t + 1)
            sp.dma_start(raw[b][:, 0:nb, :], src).then_inc(w_raw[b], 16)

        def cols(w, n, k0=0, nb=KB):
            return w[k0 * P:(k0 + nb) * P, ds(n * P, P)].rearrange("(k p) n -> p k n", p=P)

        def split_hi(act, t, turn, b):
            act.wait_ge(w_raw[b], 16 * (turn + 1))
            act.wait_ge(w_used, t + 1)
            nc.scalar.copy(whi[b][:], raw[b][:]).then_inc(w_hi, 1)

        def split_lo(dve, t, b):
            dve.wait_ge(w_hi, t + 1)
            nc.vector.tensor_tensor(wlo[b][:], raw[b][:], whi[b][:].bitcast(F32), ALU.subtract).then_inc(w_lo, 1)

        def product(pe, t, b, s, nb, k0, hi, lo, chunks, start, stop, split=None):
            pe.wait_ge(w_lo, t + 3)
            for k in range(nb):
                if split is not None:
                    pe.wait_ge(n_lo, KB * split + k + 1)
                for wt, x in ((whi, hi), (whi, lo), (wlo, hi)):
                    for c, (c0, w) in enumerate(chunks):
                        mm = nc.tensor.matmul(ps(s, c, w), wt[b][:, k, :], x[:, k0 + k, c0:c0 + w],
                                              start=start and k == 0 and wt is whi and x is hi,
                                              stop=stop and k == nb - 1 and wt is wlo)
            mm.then_inc(w_used, 1)

        vec_rows = [(V_MIX_PRE, A["norm_mix_pre"], 2), (V_MIX_POST, A["norm_mix_post"], 2),
                    (V_FFN_PRE, A["norm_ffn_pre"], 2), (V_FFN_POST, A["norm_ffn_post"], 2),
                    (V_BGLU, A["conv_b_glu"].rearrange("a (g d) -> (a g) d", g=2), 2),
                    (V_BDW, A["conv_b_dw"], 1), (V_LNG, A["conv_ln_g"], 1), (V_LNB, A["conv_ln_b"], 1),
                    (V_BOUT, A["conv_b_out"], 1), (V_KV, A["kv_norm"].rearrange("(a d) -> a d", a=1), 1),
                    (V_DW, A["conv_w_dw"][0], CW)]

        def load_sp(sp):
            sp.dma_start(xtok[:, 0:TT, :], A["x_prompt"][0].rearrange("(t p) d -> p t d", p=P)).then_inc(ld_x, 16)
            sp.dma_start(xtok[0:NS, TT, :], A["x_sample"].rearrange("b q d -> (b q) d")).then_inc(ld_x, 16)
            for r, src, n in vec_rows:
                sp.dma_start(vrow[r:r + n, :], src).then_inc(ld_v, 16)
            st = A["state_conv_a"][0].rearrange("b s d -> (b s) d")
            for j in range(2):
                sp.dma_start(srow[:, j, :], st[120 * j:120 * j + 120, :]).then_inc(ld_v, 16)
            sp.dma_start(sbias[:, :], A["sb_bias"].broadcast_to([P, HEADS])).then_inc(ld_v, 16)
            sp.dma_start(ptab[:, :], A["page_table"].rearrange("b n -> (b n)").rearrange("(a n) -> a n", a=1)).then_inc(s_tab, 16)

        LD_V = 16 * (len(vec_rows) + 3)

        def load_pool(pool):
            for t, v in ((ident, 0.0), (mean1, 1.0 / D), (ninc, -1.0), (nall, -1.0), (one1, 1.0), (eps, EPS)):
                nc.gpsimd.memset(t[:], v)
            for j in range(2):
                nc.gpsimd.memset(u[j][:, 0:ST], 0.0)
            pool.drain().then_inc(cst, 1)
            pool.wait_ge(cst, 1)
            nc.gpsimd.affine_select(out=ident[:], in_=ident[:], compare_op=ALU.not_equal, fill=1.0, base=0,
                                    pattern=[[-1, P]], channel_multiplier=1)
            nc.gpsimd.affine_select(out=ninc[:], in_=ninc[:], compare_op=ALU.is_ge, fill=0.0, base=0,
                                    pattern=[[-1, P]], channel_multiplier=1)
            pool.drain().then_inc(cst, 1)

        def load_pe(pe):
            pe.wait_ge(cst, 2)
            pe.wait_ge(ld_x, 32)
            for k in range(KB):
                if k >= 2:
                    pe.wait_ge(tr_a, k - 1)
                    pe.wait_ge(tr_v, k - 1)
                for t in range(TT + 1):
                    n = P if t < TT else NS
                    mm = nc.tensor.transpose(PS[:, 3 * (k % 2) + t // 4, (t % 4) * P:(t % 4) * P + n],
                                             xtok[0:n, t, k * P:(k + 1) * P], ident[0:n, 0:n])
                mm.then_inc(tr_pe, 1)
            pe.wait_ge(ld_v, LD_V)
            pe.wait_ge(tr_a, KB)
            pe.wait_ge(tr_v, KB)
            for k in range(KB):
                mm = nc.tensor.transpose(PS[:, 0, k * NV:(k + 1) * NV], vrow[:, k * P:(k + 1) * P], ident[0:NV, 0:NV])
            mm.then_inc(tr_pe, 1)
            for k in range(KB):
                for j in range(2):
                    mm = nc.tensor.transpose(PS[:, 2 + k // 2, (k % 2) * 240 + j * 120:(k % 2) * 240 + j * 120 + 120],
                                             srow[:, j, k * P:(k + 1) * P], ident[0:120, 0:120])
            mm.then_inc(tr_pe, 1)

        def load_act(act):
            for k in range(KB):
                act.wait_ge(tr_pe, k + 1)
                nc.scalar.copy(hT[:, k, 0:512], PS[:, 3 * (k % 2), :]).then_inc(tr_a, 1)

        def load_dve(dve):
            for k in range(KB):
                dve.wait_ge(tr_pe, k + 1)
                nc.vector.tensor_copy(hT[:, k, 512:1024], PS[:, 3 * (k % 2) + 1, :])
                nc.vector.tensor_copy(hT[:, k, 1024:T], PS[:, 3 * (k % 2) + 2, 0:NS]).then_inc(tr_v, 1)
            dve.wait_ge(tr_pe, KB + 1)
            nc.vector.tensor_copy(vec[:, :, :], PS[:, 0, 0:KB * NV].rearrange("p (k v) -> p k v", k=KB))
            dve.wait_ge(tr_pe, KB + 2)
            for k2 in range(KB // 2):
                nc.vector.tensor_copy(stA[:, 2 * k2:2 * k2 + 2, :],
                                      PS[:, 2 + k2, 0:480].rearrange("p (k v) -> p k v", k=2))

        def stats_act(act, q, src, n, chunks, made=None):
            for k in range(KB):
                if made is not None:
                    act.wait_ge(made[0], made[1] + k + 1)
                nc.scalar.activation(sq[k][:, 0:n], src(k), ACT.Square).then_inc(n_sq, 1)
            root_act(act, q, chunks)

        def root_act(act, q, chunks, bank=0, r0=0):
            nc.scalar.preload_act_table_set("sqrt_and_others")
            act.wait_ge(n_mean, q + 1)
            for c, (c0, w) in enumerate(chunks):
                ins_ = nc.scalar.activation(rs[:, r0 + c0:r0 + c0 + w], PS[:, bank + c, 0:w], ACT.Sqrt, bias=eps[:, 0:1])
            ins_.then_inc(n_rt, 1)

        def stats_dve(dve, q, n):
            for k in range(1, KB):
                dve.wait_ge(n_sq, 8 * q + k + 1)
                if k == 1:
                    nc.vector.tensor_tensor(acc[:, 0:n], sq[0][:, 0:n], sq[1][:, 0:n], ALU.add).then_inc(n_add, 1)
                else:
                    dve.wait_ge(n_add, 7 * q + k - 1)
                    nc.vector.tensor_tensor(acc[:, 0:n], acc[:, 0:n], sq[k][:, 0:n], ALU.add).then_inc(n_add, 1)
            scale_dve(dve, q, n)

        def scale_dve(dve, q, n, r0=0):
            dve.wait_ge(n_rt, q + 1)
            nc.vector.reciprocal(rs[:, r0:r0 + n], rs[:, r0:r0 + n]).then_inc(n_rs, 1)

        def early_act(act, q):
            for k in range(KB):
                if k >= 2:
                    act.wait_ge(n_add, 7 * q + max(1, k - 2))
                nc.scalar.activation(tmp[k % 2][:, 0:NH], hT[:, k, NH:T], ACT.Square).then_inc(n_sq, 1)

        def early_dve(dve, q):
            for k in range(1, KB):
                dve.wait_ge(n_sq, KB * q + k + 1)
                if k == 1:
                    nc.vector.tensor_tensor(acc[:, 0:NH], tmp[0][:, 0:NH], tmp[1][:, 0:NH], ALU.add).then_inc(n_add, 1)
                else:
                    dve.wait_ge(n_add, 7 * q + k - 1)
                    nc.vector.tensor_tensor(acc[:, 0:NH], acc[:, 0:NH], tmp[k % 2][:, 0:NH], ALU.add).then_inc(n_add, 1)

        def zero_dve(dve, r, total):
            dve.wait_ge(m_add, 9 * r + 2)
            nc.vector.memset(total, 0.0).then_inc(m_add, 1)

        def add_dve(dve, r, n, total, square):
            dve.wait_ge(m_sq, KB * r + n + 1)
            dve.wait_ge(m_add, 9 * r + n + 3)
            nc.vector.tensor_tensor(total, total, square, ALU.add).then_inc(m_add, 1)

        def summed_dve(dve, r):
            dve.wait_ge(m_add, 9 * r + 11)
            dve.sem_inc(n_add, KB - 1)

        def stats_pe(pe, q, chunks, acc=acc, bank=0):
            pe.wait_ge(n_add, 7 * q + 7)
            for c, (c0, w) in enumerate(chunks):
                mm = nc.tensor.matmul(PS[:, bank + c, 0:w], mean1[:], acc[:, c0:c0 + w], start=True, stop=True)
            mm.then_inc(n_mean, 1)

        def apply_act(act, a, hi, n):
            for k in range(KB):
                act.wait_ge(n_t, 8 * a + k + 1)
                nc.scalar.copy(hi(k), tmp[k % 2][:, 0:n]).then_inc(n_hi, 1)

        def apply_dve(dve, a, q, src, row, hi, lo, n, r0=0):
            dve.wait_ge(n_rs, q + 1)

            def low(k):
                dve.wait_ge(n_hi, 8 * a + k + 1)
                nc.vector.tensor_tensor(lo(k), tmp[k % 2][:, 0:n], hi(k).bitcast(F32), ALU.subtract).then_inc(n_lo, 1)

            for k in range(KB):
                if k >= 2:
                    dve.wait_ge(n_lo, 8 * a + k - 1)
                nc.vector.scalar_tensor_tensor(out=tmp[k % 2][:, 0:n], in0=src(k), scalar=vec[:, k, row:row + 1],
                                               in1=rs[:, r0:r0 + n], op0=ALU.mult, op1=ALU.mult).then_inc(n_t, 1)
                if k >= 1:
                    low(k - 1)
            low(KB - 1)

        def post_dve(dve, p, q, src, row, c0, n):
            dve.wait_ge(n_rs, q + 1)
            for k in range(KB + 1):
                if k < KB:
                    if k >= 2:
                        dve.wait_ge(p_h, 8 * p + k - 1)
                    nc.vector.scalar_tensor_tensor(out=tmp[k % 2][:, 0:n], in0=src(k), scalar=vec[:, k, row:row + 1],
                                                   in1=rs[:, 0:n], op0=ALU.mult, op1=ALU.mult).then_inc(p_t, 1)
                if k >= 1:
                    dve.wait_ge(p_t, 8 * p + k)
                    h = hT[:, k - 1, c0:c0 + n]
                    nc.vector.tensor_tensor(h, h, tmp[(k - 1) % 2][:, 0:n], ALU.add).then_inc(p_h, 1)
            dve.wait_ge(p_h, 8 * (p + 1))

        full = lambda t: (lambda k: t[:, k, :])
        part = lambda t, c0, n: (lambda k: t[:, k, c0:c0 + n])

        w_glu = A["conv_w_glu"][0]

        def glu_sp(sp):
            with sp.Fori(0, KB // 2) as i:
                for q in range(4):
                    t, _ = tile_no("glu", 4, i, q)
                    load_tile(sp, t, q % 2, cols(w_glu, 2 * i + q // 2 + KB * (q % 2)), KB)

        def glu_pe(pe):
            with pe.Fori(0, KB // 2) as i:
                for mm_ in range(2):
                    m = 2 * i + mm_
                    pe.wait_ge(g_u, m + 1)
                    for b in range(2):
                        t, _ = tile_no("glu", 4, i, 2 * mm_ + b)
                        product(pe, t, b, b, KB, 0, xh, xl, CH, True, True, 0)
                    pe.wait_ge(g_ut, m + 1)
                    pe.wait_ge(g_tre, m + 1)
                    nc.tensor.transpose(PS[0:ST, 6, 0:P], ut[:, 0:ST], ident[:, :])
                    for j in range(2):
                        mm = nc.tensor.transpose(PS[0:120, 6, (j + 1) * P:(j + 2) * P],
                                                 ut[:, ST + 120 * j:ST + 120 * j + 120], ident[:, :])
                    mm.then_inc(g_tr, 1)

        def table(name):
            nc.scalar.preload_act_table_set(name)

        def glu_act(act):
            table("sigmoid_and_others")
            with act.Fori(0, KB // 2) as i:
                for mm_ in range(2):
                    m = 2 * i + mm_
                    t, turn = tile_no("glu", 4, i, 2 * mm_ + 1)
                    act.wait_ge(w_used, t + 3)
                    act.wait_ge(g_smp, m + 1)
                    alone(act)
                    for c, (c0, w) in enumerate(CH):
                        ins_ = nc.scalar.activation(tmp[0][:, c0:c0 + w], ps(1, c, w), ACT.Sigmoid,
                                                    bias=vec[:, ds(m, 1), V_BGLU + 1].opt())
                    ins_.then_inc(g_sig, 1)
                    for b in range(2):
                        t, turn = tile_no("glu", 4, i, 2 * mm_ + b + 2)
                        split_hi(act, t, turn, b)
                    act.wait_ge(g_u, m + 2)
                    for j in range(POOL_TAPS):
                        tap = DVE_TAPS + j
                        if j == 0:
                            act.wait_ge(g_cv, m + 1)
                        else:
                            act.wait_ge(g_pool, (POOL_TAPS - 1) * m + max(1, j - 1))
                        alone(act)
                        nc.scalar.activation((pacc, acc, rs)[0 if j == 0 else 1 + j % 2][:, 0:NP], u[mm_][:, tap:tap + NP], ACT.Copy,
                                             scale=vec[:, ds(m, 1), V_DW + tap].opt()).then_inc(g_tap, 1)

        def glu_pool(pool):
            with pool.Fori(0, KB // 2) as i:
                for mm_ in range(2):
                    m = 2 * i + mm_
                    for j in range(1, POOL_TAPS):
                        pool.wait_ge(g_tap, POOL_TAPS * (m + 2) + j + 1)
                        pool.wait_ge(g_pool, (POOL_TAPS - 1) * m + j)
                        nc.gpsimd.tensor_tensor(pacc[:, 0:NP], pacc[:, 0:NP], (acc, rs)[j % 2][:, 0:NP],
                                                ALU.add).then_inc(g_pool, 1)
                    pool.wait_ge(g_tre, m + 2)
                    pool.dma_start(oc_p[0, 0][:, ds(m * P, P)], ustg[0:ST, 0, :]).then_inc(g_out, 16)
                    for j in range(2):
                        pool.dma_start(oc_s[0].rearrange("b s d -> (b s) d")[120 * j:120 * j + 120, ds(m * P, P)],
                                       ustg[:, j + 1, :]).then_inc(g_out, 16)
                    pool.wait_ge(g_out, 48 * m + 48)
                    pool.sem_inc(g_of, 1)

        GV = DVE_TAPS + 3

        def glu_dve(dve):
            with dve.Fori(0, KB // 2) as i:
                for mm_ in range(2):
                    m = 2 * i + mm_
                    step = [0]

                    def then(ins_):
                        step[0] += 1
                        ins_.then_inc(g_dve, 1)

                    def own(n=0):
                        dve.wait_ge(g_dve, GV * m + step[0] - n)

                    us = u[mm_]
                    usv = us[:, ST + NP:UW].rearrange("p (b w) -> p b w", b=DB)
                    dve.wait_ge(g_tap, POOL_TAPS * (m + 1))
                    nc.vector.tensor_copy(usv[:, :, 0:ST], stA[:, ds(m, 1), :].rearrange("p k (b s) -> p (k b) s", b=DB))
                    dve.wait_ge(g_sig, m + 1)
                    ba = vec[:, ds(m, 1), V_BGLU].opt()
                    for c, (c0, w) in enumerate(CH):
                        n = min(c0 + w, NP) - c0
                        nc.vector.scalar_tensor_tensor(out=us[:, ST + c0:ST + c0 + n], in0=ps(0, c, n), scalar=ba,
                                                       in1=tmp[0][:, c0:c0 + n], op0=ALU.add, op1=ALU.mult)
                    c0 = CH[2][0]
                    nc.vector.scalar_tensor_tensor(
                        out=usv[:, :, ST:ST + DQ], in0=PS[:, 2, NP - c0:T - c0].rearrange("p (b q) -> p b q", b=DB),
                        scalar=ba, in1=tmp[0][:, NP:T].rearrange("p (b q) -> p b q", b=DB),
                        op0=ALU.add, op1=ALU.mult).then_inc(g_u, 1)
                    for b in range(2):
                        t, _ = tile_no("glu", 4, i, 2 * mm_ + b + 2)
                        split_lo(dve, t, b)
                    dve.wait_ge(g_u, m + 2)
                    dve.wait_ge(g_tr, m + 2)
                    nc.vector.tensor_copy(ut[:, 0:ST], us[:, NP:NP + ST])
                    nc.vector.tensor_copy(ut[:, ST:ST + DB * ST].rearrange("p (b s) -> p b s", b=DB),
                                          usv[:, :, DQ:DQ + ST]).then_inc(g_ut, 1)
                    prod = tmp[0][:, 0:NS * CW].rearrange("p (b q w) -> p b q w", b=DB, q=DQ)
                    win = bass.AP(us, ST + NP, [(UP, P), (ST + DQ, DB), (1, DQ), (1, CW)])
                    wv = bass.AP(vec, m * NV + V_DW, [(KB * NV, P), (0, DB), (0, DQ), (1, CW)])
                    then(nc.vector.tensor_tensor(prod, win, wv, ALU.mult))
                    own()
                    smp = mT[:, ds(m, 1), NP:T].opt()
                    then(nc.vector.tensor_reduce(smp, tmp[0][:, 0:NS * CW].rearrange("p (s w) -> p s w", w=CW),
                                                 mybir.AxisListType.X, ALU.add))
                    own()
                    bdw = vec[:, ds(m, 1), V_BDW].opt()
                    nc.vector.tensor_scalar(smp, smp, bdw, None, ALU.add).then_inc(g_smp, 1)
                    sums = (mT[:, ds(m, 1), 0:NP].opt(), tmp[1][:, 0:NP])
                    for tap in range(DVE_TAPS):
                        win = us[:, tap:tap + NP]
                        wt = vec[:, ds(m, 1), V_DW + tap].opt()
                        d = sums[tap % 2]
                        if tap == 0:
                            then(nc.vector.tensor_scalar(d, win, wt, bdw, ALU.mult, ALU.add))
                        elif tap == 1:
                            dve.wait_ge(g_cv, m + 1)
                            then(nc.vector.tensor_scalar(d, win, wt, None, ALU.mult))
                        else:
                            own(1)
                            then(nc.vector.scalar_tensor_tensor(out=d, in0=win, scalar=wt, in1=d,
                                                                op0=ALU.mult, op1=ALU.add))
                    own()
                    then(nc.vector.tensor_tensor(sums[0], sums[0], sums[1], ALU.add))
                    dve.wait_ge(g_tr, m + 3)
                    dve.wait_ge(g_of, m + 1)
                    nc.vector.tensor_copy(ustg[0:ST, 0, :], PS[0:ST, 6, 0:P])
                    nc.vector.tensor_copy(ustg[:, 1:3, :],
                                          PS[0:120, 6, P:3 * P].rearrange("p (j n) -> p j n", j=2)).then_inc(g_tre, 1)
                    own()
                    dve.wait_ge(g_pool, (POOL_TAPS - 1) * (m + 1) + 1)
                    nc.vector.tensor_tensor(sums[0], sums[0], pacc[:, 0:NP], ALU.add).then_inc(g_cv, 1)
                    assert step[0] == GV

        def ln_dve_sum(dve):
            dve.wait_ge(g_cv, KB + 1)
            for k in range(1, KB):
                if k == 1:
                    nc.vector.tensor_tensor(acc[:], mT[:, 0, :], mT[:, 1, :], ALU.add).then_inc(l_s, 1)
                else:
                    dve.wait_ge(l_s, k - 1)
                    nc.vector.tensor_tensor(acc[:], acc[:], mT[:, k, :], ALU.add).then_inc(l_s, 1)
            dve.wait_ge(l_m, 1)
            for k in range(KB):
                block = mT[:, k, :].rearrange("p (c w) -> p c w", c=3)
                nc.vector.tensor_tensor(block, block, PS[:, 3:6, 0:T // 3], ALU.subtract).then_inc(l_xc, 1)

        def ln_pe_mean(pe):
            pe.wait_ge(l_s, KB - 1)
            for c, (c0, w) in enumerate(CH):
                mm = nc.tensor.matmul(ps(1, c, w), mean1[:], acc[:, c0:c0 + w], start=True, stop=True)
            mm.then_inc(l_m, 1)

        def ln_dve_scale(dve, q, a):
            dve.wait_ge(n_rs, q + 1)

            def low(k):
                dve.wait_ge(n_hi, 8 * a + k + 1)
                nc.vector.tensor_tensor(xl[:, k, :], tmp[k % 2][:], xh[:, k, :].bitcast(F32), ALU.subtract).then_inc(n_lo, 1)

            for k in range(KB):
                nc.vector.tensor_tensor(mT[:, k, :], mT[:, k, :], rs[:], ALU.mult).then_inc(l_t, 1)
                if k >= 1:
                    low(k - 1)
            low(KB - 1)

        def ln_act(act, a):
            for k in range(KB):
                act.wait_ge(l_t, k + 1)
                if k >= 2:
                    act.wait_ge(n_lo, 8 * a + k - 1)
                nc.scalar.activation(tmp[k % 2][:], mT[:, k, :], ACT.Silu, bias=vec[:, k, V_LNB:V_LNB + 1],
                                     scale=vec[:, k, V_LNG:V_LNG + 1]).then_inc(n_t, 1)
                act.wait_ge(n_t, 8 * a + k + 1)
                nc.scalar.copy(xh[:, k, :], tmp[k % 2][:]).then_inc(n_hi, 1)

        def proj_sp(sp, name, w):
            with sp.Fori(0, KB // 2) as i:
                for q in range(2):
                    t, _ = tile_no(name, 2, i, q)
                    load_tile(sp, t, q, cols(w, 2 * i + q), KB)

        def proj_pe(pe, name, split, turned=None):
            def turn(n, b):
                pe.wait_ge(k_ev, turned * KB + n + 1)
                for g, ts_ in enumerate(((0, 1, 2, 3), (4, 5, 6, 7), (8,))):
                    if g != 1:
                        pe.wait_ge(k_te, 3 * (turned * KB + n) + g // 2 + 2)
                    for t in ts_:
                        w = P if t < TT else NS
                        mm = nc.tensor.transpose(PS[0:w, 6 + g % 2, (t % 4) * P:(t % 4) * P + P],
                                                 tmp[b][:, t * P:t * P + w], ident[:, :])
                    mm.then_inc(k_tr, 1)

            def block(i, q):
                t, _ = tile_no(name, 2, i, q)
                pe.wait_ge(ps_free, sets[name] + 2 * i + q + 1)
                product(pe, t, q % 2, q % 2, KB, 0, xh, xl, CH, True, True, split)

            if turned is None:
                with pe.Fori(0, KB // 2) as i:
                    block(i, 0)
                    block(i, 1)
            else:
                block(0, 0)
                with pe.Fori(0, KB // 2 - 1) as i:
                    for b in range(2):
                        block(i, b + 1)
                        turn(2 * i + b, b)
                block(KB // 2 - 1, 1)
                turn(KB - 2, 0)
                turn(KB - 1, 1)

        def proj_act(act, name, dest, bias=None, scale=1.0, kv=None, post=None):
            with act.Fori(0, KB // 2) as i:
                for b in range(2):
                    n = 2 * i + b
                    t, turn = tile_no(name, 2, i, b)
                    act.wait_ge(w_used, t + 3)
                    if kv is not None:
                        act.wait_ge(k_free, kv * KB + n + 1)
                    alone(act)
                    d = dest(n, b)
                    for c, (c0, w) in enumerate(CH):
                        if bias is not None:
                            ins_ = nc.scalar.activation(d[:, c0:c0 + w], ps(b, c, w), ACT.Identity,
                                                        bias=vec[:, ds(n, 1), bias].opt())
                        else:
                            ins_ = nc.scalar.activation(d[:, c0:c0 + w], ps(b, c, w), ACT.Copy, scale=scale)
                    if post is not None:
                        act.wait_ge(m_add, 9 * post + n + 2)
                        alone(act)
                        for c, (c0, w) in enumerate(CH):
                            ins_ = nc.scalar.activation(tmp[b][:, c0:c0 + w], ps(b, c, w), ACT.Square,
                                                        bias=0.0 if bias is None else vec[:, ds(n, 1), bias].opt())
                        ins_.then_inc(m_sq, 1)
                        act.wait_ge(m_sq, KB * post + n + 1)
                        act.sem_inc(ps_free, 1)
                    else:
                        ins_.then_inc(ps_free if kv is None else k_ev, 1)
                    if kv is not None:
                        act.wait_ge(k_ev, kv * KB + n + 1)
                        act.sem_inc(ps_free, 1)
                    t, turn = tile_no(name, 2, i, b + 2)
                    split_hi(act, t, turn, b)

        def proj_dve(dve, name, turned=None, post=None):
            if post is not None:
                zero_dve(dve, post, acc[:])
            with dve.Fori(0, KB // 2) as i:
                for b in range(2):
                    t, _ = tile_no(name, 2, i, b + 2)
                    split_lo(dve, t, b)
                    if post is not None:
                        add_dve(dve, post, 2 * i + b, acc[:], tmp[b][:])
                    if turned is not None:
                        g0 = 3 * (turned * KB + 2 * i + b)
                        dve.wait_ge(k_tf, turned * KB + 2 * i + b + 1)
                        for g in range(3):
                            dve.wait_ge(k_tr, g0 + g + 1)
                            if g < 2:
                                src = PS[:, 6 + g, :].rearrange("p (t n) -> p t n", t=4)
                                nc.vector.tensor_copy(tok[b][:, 4 * g:4 * g + 4, :], src).then_inc(k_te, 1)
                            else:
                                nc.vector.tensor_copy(tok[b][0:NS, TT, :], PS[0:NS, 6, 0:P]).then_inc(k_te, 1)

        def proj_pool(pool, kv, dram, turned=None, out_p=None, out_s=None):
            with pool.Fori(0, KB // 2) as i:
                for b in range(2):
                    n = 2 * i + b
                    if dram is not None:
                        pool.wait_ge(k_ev, kv * KB + n + 1)
                        pool.dma_start(dram[ds(n, 1)].rearrange("a p t -> p (a t)"), tmp[b][:]).then_inc(k_st[b], 16)
                        done = 16 * (stored[kv] // 2 + i + 1)
                    if turned is not None:
                        pool.wait_ge(k_te, 3 * (turned * KB + n) + 3 + 2)
                        pool.dma_start(out_p[:, ds(n * P, P)].rearrange("(t p) f -> p t f", p=P),
                                       tok[b][:, 0:TT, :]).then_inc(k_tst[b], 16)
                        pool.dma_start(out_s[:, ds(n * P, P)], tok[b][0:NS, TT, :]).then_inc(k_tst[b], 16)
                    if dram is not None:
                        pool.wait_ge(k_st[b], done)
                    if turned is not None:
                        pool.wait_ge(k_tst[b], 32 * (turned * KB // 2 + i + 1))
                        pool.sem_inc(k_tf, 1)
                    pool.sem_inc(k_free, 1)
        stored = {0: 0, 1: 8, 2: 8}

        def ffn_rows_pool(pool, layer):
            pool.dma_start(frow[0:16, :], A["state_ffn_conv"][layer].rearrange("b s f -> (b s) f")).then_inc(ld_f, 16)
            pool.dma_start(frow[16:19, :], A["ffn_w_dw"][layer]).then_inc(ld_f, 16)

        def ffn_rows_pe(pe, layer):
            pe.wait_ge(ld_f, 32 * (layer + 1))
            for f in range(FB):
                mm = nc.tensor.transpose(PS[:, 6, f * 19:(f + 1) * 19], frow[:, f * P:(f + 1) * P], ident[0:19, 0:19])
            mm.then_inc(f_st, 1)

        def ffn_rows_dve(dve, layer):
            dve.wait_ge(f_st, layer + 1)
            nc.vector.tensor_copy(fT[:, :, :], PS[:, 6, 0:19 * FB].rearrange("p (f r) -> p f r", f=FB)).then_inc(f_ft, 1)
            dve.wait_ge(f_ft, layer + 1)

        def up_sp(sp, layer, half):
            with sp.Fori(0, FB // 2) as i:
                for q in range(4):
                    t, _ = tile_no(f"up{layer}{half}", 4, i, q)
                    w = A["ffn_w_gate"] if q % 2 == 0 else A["ffn_w_up"]
                    load_tile(sp, t, q % 2, cols(w[layer], 2 * i + q // 2), KB)

        def up_pe(pe, layer, half):
            f0 = ffn_of[f"{layer}{half}"]
            with pe.Fori(0, FB // 2) as i:
                for ff in range(2):
                    f = f0 + 2 * i + ff
                    for b in range(2):
                        t, _ = tile_no(f"up{layer}{half}", 4, i, 2 * ff + b)
                        pe.wait_ge((f_g, f_p)[b], f + 1)
                        product(pe, t, b, b, KB, 0, xhh, xlh, HCH, True, True,
                                    2 + half + 5 * layer)

        def up_act(act, layer, half):
            f0 = ffn_of[f"{layer}{half}"]
            name = f"up{layer}{half}"
            table("gelu_apprx_tanh_and_others")
            with act.Fori(0, FB // 2) as i:
                for ff in range(2):
                    f = f0 + 2 * i + ff
                    g = gx[ff]
                    t, _ = tile_no(name, 4, i, 2 * ff)
                    act.wait_ge(w_used, t + 3)
                    act.wait_ge(f_cv, f + 1)
                    nc.scalar.copy(g[:, 2:2 + 264], ps(0, 0, 264))
                    if half == 0:
                        ins_ = nc.scalar.copy(g[:, 2 + 264:2 + NH], ps(0, 1, 264))
                    else:
                        nc.scalar.copy(g[:, 2 + 264:2 + HP1], ps(0, 1, HP1 - 264))
                        ins_ = nc.scalar.copy(g[:, 2 + HP1:GW].rearrange("p (b w) -> p b w", b=DB)[:, :, 2:6],
                                              PS[:, 1, HP1 - 264:264].rearrange("p (b q) -> p b q", b=DB))
                    ins_.then_inc(f_g, 1)
                    t, turn = tile_no(name, 4, i, 2 * ff + 2)
                    split_hi(act, t, turn, 0)
                    act.wait_ge(f_cv, f + 3)
                    act.wait_ge(f_p, f + 1)
                    nc.scalar.activation(gel[:], cv[0][:], ACT.Gelu_apprx_tanh).then_inc(f_gel, 1)
                    t, turn = tile_no(name, 4, i, 2 * ff + 3)
                    split_hi(act, t, turn, 1)
                    act.wait_ge(f_p, f + 2)
                    nc.scalar.copy(ph[:, ds(2 * i + ff, 1), :].opt(), pf[ff][:]).then_inc(f_hi, 1)

        def up_dve(dve, layer, half):
            f0 = ffn_of[f"{layer}{half}"]
            name = f"up{layer}{half}"
            PER = (4, 10)[half]
            v0 = FB * (14 * layer + 4 * half)
            dve.wait_ge(n_lo, KB * (2 + half + 5 * layer + 1))
            if half == 0:
                for j in range(2):
                    nc.vector.memset(gx[j][:, 0:2], 0.0)
                dve.drain().then_inc(f_lo, 1)
                dve.wait_ge(f_lo, layer + 1)
            with dve.Fori(0, FB // 2) as i:
                for ff in range(2):
                    fl = 2 * i + ff
                    f = f0 + fl
                    step = [0]

                    def then(ins_):
                        step[0] += 1
                        ins_.then_inc(f_v, 1)

                    def own(n=0):
                        dve.wait_ge(f_v, v0 + PER * fl + step[0] - n)

                    g = gx[ff]
                    gs = g[:, 2 + HP1:GW].rearrange("p (b w) -> p b w", b=DB)
                    tap = lambda j: fT[:, ds(fl, 1), 16 + j].opt()
                    n = NH if half == 0 else HP1
                    if half == 1:
                        then(nc.vector.tensor_copy(g[:, 0:2], gtail[:, ds(fl, 1), :].opt()))
                        then(nc.vector.tensor_copy(gs[:, :, 0:2], fT[:, ds(fl, 1), 0:16].rearrange(
                            "p f (b s) -> p (f b) s", b=DB)))
                        own()
                    dve.wait_ge(f_g, f + 2)
                    dve.wait_ge(f_gel, f + 1)
                    parts = [(cv[0][:, 0:n], cv[1][:, 0:n], lambda j, g=g, n=n: g[:, j:j + n])]
                    if half == 1:
                        parts.append((cv[0][:, n:NH].rearrange("p (b q) -> p b q", b=DB),
                                      cv[1][:, n:NH].rearrange("p (b q) -> p b q", b=DB),
                                      lambda j, gs=gs: gs[:, :, j:j + DQ]))
                    for j in range(3):
                        for a_, b_, win in parts:
                            if j == 0:
                                then(nc.vector.tensor_scalar(a_, win(0), tap(0), None, ALU.mult))
                            else:
                                d, s_ = (b_, a_) if j == 1 else (a_, b_)
                                own(len(parts) - 1)
                                then(nc.vector.scalar_tensor_tensor(out=d, in0=win(j), scalar=tap(j), in1=s_,
                                                                    op0=ALU.mult, op1=ALU.add))
                    if half == 0:
                        then(nc.vector.tensor_copy(gtail[:, ds(fl, 1), :].opt(), g[:, NH:NH + 2]))
                    else:
                        then(nc.vector.tensor_copy(fstg[:, ds(fl, 1), 0:2].opt(), g[:, HP1:HP1 + 2]))
                        then(nc.vector.tensor_copy(fstg[:, ds(fl, 1), 2:18].rearrange("p f (b s) -> p (f b) s", b=DB),
                                                   gs[:, :, 4:6]))
                    own()
                    dve.sem_inc(f_cv, 1)
                    t, _ = tile_no(name, 4, i, 2 * ff + 2)
                    split_lo(dve, t, 0)
                    t, _ = tile_no(name, 4, i, 2 * ff + 1)
                    dve.wait_ge(w_used, t + 3)
                    dve.wait_ge(f_gel, f + 2)
                    for c, (c0, w) in enumerate(HCH):
                        ins_ = nc.vector.tensor_tensor(pf[ff][:, c0:c0 + w], gel[:, c0:c0 + w], ps(1, c, w), ALU.mult)
                    ins_.then_inc(f_p, 1)
                    t, _ = tile_no(name, 4, i, 2 * ff + 3)
                    split_lo(dve, t, 1)
                    dve.wait_ge(f_hi, f + 1)
                    nc.vector.tensor_tensor(pl[:, ds(fl, 1), :].opt(), pf[ff][:],
                                            ph[:, ds(fl, 1), :].opt().bitcast(F32), ALU.subtract)
                    assert step[0] == PER

        def down_sp(sp, layer, half):
            with sp.Fori(0, KB // 2) as i:
                for q in range(6):
                    t, _ = tile_no(f"down{layer}{half}", 6, i, q)
                    nb = DOWN_KB[q % 3]
                    load_tile(sp, t, q % 2, cols(A["ffn_w_down"][layer], 2 * i + q // 3, 8 * (q % 3), nb), nb)

        def down_pe(pe, layer, half):
            name = f"down{layer}{half}"
            with pe.Fori(0, KB // 2) as i:
                for q in range(6):
                    t, _ = tile_no(name, 6, i, q)
                    if q % 3 == 0:
                        pe.wait_ge(ps_free, sets[name] + 2 * i + q // 3 + 1)
                    product(pe, t, q % 2, q // 3, DOWN_KB[q % 3], 8 * (q % 3), ph, pl, HCH, q % 3 == 0, q % 3 == 2)

        def loop_with_tail(eng, last, body):
            if last:
                with eng.Fori(0, KB // 2 - 1) as i:
                    body(i, False)
                body(KB // 2 - 1, True)
            else:
                with eng.Fori(0, KB // 2) as i:
                    body(i, False)

        def down_act(act, layer, half, last):
            name = f"down{layer}{half}"
            r = 1 + half + 3 * layer

            def body(i, tail):
                for q in range(6):
                    if q % 3 == 2:
                        t, _ = tile_no(name, 6, i, q)
                        act.wait_ge(w_used, t + 3)
                        n = 2 * i + q // 3
                        for c, (c0, w) in enumerate(HCH):
                            nc.scalar.copy(mTh[:, ds(n, 1), c0:c0 + w].opt(), ps(q // 3, c, w))
                        act.wait_ge(m_add, 9 * r + n + 2)
                        for c, (c0, w) in enumerate(HCH):
                            ins_ = nc.scalar.activation(sqh[q // 3][:, c0:c0 + w], ps(q // 3, c, w), ACT.Square)
                        ins_.then_inc(m_sq, 1)
                        act.wait_ge(m_sq, KB * r + n + 1)
                        act.sem_inc(ps_free, 1)
                    t, turn = tile_no(name, 6, i, q + 2)
                    if not (tail and q >= 4):
                        split_hi(act, t, turn, q % 2)
            loop_with_tail(act, last, body)

        def down_dve(dve, layer, half, last):
            name = f"down{layer}{half}"
            r = 1 + half + 3 * layer
            zero_dve(dve, r, acch[:])

            def body(i, tail):
                for q in range(6):
                    t, _ = tile_no(name, 6, i, q + 2)
                    if not (tail and q >= 4):
                        split_lo(dve, t, q % 2)
                    if q % 3 == 2:
                        add_dve(dve, r, 2 * i + q // 3, acch[:], sqh[q // 3][:])
            loop_with_tail(dve, last, body)
            summed_dve(dve, r)

        FG = [(g, min(4, FB - g)) for g in range(0, FB, 4)]

        def ffn_state_pe(pe, layer):
            for j, (g, n) in enumerate(FG):
                if j >= 2:
                    pe.wait_ge(fs_v, 6 * layer + j - 1)
                for x in range(n):
                    mm = nc.tensor.transpose(PS[0:18, 6 + j % 2, x * P:(x + 1) * P], fstg[:, g + x, :], ident[:, :])
                mm.then_inc(fs_pe, 1)

        def ffn_state_dve(dve, layer):
            for j, (g, n) in enumerate(FG):
                dve.wait_ge(fs_pe, 6 * layer + j + 1)
                nc.vector.tensor_copy(rows18[:, g * P:(g + n) * P], PS[0:18, 6 + j % 2, 0:n * P]).then_inc(fs_v, 1)

        def ffn_state_pool(pool, layer):
            pool.wait_ge(fs_v, 6 * layer + 6)
            pool.dma_start(of_p[layer, 0], rows18[0:2, :]).then_inc(st_out, 16)
            pool.dma_start(of_s[layer].rearrange("b s f -> (b s) f"), rows18[2:18, :]).then_inc(st_out, 16)
            pool.wait_ge(st_out, 32 * (layer + 1))
        rows18 = at("rows18", [18, FF], F32, TB_AT)

        UNITS = [(hh, c, j) for hh in range(2) for c in range(2) for j in range(4 * c + 3, -1, -1)]
        NU = len(UNITS)
        UN = [(pp, hh, c, j) for pp in range(2) for hh, c, j in UNITS]
        LOOPS = PAIRS // 2
        L1, L2 = 4, 6

        def span(c, j):
            t0 = max(512 * c, P * j)
            return t0 - 512 * c, 512 * (c + 1) - t0, P * j >= 512 * c

        def bank(x):
            return x % UR + (2 if x % UR >= 4 else 0)

        NMASK = sum(span(c, j)[2] for _, _, c, j in UN)
        mask_no = []
        for x in UN:
            mask_no.append(sum(span(y[2], y[3])[2] for y in UN[:len(mask_no) + 1]))

        def att_sp(sp, stage):
            sp.wait_ge(fence_s, 4 * stage)
            with sp.Fori(0, LOOPS) as i:
                for pp in range(2):
                    n = 2 * i + pp
                    sp.wait_ge(a_o, 4 * n + 4)
                    sp.dma_start(kp[pp][:], k_dram[ds(n, 1), :, 0:NP].rearrange("a p t -> p (a t)")).then_inc(a_ld[pp], 16)
                    sp.dma_start(qp[pp][:], q_dram[ds(n, 1), :, 0:NP].rearrange("a p t -> p (a t)")).then_inc(a_ld[pp], 16)
                    sp.dma_start(vp[pp][:], ov_p[:, ds(n * P, P)].rearrange("(t p) f -> p t f", p=P)).then_inc(a_ld[pp], 16)

        NL = len(UN)
        LM = L2 + 1

        def units(eng, body):
            for s in range(LM):
                body(0, lambda lag, s=s: s - lag if s >= lag else None)
            with eng.Fori(0, LOOPS - 1) as i:
                for s in range(NL):
                    body(i, lambda lag, s=s: LM + s - lag)
            for s in range(NL):
                body(LOOPS - 1, lambda lag, s=s: LM + s - lag if LM + s - lag < NL else None)

        def turn(i, x):
            return i + x // NL if x >= NL else i

        def att_pe(pe):
            def body(i, at):
                u0, x = NL * i, at(0)
                if x is not None:
                    pp, hh, c, j = UN[x % NL]
                    o, w, _ = span(c, j)
                    if (hh, c, j) == UNITS[0]:
                        pe.wait_ge(a_ld[pp], 48 * turn(i, x) + 48)
                    pe.wait_ge(a_w, u0 + x + 1)
                    r = slice(HD * hh, HD * hh + HD)
                    nc.tensor.matmul(PS[:, bank(x), o:o + w], kp[pp][r, j * P:(j + 1) * P],
                                     qp[pp][r, 512 * c + o:512 * c + o + w], start=True, stop=False,
                                     skip_group_check=True).then_inc(a_z, 1)
                y = at(L1)
                if y is not None:
                    pp, hh, c, j = UN[y % NL]
                    o, w, diag = span(c, j)
                    top = j == 4 * c + 3
                    pe.wait_ge(a_sp, u0 + y + 4)
                    if diag:
                        pe.wait_ge(a_sm, NMASK * turn(i, y) + mask_no[y % NL])
                    mm = nc.tensor.matmul(PS[:, bank(y), o:o + w], ninc[:], spb[y % UR][:, o:o + w], start=False,
                                          stop=top, skip_group_check=True)
                    if not top:
                        pe.wait_ge(a_s, u0 + y + UR)
                        mm = nc.tensor.matmul(PS[:, bank(y), o:o + w], nall[:], sb_[y % UR][:, o:o + w], start=False,
                                              stop=True, skip_group_check=True)
                    mm.then_inc(a_cum, 1)
                y = at(L2)
                if y is not None:
                    pp, hh, c, j = UN[y % NL]
                    o, w, diag = span(c, j)
                    top = j == 4 * c + 3
                    if top:
                        pe.wait_ge(a_o, 4 * (2 * turn(i, y) + pp) + 2 * hh + c + 5)
                    pe.wait_ge(a_w, u0 + y + 1 + UR)
                    if diag:
                        pe.wait_ge(a_wm, NMASK * turn(i, y) + mask_no[y % NL])
                    nc.tensor.matmul(PS[HD * hh:HD * hh + HD, 4 + c, o:o + w], vp[pp][:, j, HD * hh:HD * hh + HD],
                                     wb[y % 4][:, o:o + w], start=top, stop=j == 0,
                                     skip_group_check=True).then_inc(a_pv, 1)
            units(pe, body)

        def att_act(act):
            def body(i, at):
                u0, x = NL * i, at(0)
                if x is not None:
                    pp, hh, c, j = UN[x % NL]
                    o, w, _ = span(c, j)
                    e = eb[x % 3][:, o:o + w]
                    act.wait_ge(a_c, u0 + x + 1)
                    nc.scalar.activation(e, e, ACT.Exp).then_inc(a_e, 1)
                    act.wait_ge(a_e, u0 + x + 1)
                    nc.scalar.activation(e, e, ACT.Ln, bias=1.0).then_inc(a_l, 1)
                y = at(L1)
                if y is not None:
                    pp, hh, c, j = UN[y % NL]
                    o, w, _ = span(c, j)
                    act.wait_ge(a_cum, u0 + y + 1 + UR)
                    act.wait_ge(a_pv, u0 + y + 1)
                    alone(act)
                    nc.scalar.activation(wb[y % 4][:, o:o + w], PS[:, bank(y), o:o + w], ACT.Exp,
                                         bias=sbias[:, ds(4 * turn(i, y) + 2 * pp + hh, 1)]).then_inc(a_w, 1)
            units(act, body)

        def att_dve(dve):
            def body(i, at):
                u0, x = NL * i, at(0)
                if x is not None:
                    pp, hh, c, j = UN[x % NL]
                    o, w, _ = span(c, j)
                    bias = sbias[:, ds(4 * turn(i, x) + 2 * pp + hh, 1)]
                    dve.wait_ge(a_z, u0 + x + 1)
                    dve.wait_ge(a_sp, u0 + x + 1)
                    nc.vector.tensor_scalar(eb[x % 3][:, o:o + w], PS[:, bank(x), o:o + w], bias, CLAMP,
                                            ALU.add, ALU.min).then_inc(a_c, 1)
                y = at(1)
                if y is not None:
                    pp, hh, c, j = UN[y % NL]
                    o, w, _ = span(c, j)
                    bias = sbias[:, ds(4 * turn(i, y) + 2 * pp + hh, 1)]
                    dve.wait_ge(a_l, u0 + y + 1)
                    dve.wait_ge(a_s, u0 + y + 1)
                    dve.wait_ge(a_cum, u0 + y + 1)
                    nc.vector.scalar_tensor_tensor(out=spb[y % UR][:, o:o + w], in0=PS[:, bank(y), o:o + w], scalar=bias,
                                                   in1=eb[y % 3][:, o:o + w], op0=ALU.add,
                                                   op1=ALU.max).then_inc(a_sp, 1)
                y = at(L2 + 1)
                if y is not None and UN[y % NL][3] == 0:
                    pp, hh, c, j = UN[y % NL]
                    dve.wait_ge(a_pv, u0 + y + 5)
                    r = slice(HD * hh, HD * hh + HD)
                    nc.vector.tensor_copy(mT[r, ds(2 * turn(i, y) + pp, 1), 512 * c:512 * c + 512].opt(),
                                          PS[r, 4 + c, :]).then_inc(a_o, 1)
            units(dve, body)

        def att_pool(pool):
            def mask(t, semaphore):
                alone(pool)
                nc.gpsimd.affine_select(out=t, in_=t, compare_op=ALU.is_ge, fill=0.0, base=-1,
                                        pattern=[[1, P]], channel_multiplier=-1).then_inc(semaphore, 1)

            def body(i, at):
                u0, x = NL * i, at(0)
                y = at(L1 + 1)
                if y is not None and span(UN[y % NL][2], UN[y % NL][3])[2]:
                    o = span(UN[y % NL][2], UN[y % NL][3])[0]
                    pool.wait_ge(a_w, u0 + y + 1 + UR)
                    mask(wb[y % 4][:, o:o + P], a_wm)
                if x is not None:
                    pp, hh, c, j = UN[x % NL]
                    o, w, diag = span(c, j)
                    pool.wait_ge(a_sp, u0 + x + 4)
                    if diag:
                        mask(spb[x % UR][:, o:o + P], a_sm)
                        pool.wait_ge(a_sm, NMASK * turn(i, x) + mask_no[x % NL])
                    pool.wait_ge(a_s, u0 + x + UR)
                    if j > 0:
                        d = sb_[(x + 1) % UR]
                        pool.wait_ge(a_cum, u0 + x + 2)
                        no = span(c, j - 1)[0]
                        alone(pool)
                        if no < o:
                            nc.gpsimd.memset(d[:, no:o], 0.0)
                        if j == 4 * c + 3:
                            ins_ = nc.gpsimd.tensor_copy(d[:, o:o + w], spb[x % UR][:, o:o + w])
                        else:
                            ins_ = nc.gpsimd.tensor_tensor(d[:, o:o + w], sb_[x % UR][:, o:o + w],
                                                           spb[x % UR][:, o:o + w], ALU.add)
                        ins_.then_inc(a_s, 1)
                    else:
                        pool.sem_inc(a_s, 1)
            units(pool, body)

        SEQ_PAIRS = PAGES // 2
        CHUNK_PAIRS = CT // 2
        LAG = 10

        def steps(eng, body):
            for s in range(LAG):
                body(0, lambda lag, s=s: s - lag if s >= lag else None)
            with eng.Fori(0, DB - 1) as b:
                for s in range(SEQ_PAIRS):
                    body(b, lambda lag, s=s: LAG + s - lag)
            for s in range(SEQ_PAIRS):
                body(DB - 1, lambda lag, s=s: LAG + s - lag if LAG + s - lag < SEQ_PAIRS else None)

        def chunk_of(b, o):
            return CPB * b + o // CHUNK_PAIRS, (o // CHUNK_PAIRS) % 2

        def is_first(o):
            return o is not None and o % CHUNK_PAIRS == 0

        def is_start(o):
            return o is not None and o % SEQ_PAIRS == 0

        def seq(b, o):
            return b + o // SEQ_PAIRS if o >= SEQ_PAIRS else b

        def smp_in_pool(pool):
            pool.dma_start(kTs[:], k_dram[:, :, NP:T].rearrange("a p t -> p a t")).then_inc(s_in, 16)
            pool.dma_start(qTs[:], q_dram[:, :, NP:T].rearrange("a p t -> p a t")).then_inc(s_in, 16)
            pool.dma_start(vn[:], ov_s).then_inc(s_in, 16)

        def smp_new_dve(dve):
            nc.vector.memset(qbd[:], 0.0)
            nc.vector.memset(spn[:], 0.0)
            nc.vector.memset(qst[:].bitcast(F32), 0.0)
            nc.vector.memset(wns[:], 0.0)
            dve.drain().then_inc(s_nv, 1)
            dve.wait_ge(s_nv, 1)
            dve.wait_ge(s_in, 48)
            for hh in range(2):
                r = slice(HD * hh, HD * hh + HD)
                for a in range(PAIRS):
                    nc.vector.tensor_copy(qbd[r, a, :, 4 * hh:4 * hh + 4], qTs[r, a, :].rearrange("p (b q) -> p b q", b=DB))
            nc.vector.tensor_copy(brow[0:1, :].rearrange("p (t h q) -> p t h q", t=CT, h=HEADS),
                                  bass.AP(sbias, 0, [(HEADS, 1), (0, CT), (1, HEADS), (0, DQ)]))
            dve.drain().then_inc(s_q, 1)
            dve.wait_ge(s_n, 1)
            zn = PS[0:NS, 7, :].rearrange("p (b c) -> p b c", b=DB)
            nc.vector.tensor_scalar(cn[:], zn, CLAMP, None, ALU.min).then_inc(s_nv, 1)
            dve.wait_ge(s_na, 2)
            nc.vector.tensor_tensor(spn[0:NS], zn, cn[:], ALU.max).then_inc(s_nv, 1)

        def smp_new_act(act):
            act.wait_ge(s_nv, 2)
            nc.scalar.activation(cn[:], cn[:], ACT.Exp).then_inc(s_na, 1)
            act.wait_ge(s_na, 1)
            nc.scalar.activation(cn[:], cn[:], ACT.Ln, bias=1.0).then_inc(s_na, 1)
            act.wait_ge(s_n, 2)
            nc.scalar.activation(wn[:], PS[0:NS, 7, :].rearrange("p (b c) -> p b c", b=DB), ACT.Exp).then_inc(s_na, 1)

        def smp_new_pool(pool):
            count = [0]

            def done():
                pool.drain().then_inc(s_np, 1)
                count[0] += 1
                pool.wait_ge(s_np, count[0])

            nc.gpsimd.memset(both[:], 0.0)
            nc.gpsimd.memset(own_head[:], 0.0)
            done()
            for g in range(2):
                nc.gpsimd.affine_select(out=both[:], in_=both[:], compare_op=ALU.not_equal, fill=1.0, base=-64 * g,
                                        pattern=[[-1, 64]], channel_multiplier=1)
                for q in range(DQ):
                    nc.gpsimd.affine_select(out=own_head[:], in_=own_head[:], compare_op=ALU.not_equal, fill=1.0,
                                            base=-64 * g - q, pattern=[[-DQ, HEADS]], channel_multiplier=1)
                    done()

            def mask(t):
                v = t.rearrange("p b (h q) -> p b h q", h=HEADS)
                nc.gpsimd.affine_select(out=v, in_=v, compare_op=ALU.is_ge, fill=0.0, base=0,
                                        pattern=[[-DQ, DB], [0, HEADS], [0, DQ]], channel_multiplier=1)
                done()
                nc.gpsimd.affine_select(out=v, in_=v, compare_op=ALU.is_ge, fill=0.0, base=-1,
                                        pattern=[[DQ, DB], [0, HEADS], [1, DQ]], channel_multiplier=-1)
                done()
            pool.wait_ge(s_nv, 3)
            mask(spn[0:NS])
            pool.sem_inc(s_nm, 1)
            pool.wait_ge(s_na, 3)
            mask(wn[:])

        def smp_new_pe(pe):
            pe.wait_ge(s_q, 1)
            nc.tensor.matmul(PS[0:NS, 7, :], one1[0:1, 0:NS], brow[:], start=True, stop=False, skip_group_check=True)
            zn = PS[0:NS, 7, :].rearrange("p (b c) -> p b c", b=DB)
            for a in range(PAIRS):
                mm = nc.tensor.matmul(zn[:, :, 8 * a:8 * a + 8], kTs[:, a, :], qbd[:, a, :, :], start=False,
                                      stop=False, skip_group_check=True)
            mm.then_inc(s_n, 1)
            pe.wait_ge(s_nm, 1)
            nc.tensor.matmul(PS[0:NS, 7, :], ninc[0:NS, 0:NS], spn[0:NS].rearrange("p b c -> p (b c)"), start=False,
                             stop=True, skip_group_check=True).then_inc(s_n, 1)

        def smp_sp(sp, stage):
            sp.wait_ge(fence_s, 4 * stage)
            sp.wait_ge(s_tab, 16)

            def load(b, o, cache, ring, landed, freed, count):
                first_entry = PAGES * seq(b, o) + PAGES - 1 - 2 * (o % SEQ_PAIRS)
                numbers = [sp.value_load(ptab[0:1, ds(first_entry - e, 1)], min_val=0, max_val=cache.shape[0] - 1)
                           for e in range(2)]
                sp.wait_ge(freed, count)
                for e, number in enumerate(numbers):
                    slot = (2 * o + e) % len(ring)
                    sp.dma_start(ring[slot][:], cache[ds(number, 1)].rearrange("a s h d -> (a s) (h d)")).then_inc(
                        landed[slot], 16)

            def body(b, at):
                k, v = at(0), at(7)
                if k is not None:
                    load(b, k, A["cache_k"], kr, s_k, s_t, 4 * (SEQ_PAIRS * b + k) + 1)
                if v is not None:
                    load(b, v, A["cache_v"], vr, s_v, s_pv, SEQ_PAIRS * b + v + 5)
            steps(sp, body)

        def smp_pe(pe):
            def turn(b, o, hf):
                e, h, unit = hf // 2, hf % 2, 4 * (SEQ_PAIRS * b + o) + hf
                slot = (2 * o + e) % KR
                if h == 0:
                    pe.wait_ge(s_k[slot], 16 * (PAGES // KR * b + (2 * o + e) // KR + 1))
                pe.wait_ge(s_kl, unit + 1)
                for j in range(4):
                    a = 4 * h + j
                    mm = nc.tensor.transpose(PS[:, 4 + hf % 2, j * P:(j + 1) * P], kr[slot][:, a * P:(a + 1) * P], ident[:])
                mm.then_inc(s_t, 1)

            def scores(b, o, h):
                pair = SEQ_PAIRS * b + o
                if h == 0:
                    pe.wait_ge(s_kl, 4 * pair + 6)
                    pe.wait_ge(s_zc, pair + 1)
                    if is_start(o):
                        pe.wait_ge(s_qst, seq(b, o) + 1)
                for a in range(4 * h, 4 * h + 4):
                    for part_ in (kth, ktl):
                        mm = nc.tensor.matmul(PS[:, 6 + o % 2, 0:2 * P], qst[:, a, :], part_[o % 2][:, a, :],
                                              start=a == 0 and part_ is kth, stop=a == PAIRS - 1 and part_ is ktl)
                if h == 1:
                    mm.then_inc(s_qk, 1)

            def combine(b, o):
                g, z = chunk_of(b, o)
                if is_first(o):
                    pe.wait_ge(s_w, g + 1)
                    nc.tensor.matmul(PS[:, z, :], one1[:], brow[:], start=True, stop=False, skip_group_check=True)
                pe.wait_ge(s_zc, SEQ_PAIRS * b + o + 3)
                for e in range(2):
                    c = 64 * (2 * (o % CHUNK_PAIRS) + e)
                    mm = nc.tensor.matmul(PS[:, z, c:c + 64], zsb[o % 2][:, e * P:(e + 1) * P], both[:], start=False,
                                          stop=False, skip_group_check=True)
                mm.then_inc(s_c1, 1)

            def sums(b, o):
                g, z = chunk_of(b, o)
                pe.wait_ge(s_sp, g + 2)
                nc.tensor.matmul(PS[:, z, :], ninc[:], ssp[:], start=False, stop=False, skip_group_check=True)
                pe.wait_ge(s_sf, (CT + 1) * g + CT + 1)
                nc.tensor.matmul(PS[:, z, :], nall[:], ssf[:], start=False, stop=True,
                                 skip_group_check=True).then_inc(s_cum, 1)

            def outputs(b, o, e):
                pair, (g, par) = SEQ_PAIRS * b + o, chunk_of(b, o)
                if e == 0:
                    if is_start(o):
                        pe.wait_ge(s_wn, seq(b, o) + 1)
                        pe.wait_ge(s_o, seq(b, o) + 1)
                        for h in range(2):
                            nc.tensor.matmul(PS[:, 2 + h, :], wns[:], vn[:, 512 * h:512 * h + 512], start=True, stop=False,
                                             skip_group_check=True)
                    if is_first(o):
                        pe.wait_ge(s_wl, g + 2)
                    pe.wait_ge(s_vl0, pair + 1)
                else:
                    pe.wait_ge(s_vl1, pair + 1)
                x, slot = (2 * o + e) % CT, (2 * o + e) % VR
                for v in (vh[(2 * o + e) % 4], vl[slot]):
                    for h in range(2):
                        mm = nc.tensor.matmul(PS[:, 2 + h, :], wst[par][:, x, :], v[:, 512 * h:512 * h + 512], start=False,
                                              stop=o % SEQ_PAIRS == SEQ_PAIRS - 1 and e == 1 and v is vl[slot],
                                              skip_group_check=True)
                if e == 1:
                    mm.then_inc(s_pv, 1)

            def body(b, at):
                k, s, c, u, o = at(0), at(1), at(2), at(7), at(9)
                if k is not None:
                    turn(b, k, 0)
                    turn(b, k, 1)
                if s is not None:
                    scores(b, s, 0)
                if k is not None:
                    turn(b, k, 2)
                if s is not None:
                    scores(b, s, 1)
                if k is not None:
                    turn(b, k, 3)
                if o is not None:
                    outputs(b, o, 0)
                if c is not None:
                    combine(b, c)
                if is_first(u):
                    sums(b, u)
                if o is not None:
                    outputs(b, o, 1)
            steps(pe, body)
            for b in range(DB):
                pe.wait_ge(s_oc, b + 2)
                for hh in range(2):
                    mm = nc.tensor.matmul(PS[HD * hh:HD * hh + HD, 4 + hh, 64 * b:64 * b + 64], oc[:, b, :], both[:],
                                          start=True, stop=True)
            mm.then_inc(s_n, 1)

        def smp_act(act):
            def k_hi(b, o, hf):
                e, h, unit = hf // 2, hf % 2, 4 * (SEQ_PAIRS * b + o) + hf
                act.wait_ge(s_t, unit + 6)
                if hf == 0:
                    act.wait_ge(s_qk, SEQ_PAIRS * b + o + 1)
                nc.scalar.copy(kth[o % 2][:, 4 * h:4 * h + 4, e * P:(e + 1) * P],
                               PS[:, 4 + hf % 2, :].rearrange("p (a s) -> p a s", a=4)).then_inc(s_kh, 1)

            def v_hi(b, o, e):
                slot = (2 * o + e) % VR
                act.wait_ge(s_v[slot], 16 * (PAGES // VR * b + (2 * o + e) // VR + 1))
                if e == 0:
                    act.wait_ge(s_pv, SEQ_PAIRS * b + o + 7)
                nc.scalar.copy(vh[(2 * o + e) % 4][:], vr[slot][:]).then_inc(s_vh, 1)

            def soft(b, o):
                g, _ = chunk_of(b, o)
                act.wait_ge(s_m, g + 1)
                nc.scalar.activation(ceb[:], ceb[:], ACT.Exp).then_inc(s_e, 1)
                act.wait_ge(s_e, g + 1)
                nc.scalar.activation(ceb[:], ceb[:], ACT.Ln, bias=1.0).then_inc(s_l, 1)

            def weights(b, o):
                g, z = chunk_of(b, o)
                act.wait_ge(s_cum, g + 2)
                act.wait_ge(s_wl, g + 1)
                nc.scalar.activation(swb[:], PS[:, z, :], ACT.Exp).then_inc(s_w, 1)
                act.wait_ge(s_w, g + 3)
                act.wait_ge(s_pv, CHUNK_PAIRS * g + 4)
                nc.scalar.copy(wst[z][:, :, 0:64], swb[:].rearrange("p (x c) -> p x c", x=CT)).then_inc(s_wh, 1)

            def body(b, at):
                k, e, w, v = at(0), at(6), at(8), at(8)
                for hf in range(4):
                    if k is not None:
                        k_hi(b, k, hf)
                    if hf == 1 and is_first(w):
                        weights(b, w)
                    if hf == 1 and is_first(e):
                        soft(b, e)
                    if v is not None and hf % 2 == 1:
                        v_hi(b, v, hf // 2)
            steps(act, body)

        def smp_dve(dve):
            def queries(b, o):
                dve.wait_ge(s_qk, SEQ_PAIRS * b + o + 2)
                for lo in range(2):
                    for hh in range(2):
                        r = slice(HD * hh, HD * hh + HD)
                        q = qTs[r, :, ds(DQ * seq(b, o), DQ)]
                        hi = bass.AP(qst, HD * hh * PAIRS * P + 4 * hh, [(PAIRS * P, HD), (P + 8, PAIRS), (1, DQ)])
                        if lo == 0:
                            nc.vector.tensor_copy(hi, q).then_inc(s_qh, 1)
                        else:
                            low = bass.AP(qst, HD * hh * PAIRS * P + 4 * hh + 64, [(PAIRS * P, HD), (P + 8, PAIRS), (1, DQ)])
                            dve.wait_ge(s_qh, 2 * seq(b, o) + 2)
                            ins_ = nc.vector.tensor_tensor(low, q, hi.bitcast(F32), ALU.subtract)
                ins_.then_inc(s_qst, 1)

            def k_lo(b, o, hf):
                e, h, unit = hf // 2, hf % 2, 4 * (SEQ_PAIRS * b + o) + hf
                dve.wait_ge(s_kh, unit + 1)
                part_ = lambda t: t[o % 2][:, 4 * h:4 * h + 4, e * P:(e + 1) * P]
                nc.vector.tensor_tensor(part_(ktl), PS[:, 4 + hf % 2, :].rearrange("p (a s) -> p a s", a=4),
                                        part_(kth).bitcast(F32), ALU.subtract).then_inc(s_kl, 1)

            def copy_scores(b, o):
                pair = SEQ_PAIRS * b + o
                dve.wait_ge(s_qk, pair + 3)
                dve.wait_ge(s_c1, pair + 1)
                nc.vector.tensor_copy(zsb[o % 2][:], PS[:, 6 + o % 2, 0:2 * P]).then_inc(s_zc, 1)

            def clamp(b, o):
                g, z = chunk_of(b, o)
                dve.wait_ge(s_c1, CHUNK_PAIRS * g + 6)
                dve.wait_ge(s_sp, g + 1)
                nc.vector.tensor_scalar(ceb[:], PS[:, z, :], CLAMP, None, ALU.min).then_inc(s_m, 1)

            def softplus(b, o):
                g, z = chunk_of(b, o)
                dve.wait_ge(s_l, g + 1)
                dve.wait_ge(s_cum, g + 1)
                dve.wait_ge(s_sf, (CT + 1) * g + 1)
                nc.vector.tensor_tensor(ssp[:], PS[:, z, :], ceb[:], ALU.max).then_inc(s_sp, 1)

            def page_sums(b, o, pages):
                g, _ = chunk_of(b, o)
                for x in pages:
                    d = ssf[:, 64 * x:64 * x + 64] if x < CT else carry[:]
                    dve.wait_ge(s_sf, (CT + 1) * g + x + 1)
                    if x == 0 and o % SEQ_PAIRS == 0:
                        nc.vector.tensor_copy(d, spn[:, ds(seq(b, o), 1), :].rearrange("p b c -> p (b c)")).then_inc(s_sf, 1)
                    elif x == 0:
                        nc.vector.tensor_copy(d, carry[:]).then_inc(s_sf, 1)
                    else:
                        if x == 1:
                            dve.wait_ge(s_sp, g + 2)
                        nc.vector.tensor_tensor(d, ssf[:, 64 * x - 64:64 * x], ssp[:, 64 * x - 64:64 * x],
                                                ALU.add).then_inc(s_sf, 1)

            def w_lo(b, o):
                g, par = chunk_of(b, o)
                dve.wait_ge(s_wh, g + 1)
                nc.vector.tensor_tensor(wst[par][:, :, 64:128], swb[:].rearrange("p (x c) -> p x c", x=CT),
                                        wst[par][:, :, 0:64].bitcast(F32), ALU.subtract).then_inc(s_wl, 1)

            def new_weights(b, o):
                dve.wait_ge(s_pv, SEQ_PAIRS * b + o + 1)
                nc.vector.tensor_copy(wns[:, 0:64], wn[:, ds(seq(b, o), 1), :].rearrange("p b c -> p (b c)")
                                      ).then_inc(s_wn, 1)

            def own_features(b, o):
                n = seq(b, o)
                dve.wait_ge(s_pv, SEQ_PAIRS * b + o + 9)
                dve.wait_ge(s_oc, n + 1)
                for h in range(2):
                    own = bass.AP(own_head, 8 * h, [(HEADS, P), (1, 8), (0, HD)])
                    ins_ = nc.vector.tensor_tensor(om[:, 512 * h:512 * h + 512].rearrange("p (h d) -> p h d", d=HD),
                                                   PS[:, 2 + h, :].rearrange("p (h d) -> p h d", d=HD), own, ALU.mult)
                ins_.then_inc(s_o, 1)

            def head_sums(b, o):
                n = seq(b, o)
                dve.wait_ge(s_o, n + 2)
                nc.vector.tensor_reduce(oc[:, ds(n, 1), :].rearrange("p b d -> p (b d)"),
                                        om[:].rearrange("p (h d) -> p d h", d=HD), mybir.AxisListType.X,
                                        ALU.add).then_inc(s_oc, 1)

            def body(b, at):
                k, s, c, l, p, w, v, o = at(0), at(1), at(5), at(6), at(7), at(8), at(8), at(10)
                is_end = o is not None and o % SEQ_PAIRS == SEQ_PAIRS - 1
                if is_start(s):
                    queries(b, s)
                for hf in range(4):
                    if hf == 3 and s is not None:
                        copy_scores(b, s)
                    if k is not None:
                        k_lo(b, k, hf)
                    if hf == 1 and is_end:
                        own_features(b, o)
                    if hf == 3 and is_end:
                        head_sums(b, o)
                    if is_first(p):
                        page_sums(b, p, range(CT + 1)[2 * hf:2 * hf + 2 + hf // 3])
                    if hf == 2 and is_first(w):
                        w_lo(b, w)
                    if hf == 2 and is_start(w):
                        new_weights(b, w)
                if is_first(l):
                    softplus(b, l)
                if v is not None:
                    v_lo(dve, nc.vector, b, v, 0, s_vl0)
                if is_first(c):
                    clamp(b, c)
            steps(dve, body)
            dve.wait_ge(s_n, 3)
            for hh in range(2):
                r = slice(HD * hh, HD * hh + HD)
                src = PS[r, 4 + hh, :].rearrange("p (b a c) -> p a b c", b=DB, a=PAIRS)
                nc.vector.tensor_copy(mT[r, :, NP:T].rearrange("p a (b q) -> p a b q", b=DB),
                                      src[:, :, :, 4 * hh:4 * hh + 4])

        def v_lo(eng, unit, b, o, e, done):
            slot = (2 * o + e) % VR
            eng.wait_ge(s_vh, 2 * (SEQ_PAIRS * b + o) + e + 1)
            unit.tensor_tensor(vl[slot][:], vr[slot][:], vh[(2 * o + e) % 4][:].bitcast(F32), ALU.subtract).then_inc(done, 1)

        def smp_pool(pool):
            def body(b, at):
                if at(8) is not None:
                    v_lo(pool, nc.gpsimd, b, at(8), 1, s_vl1)
            steps(pool, body)

        def split_act(act, a):
            for k in range(KB):
                nc.scalar.copy(xh[:, k, :], mT[:, k, :]).then_inc(n_hi, 1)

        def split_dve(dve, a):
            for k in range(KB):
                dve.wait_ge(n_hi, 8 * a + k + 1)
                nc.vector.tensor_tensor(xl[:, k, :], mT[:, k, :], xh[:, k, :].bitcast(F32), ALU.subtract).then_inc(n_lo, 1)
            dve.sem_inc(n_t, KB)

        def y_rows(t):
            return (P, y_p[0][t * P:(t + 1) * P, :]) if t < TT else (NS, y_s.rearrange("b q d -> (b q) d"))

        def out_pe(pe):
            for t in range(TT + 1):
                w = y_rows(t)[0]
                if t >= 2:
                    pe.wait_ge(y_a, t - 1)
                    pe.wait_ge(y_v, t - 1)
                for k in range(KB):
                    mm = nc.tensor.transpose(PS[0:w, 2 * (t % 2) + k // 4, (k % 4) * P:(k % 4) * P + P],
                                             hT[:, k, t * P:t * P + w], ident[:, :])
                mm.then_inc(y_pe, 1)

        def out_copy(eng, copy, b, done):
            for t in range(TT + 1):
                w = y_rows(t)[0]
                eng.wait_ge(y_pe, t + 1)
                if t >= 2:
                    eng.wait_ge(y_st[t % 2], 16 * (t // 2))
                copy(ytok[t % 2][0:w, 512 * b:512 * b + 512], PS[0:w, 2 * (t % 2) + b, :]).then_inc(done, 1)

        def out_sp(sp):
            for t in range(TT + 1):
                w, dst = y_rows(t)
                sp.wait_ge(y_a, t + 1)
                sp.wait_ge(y_v, t + 1)
                sp.dma_start(dst, ytok[t % 2][0:w, :]).then_inc(y_st[t % 2], 16)
            for j in range(2):
                sp.wait_ge(y_st[j], 16 * ((TT + 1 - j + 1) // 2))

        hsrc = [part(hT, 0, NH), part(hT, NH, NH)]

        (F_LOAD, F_OUT, F_FFN0) = range(1, 4)
        FFN_FENCES = 4
        F_KV, S_NEW, S_SMP, S_ATT, F_ATT, F_O = range(F_FFN0 + FFN_FENCES, F_FFN0 + FFN_FENCES + 6)
        F_FFN1 = F_O + 1
        F_END = F_FFN1 + FFN_FENCES

        def ffn(stage0, layer, q0, a0, p0, parts):
            for half in range(2):
                parts[0](half, q0 + half, a0 + half)
                parts[1](half)
                yield stage0 + 2 * half
                parts[2](half)
                yield stage0 + 2 * half + 1
                parts[3](half, q0 + 2 + half, p0 + half)


        @block.sync
        def _(sp):
            load_sp(sp)
            glu_sp(sp)
            proj_sp(sp, "out", A["conv_w_out"][0])
            for half in range(2):
                up_sp(sp, 0, half)
                down_sp(sp, 0, half)
            proj_sp(sp, "k", A["w_k"])
            proj_sp(sp, "v", A["w_v"])
            proj_sp(sp, "q", A["w_q"][0])
            for q in range(2):
                load_tile(sp, first["o"] + q, q, cols(A["w_o"][0], q), KB)
            smp_sp(sp, S_NEW)
            att_sp(sp, S_ATT)
            with sp.Fori(1, KB // 2) as i:
                for q in range(2):
                    t, _ = tile_no("o", 2, i, q)
                    load_tile(sp, t, q, cols(A["w_o"][0], 2 * i + q), KB)
            for half in range(2):
                up_sp(sp, 1, half)
                down_sp(sp, 1, half)
            out_sp(sp)

        @block.tensor
        def _(pe):
            pe.sem_inc(w_used, 2)
            pe.sem_inc(g_tr, 2)
            pe.sem_inc(a_cum, UR)
            pe.sem_inc(a_pv, 4)
            pe.sem_inc(s_t, 5)
            pe.sem_inc(s_qk, 2)
            pe.sem_inc(s_c1, 2)
            pe.sem_inc(s_cum, 1)
            pe.sem_inc(s_pv, 8)
            load_pe(pe)
            fence(pe, F_LOAD)
            stats_pe(pe, 0, CH)
            glu_pe(pe)
            ln_pe_mean(pe)
            stats_pe(pe, 1, CH)
            proj_pe(pe, "out", 1)
            fence(pe, F_OUT)
            stats_pe(pe, 2, CH)

            def run_ffn(layer, stage0, q0, a0, p0):
                def inp(half, q, a):
                    if half == 0:
                        stats_pe(pe, q, HCH)
                        ffn_rows_pe(pe, layer)

                def post(half, q, p):
                    if half == 0:
                        stats_pe(pe, q0 + 1, HCH, acc, 6)
                    stats_pe(pe, q, HCH, acch)

                def down(half):
                    if half == 1:
                        ffn_state_pe(pe, layer)
                    down_pe(pe, layer, half)
                for n in ffn(stage0, layer, q0, a0, p0, (inp, lambda half: up_pe(pe, layer, half), down,
                                                         post)):
                    fence(pe, n)
            run_ffn(0, F_FFN0, 3, 2, 1)
            stats_pe(pe, 7, CH)
            proj_pe(pe, "k", 4, 0)
            proj_pe(pe, "v", 4, 1)
            fence(pe, F_KV)
            proj_pe(pe, "q", 5)
            fence(pe, S_NEW)
            smp_new_pe(pe)
            fence(pe, S_SMP)
            smp_pe(pe)
            fence(pe, S_ATT)
            att_pe(pe)
            fence(pe, F_ATT)
            proj_pe(pe, "o", 6)
            fence(pe, F_O)
            stats_pe(pe, 8, CH)
            run_ffn(1, F_FFN1, 9, 7, 4)
            fence(pe, F_END)
            out_pe(pe)

        @block.scalar
        def _(act):
            act.sem_inc(ps_free, 2)
            act.sem_inc(f_g, 1)
            act.sem_inc(f_gel, 1)
            act.sem_inc(g_tap, 2 * POOL_TAPS)
            act.sem_inc(a_w, UR)
            act.sem_inc(s_w, 2)
            load_act(act)
            for b in range(2):
                split_hi(act, b, 0, b)
            fence(act, F_LOAD)
            stats_act(act, 0, full(hT), T, CH)
            apply_act(act, 0, full(xh), T)
            glu_act(act)
            stats_act(act, 1, full(mT), T, CH, (l_xc, 0))
            ln_act(act, 1)
            proj_act(act, "out", lambda n, b: mT[:, ds(n, 1), :].opt(), bias=V_BOUT, post=0)
            fence(act, F_OUT)
            act.sem_inc(n_sq, KB)
            root_act(act, 2, CH)

            def run_ffn(layer, stage0, q0, a0, p0):
                def inp(half, q, a):
                    if half == 0:
                        stats_act(act, q, hsrc[half], NH, HCH, (p_h, KB * (p0 - 1)))
                    apply_act(act, a, full(xhh), NH)

                def down(half):
                    if half == 0:
                        early_act(act, q0 + 1)
                    down_act(act, layer, half, layer == 1 and half == 1)

                def post(half, q, p):
                    if half == 0:
                        root_act(act, q0 + 1, HCH, 6, NH)
                    act.sem_inc(n_sq, KB)
                    root_act(act, q, HCH)
                for n in ffn(stage0, layer, q0, a0, p0, (
                        inp, lambda half: up_act(act, layer, half),
                        down, post)):
                    fence(act, n)
            run_ffn(0, F_FFN0, 3, 2, 1)
            stats_act(act, 7, full(hT), T, CH, (p_h, KB * 2))
            apply_act(act, 4, full(xh), T)
            proj_act(act, "k", lambda n, b: tmp[b], kv=0)
            proj_act(act, "v", lambda n, b: tmp[b], kv=1)
            fence(act, F_KV)
            apply_act(act, 5, full(xh), T)
            proj_act(act, "q", lambda n, b: tmp[b], scale=HD ** -0.5, kv=2)
            fence(act, S_NEW)
            table("natural_log_exp_and_others")
            smp_new_act(act)
            fence(act, S_SMP)
            smp_act(act)
            fence(act, S_ATT)
            att_act(act)
            fence(act, F_ATT)
            split_act(act, 6)
            proj_act(act, "o", lambda n, b: mT[:, ds(n, 1), :].opt(), post=3)
            fence(act, F_O)
            act.sem_inc(n_sq, KB)
            root_act(act, 8, CH)
            run_ffn(1, F_FFN1, 9, 7, 4)
            fence(act, F_END)
            out_copy(act, nc.scalar.copy, 0, y_a)

        @block.vector
        def _(dve):
            dve.sem_inc(w_lo, 2)
            for s_, n in ((g_u, 1), (g_smp, 1), (g_cv, 1), (g_tre, 1), (k_te, 2), (f_cv, 2), (f_p, 1), (a_o, 8), (a_sp, 3), (m_add, 2),
                          (s_kl, 2), (s_zc, 2), (s_sp, 1), (s_sf, 1), (s_wl, 1), (s_o, 1), (s_oc, 1)):
                dve.sem_inc(s_, n)
            load_dve(dve)
            for b in range(2):
                split_lo(dve, b, b)
            fence(dve, F_LOAD)
            stats_dve(dve, 0, T)
            apply_dve(dve, 0, 0, full(hT), V_MIX_PRE, full(xh), full(xl), T)
            glu_dve(dve)
            ln_dve_sum(dve)
            stats_dve(dve, 1, T)
            ln_dve_scale(dve, 1, 1)
            proj_dve(dve, "out", post=0)
            summed_dve(dve, 0)
            fence(dve, F_OUT)
            scale_dve(dve, 2, T)
            post_dve(dve, 0, 2, full(mT), V_MIX_POST, 0, T)

            def run_ffn(layer, stage0, q0, a0, p0):
                def inp(half, q, a):
                    if half == 0:
                        stats_dve(dve, q, NH)
                    apply_dve(dve, a, q, hsrc[half], V_FFN_PRE + layer, full(xhh), full(xlh), NH, half * NH)
                    if half == 0:
                        ffn_rows_dve(dve, layer)

                def down(half):
                    if half == 1:
                        ffn_state_dve(dve, layer)
                    else:
                        early_dve(dve, q0 + 1)
                    down_dve(dve, layer, half, layer == 1 and half == 1)

                def post(half, q, p):
                    if half == 0:
                        scale_dve(dve, q0 + 1, NH, NH)
                    scale_dve(dve, q, NH)
                    post_dve(dve, p, q, full(mTh), V_FFN_POST + layer, NH * half, NH)
                for n in ffn(stage0, layer, q0, a0, p0, (inp, lambda half: up_dve(dve, layer, half), down, post)):
                    fence(dve, n)
            run_ffn(0, F_FFN0, 3, 2, 1)
            stats_dve(dve, 7, T)
            apply_dve(dve, 4, 7, full(hT), V_KV, full(xh), full(xl), T)
            proj_dve(dve, "k", 0)
            proj_dve(dve, "v", 1)
            fence(dve, F_KV)
            apply_dve(dve, 5, 7, full(hT), V_MIX_PRE + 1, full(xh), full(xl), T)
            proj_dve(dve, "q")
            fence(dve, S_NEW)
            smp_new_dve(dve)
            fence(dve, S_SMP)
            smp_dve(dve)
            fence(dve, S_ATT)
            att_dve(dve)
            fence(dve, F_ATT)
            split_dve(dve, 6)
            proj_dve(dve, "o", post=3)
            summed_dve(dve, 3)
            fence(dve, F_O)
            scale_dve(dve, 8, T)
            post_dve(dve, 3, 8, full(mT), V_MIX_POST + 1, 0, T)
            run_ffn(1, F_FFN1, 9, 7, 4)
            fence(dve, F_END)
            out_copy(dve, nc.vector.tensor_copy, 1, y_v)

        @block.gpsimd
        def _(pool):
            for s_, n in ((g_pool, 1), (g_of, 1), (k_free, 2), (k_tf, 2), (a_s, UR)):
                pool.sem_inc(s_, n)
            load_pool(pool)
            fence(pool, F_LOAD)
            glu_pool(pool)
            fence(pool, F_OUT)
            ffn_rows_pool(pool, 0)

            def run_ffn(layer, stage0, q0, a0, p0):
                def down(half):
                    if half == 1:
                        ffn_state_pool(pool, layer)
                for n in ffn(stage0, layer, q0, a0, p0, (
                        lambda half, q, a: None, lambda half: None, down, lambda half, q, p: None)):
                    fence(pool, n)
            run_ffn(0, F_FFN0, 3, 2, 1)
            proj_pool(pool, 0, k_dram, 0, ok_p, ok_s)
            proj_pool(pool, 1, None, 1, ov_p, ov_s)
            fence(pool, F_KV)
            proj_pool(pool, 2, q_dram)
            fence(pool, S_NEW)
            smp_in_pool(pool)
            smp_new_pool(pool)
            fence(pool, S_SMP)
            smp_pool(pool)
            fence(pool, S_ATT)
            att_pool(pool)
            for n in (F_ATT, F_O):
                fence(pool, n)
            ffn_rows_pool(pool, 1)
            run_ffn(1, F_FFN1, 9, 7, 4)
            fence(pool, F_END)


_INS = ["x_prompt", "x_sample", "state_conv_a", "state_ffn_conv", "cache_k", "cache_v", "page_table",
        "norm_mix_pre", "norm_mix_post", "norm_ffn_pre", "norm_ffn_post", "conv_w_glu", "conv_b_glu", "conv_w_dw",
        "conv_b_dw", "conv_ln_g", "conv_ln_b", "conv_w_out", "conv_b_out", "kv_norm", "w_k", "w_v", "w_q", "w_o",
        "sb_bias", "ffn_w_gate", "ffn_w_up", "ffn_w_dw", "ffn_w_down"]
_OUTS = [(1, NP, D), (DB, DQ, D), (1, 1, ST, D), (1, DB, ST, D), (2, 1, 2, FF), (2, DB, 2, FF),
         (NP, D), (NP, D), (NS, D), (NS, D)]
_RETURNED = _OUTS[:6] + [(1, NP, HEADS, HD)] * 2 + [(DB, DQ, HEADS, HD)] * 2


def build(nc, shapes):
    ins = {n: nc.dram_tensor(f"in_{n}", s, dt, kind="ExternalInput").ap() for n, (s, dt) in shapes.items()}
    outs = [nc.dram_tensor(f"out_{i}", s, F32, kind="ExternalOutput").ap() for i, s in enumerate(_OUTS)]
    yoco_step(nc, ins, outs)


def kernel(**inputs):
    import numpy as np
    import concourse.bacc as bacc
    from concourse.bass_utils import run_bass_kernel_spmd

    nc = bacc.Bacc("TRN2", target_bir_lowering=False, num_devices=1)
    arrays = {n: np.ascontiguousarray(inputs[n]) for n in _INS}
    build(nc, {n: (a.shape, mybir.dt.from_np(a.dtype)) for n, a in arrays.items()})
    r = run_bass_kernel_spmd(nc, [{f"in_{n}": a for n, a in arrays.items()}], core_ids=[0])
    return tuple(r.results[0][f"out_{i}"].reshape(s) for i, s in enumerate(_RETURNED))
```
